# Optimizing a Trainium2 kernel written in Bass

```python
import math
import jax, jax.numpy as jnp
from jax import lax
import numpy as np

D_MODEL = 2048
BATCH = 1
SEQ = 256
DEPTH = 1

CHUNK = 64
RET_WIDTH = D_MODEL // 2
RET_HEADS = 8
RET_HEAD_DIM = RET_WIDTH // RET_HEADS
SSM_WIDTH = D_MODEL - RET_WIDTH
SSM_GROUP = 16
SSM_GROUPS = SSM_WIDTH // SSM_GROUP
SSM_STATE = 64
D_FF = -(-8 * D_MODEL // (3 * 256)) * 256
IN_WIDTH = 4 * RET_WIDTH + SSM_WIDTH
ROPE_BASE = 10000.0
EPS = 1e-6

kernel_name = "hybrid_retention_s5_block"

def rmsnorm(x, g):
    xf = x.astype(jnp.float32)
    y = xf * lax.rsqrt(jnp.mean(xf * xf, axis=-1, keepdims=True) + EPS) * g.astype(jnp.float32)
    return y.astype(x.dtype)

def rope(x, pos):
    dh = x.shape[-1]
    half = dh // 2
    freqs = ROPE_BASE ** (-jnp.arange(half, dtype=jnp.float32) / half)
    ang = pos[:, None] * freqs[None, :]
    cos = jnp.cos(ang)[None, :, None, :]
    sin = jnp.sin(ang)[None, :, None, :]
    xf = x.astype(jnp.float32)
    x1, x2 = xf[..., :half], xf[..., half:]
    return jnp.concatenate([x1 * cos - x2 * sin, x2 * cos + x1 * sin], axis=-1)

def retention_group(q, k, v, g, gn_gain):
    b, s, h, dk = q.shape
    n_chunks = s // CHUNK
    hh = jnp.arange(h, dtype=jnp.float32)
    log_g = jnp.log1p(-(2.0 ** (-5.0 - hh)))
    q = q.reshape(b, n_chunks, CHUNK, h, dk)
    k = k.reshape(b, n_chunks, CHUNK, h, dk) * (dk ** -0.5)
    v = v.astype(jnp.float32).reshape(b, n_chunks, CHUNK, h, dk)
    idx = jnp.arange(CHUNK, dtype=jnp.float32)
    dist = jnp.abs(idx[:, None] - idx[None, :])
    intra_decay = jnp.exp(log_g[:, None, None] * dist)
    scores = jnp.einsum('bnqhd,bnkhd->bnhqk', q, k) * intra_decay
    intra = jnp.einsum('bnhqk,bnkhe->bnqhe', scores, v)
    k_dec = jnp.exp(log_g[None, :] * (CHUNK - 1 - idx)[:, None])
    kv = jnp.einsum('bnchd,bnche->nbhde', k * k_dec[..., None], v)
    chunk_dec = jnp.exp(log_g * CHUNK)[:, None, None]

    def step(state, kv_i):
        return state * chunk_dec + kv_i, state

    _, state_prev = lax.scan(step, jnp.zeros_like(kv[0]), kv)
    q_dec = jnp.exp(log_g[None, :] * (idx + 1.0)[:, None])
    inter = jnp.einsum('bnchd,nbhde->bnche', q * q_dec[..., None], state_prev)
    out = (intra + inter).reshape(b, s, h, dk)
    mu = jnp.mean(out, axis=-1, keepdims=True)
    var = jnp.mean(jnp.square(out - mu), axis=-1, keepdims=True)
    out = ((out - mu) * lax.rsqrt(var + EPS)).reshape(b, s, h * dk) * gn_gain.astype(jnp.float32)
    return jax.nn.silu(g.astype(jnp.float32)) * out

def s5_group(u, a_re, a_im, log_dt, b_re, b_im, c_re, c_im, d_skip, w_glu, b_glu, out_gain):
    b, s, _ = u.shape
    f32 = jnp.float32
    uf = u.astype(f32).reshape(b, s, SSM_GROUPS, SSM_GROUP)
    lam = lax.complex(a_re.astype(f32), a_im.astype(f32))
    dt = jnp.exp(log_dt.astype(f32))[:, None]
    lam_bar = jnp.exp(lam * dt)
    b_c = lax.complex(b_re.astype(f32), b_im.astype(f32))
    b_bar = ((lam_bar - 1.0) / lam)[..., None] * b_c
    bu = lax.complex(jnp.einsum('gpc,bsgc->bsgp', jnp.real(b_bar), uf),
                     jnp.einsum('gpc,bsgc->bsgp', jnp.imag(b_bar), uf))
    a = jnp.broadcast_to(lam_bar, bu.shape)

    def combine(left, right):
        a_l, b_l = left
        a_r, b_r = right
        return a_r * a_l, a_r * b_l + b_r

    _, states = lax.associative_scan(combine, (a, bu), axis=1)
    y = (jnp.einsum('gcp,bsgp->bsgc', c_re.astype(f32), jnp.real(states))
         - jnp.einsum('gcp,bsgp->bsgc', c_im.astype(f32), jnp.imag(states)))
    y = (y + d_skip.astype(f32).reshape(SSM_GROUPS, SSM_GROUP) * uf).reshape(b, s, SSM_WIDTH)
    y1 = jax.nn.gelu(y)
    y = y1 * jax.nn.sigmoid(y1 @ w_glu.astype(f32) + b_glu.astype(f32))
    return rmsnorm(y, out_gain)

def setup_inputs(seed: int = 0) -> dict:
    key = jax.random.key(seed)
    ks = jax.random.split(key, 24)
    f32 = jnp.float32
    L = DEPTH

    def nrm(k, shape, scale):
        return jax.random.normal(k, shape, f32) * scale

    def gain(k, shape):
        return 1.0 + 0.02 * jax.random.normal(k, shape, f32)

    n = jnp.arange(SSM_STATE, dtype=f32)
    return {
        "x": nrm(ks[0], (BATCH, SEQ, D_MODEL), 1.0),
        "norm_mix_g": gain(ks[1], (L, D_MODEL)),
        "w_in": nrm(ks[2], (L, D_MODEL, IN_WIDTH), D_MODEL ** -0.5),
        "ret_gn_g": gain(ks[3], (L, RET_WIDTH)),
        "ssm_a_re": -0.5 + 0.01 * nrm(ks[4], (L, SSM_GROUPS, SSM_STATE), 1.0),
        "ssm_a_im": math.pi * n + 0.01 * nrm(ks[5], (L, SSM_GROUPS, SSM_STATE), 1.0),
        "ssm_log_dt": jax.random.uniform(ks[6], (L, SSM_GROUPS), f32, math.log(1e-3), math.log(1e-1)),
        "ssm_b_re": nrm(ks[7], (L, SSM_GROUPS, SSM_STATE, SSM_GROUP), (2 * SSM_GROUP) ** -0.5),
        "ssm_b_im": nrm(ks[8], (L, SSM_GROUPS, SSM_STATE, SSM_GROUP), (2 * SSM_GROUP) ** -0.5),
        "ssm_c_re": nrm(ks[9], (L, SSM_GROUPS, SSM_GROUP, SSM_STATE), (2 * SSM_STATE) ** -0.5),
        "ssm_c_im": nrm(ks[10], (L, SSM_GROUPS, SSM_GROUP, SSM_STATE), (2 * SSM_STATE) ** -0.5),
        "ssm_d": nrm(ks[11], (L, SSM_WIDTH), 1.0),
        "ssm_w_glu": nrm(ks[12], (L, SSM_WIDTH, SSM_WIDTH), SSM_WIDTH ** -0.5),
        "ssm_b_glu": nrm(ks[13], (L, SSM_WIDTH), 0.01),
        "ssm_out_g": gain(ks[14], (L, SSM_WIDTH)),
        "w_out": nrm(ks[15], (L, D_MODEL, D_MODEL), D_MODEL ** -0.5),
        "norm_ffn_g": gain(ks[16], (L, D_MODEL)),
        "w_gate": nrm(ks[17], (L, D_MODEL, D_FF), D_MODEL ** -0.5),
        "w_up": nrm(ks[18], (L, D_MODEL, D_FF), D_MODEL ** -0.5),
        "w_down": nrm(ks[19], (L, D_FF, D_MODEL), D_FF ** -0.5),
        "norm_final_g": gain(ks[20], (D_MODEL,)),
    }

def reference(x, norm_mix_g, w_in, ret_gn_g, ssm_a_re, ssm_a_im, ssm_log_dt, ssm_b_re, ssm_b_im,
              ssm_c_re, ssm_c_im, ssm_d, ssm_w_glu, ssm_b_glu, ssm_out_g, w_out, norm_ffn_g,
              w_gate, w_up, w_down, norm_final_g):
    b, s, _ = x.shape
    pos = jnp.arange(s, dtype=jnp.float32)
    R = RET_WIDTH
    for l in range(DEPTH):
        h = rmsnorm(x, norm_mix_g[l])
        proj = h @ w_in[l]
        q = rope(proj[..., 0:R].reshape(b, s, RET_HEADS, RET_HEAD_DIM), pos)
        k = rope(proj[..., R:2 * R].reshape(b, s, RET_HEADS, RET_HEAD_DIM), pos)
        v = proj[..., 2 * R:3 * R].reshape(b, s, RET_HEADS, RET_HEAD_DIM)
        g = proj[..., 3 * R:4 * R]
        u = proj[..., 4 * R:]
        y_ret = retention_group(q, k, v, g, ret_gn_g[l])
        y_ssm = s5_group(u, ssm_a_re[l], ssm_a_im[l], ssm_log_dt[l], ssm_b_re[l], ssm_b_im[l],
                         ssm_c_re[l], ssm_c_im[l], ssm_d[l], ssm_w_glu[l], ssm_b_glu[l], ssm_out_g[l])
        mix = jnp.concatenate([y_ret, y_ssm.astype(jnp.float32)], axis=-1).astype(x.dtype)
        x = x + mix @ w_out[l]
        h = rmsnorm(x, norm_ffn_g[l])
        x = x + (jax.nn.silu(h @ w_gate[l]) * (h @ w_up[l])) @ w_down[l]
    return rmsnorm(x, norm_final_g)


_drawn_inputs = setup_inputs


def setup_inputs(seed=0):
    import zlib

    import numpy as np

    out = dict(_drawn_inputs(seed))
    spreads = {}
    factors = {'norm_mix_g': 2.801,
     'ret_gn_g': 54.652,
     'ssm_a_re': 200.0,
     'ssm_b_glu': 45.616,
     'ssm_out_g': 100.96,
     'norm_ffn_g': 18.974,
     'norm_final_g': 23.685,
     'ssm_a_im': 44.008,
     'ssm_log_dt': 45.848,
     'ssm_b_re': 61.48,
     'ssm_b_im': 60.192,
     'ssm_c_re': 60.696,
     'ssm_c_im': 61.384}
    for name, (base, spread) in spreads.items():
        noise = np.random.default_rng([zlib.crc32(name.encode()), seed]).standard_normal(out[name].shape)
        drawn = base * np.exp(spread * noise) if base else spread * noise
        out[name] = __import__('jax').numpy.asarray(drawn.astype(out[name].dtype))
    for name, factor in factors.items():
        out[name] = (out[name] * factor).astype(out[name].dtype)
    return out
```

```python
from contextlib import ExitStack

import numpy as np

import concourse.bass as bass
from concourse import mybir

P = 128
D_MODEL = 2048
SEQ = 256
TOK = SEQ // P
CHUNK = 64
HEADS = 8
HEAD_DIM = 128
RET_W = D_MODEL // 2
GROUPS, STATE, CH = 64, 64, 16
D_FF = -(-8 * D_MODEL // (3 * 256)) * 256
IN_W = 5 * RET_W
KB = D_MODEL // P
NCOL = 512
EPS = 1e-6
LOC, NCH = 8, 32
KPAD = 2 * LOC - 1

RAW = 4
SPL = 4
CK = 2 * NCOL
GRP = KB // 2
IN_COLS = [8, 9, 6, 7, 4, 5, 0, 1, 2, 3]
N_IN = len(IN_COLS) * GRP
N_GLU = 8
N_OUT = 16
GLU0 = N_IN
RET0 = GLU0 + N_GLU
SSM0 = RET0 + N_OUT
FFN0 = SSM0 + N_OUT
FG = D_FF // NCOL
LOOP0 = FFN0 + 2 * GRP
TURN = 3 * GRP
TAIL0 = LOOP0 + TURN * (FG - 1)

F32 = mybir.dt.float32
F32R = mybir.dt.float32r
ALU = mybir.AluOpType
ACT = mybir.ActivationFunctionType

V_MIX, V_FFN, V_BGLU, V_OUTG, V_RETG, V_SGN = 0, 16, 32, 40, 48, 56
N_VEC = 57

S5_AT, S5_STEP, BG = 21, 4, 8
NB = GROUPS // BG


def build(nc, A, out):
    ctx = ExitStack()

    def sb(name, shape, dt=F32):
        return ctx.enter_context(nc.sbuf_tensor(name, shape, dt))

    def overlay(*layers):
        made, size = {}, 0
        for layer in layers:
            with ExitStack() as scope:
                for name, shape, dt in layer:
                    made[name] = scope.enter_context(nc.sbuf_tensor(name, shape, dt))
                size = max(size, sum(4 * int(np.prod(s[1:])) for _, s, _ in layer))
        sb("room_" + layers[0][0][0], [P, size // 4])
        return made

    def sem(name):
        return ctx.enter_context(nc.semaphore(name))

    with ctx:
        raw = sb("raw", [P, RAW, CK])
        w_hi = sb("w_hi", [P, SPL, CK], F32R)
        w_lo = sb("w_lo", [P, SPL, CK], F32R)
        actA_hi = sb("actA_hi", [P, 8, SEQ], F32R)
        actA_lo = sb("actA_lo", [P, 8, SEQ], F32R)
        m = overlay(
            [("actB_hi", [P, 8, SEQ], F32R), ("actB_lo", [P, 8, SEQ], F32R)],
            [("ffT_hi", [P, 4, SEQ], F32R), ("ffT_lo", [P, 4, SEQ], F32R), ("ff_act", [P, TOK, NCOL], F32)],
        )
        actB_hi, actB_lo, ffT_hi, ffT_lo, ff_act = (m[k] for k in ("actB_hi", "actB_lo", "ffT_hi", "ffT_lo", "ff_act"))
        m = overlay([("x2", [P, TOK, D_MODEL], F32)], [("state", [P, NCH, 2, GROUPS], F32)])
        x2, state = m["x2"], m["state"]
        m = overlay([("qT", [P, HEADS, SEQ], F32)], [("u_tok", [P, TOK, 1024], F32)])
        qT, u_tok = m["qT"], m["u_tok"]
        ret = qT
        m = overlay([("kT", [P, HEADS, SEQ], F32)], [("u_loc", [P, GROUPS, NCH], F32)])
        kT, u_loc = m["kT"], m["u_loc"]
        m = overlay(
            [("v", [P, TOK, RET_W], F32), ("sg", [P, TOK, RET_W], F32)],
            [("uT", [P, 8, SEQ], F32)],
            [("x_tok", [P, TOK, D_MODEL], F32)],
            [("g_final", [P, D_MODEL], F32)],
        )
        v, sg, uT, x_tok, g_final = (m[k] for k in ("v", "sg", "uT", "x_tok", "g_final"))
        m = overlay(
            [("bc", [P, 4, GROUPS, CH], F32), ("bb", [P, GROUPS + 1, CH], F32), ("bbx", [P, GROUPS, CH], F32),
             ("pr", [P, LOC + 1, GROUPS], F32), ("pi", [P, LOC + 1, GROUPS], F32)],
            [("u_loc2", [P, GROUPS, NCH], F32), ("y1", [P, GROUPS, NCH], F32), ("qs", [P, TOK, NCOL], F32),
             ("qr", [P, TOK, NCOL], F32), ("rot", [P, TOK, NCOL], F32)],
            [("zT", [P, 8, SEQ], F32), ("sqT", [P, 8, SEQ], F32), ("y1T", [P, 8, SEQ], F32)],
        )
        bc, bb, bbx, pr, pi = (m[k] for k in ("bc", "bb", "bbx", "pr", "pi"))
        u_loc2, y1, qs, qr, rot, zT, sqT, y1T = (
            m[k] for k in ("u_loc2", "y1", "qs", "qr", "rot", "zT", "sqT", "y1T"))
        m = overlay(
            [("y1T_hi", [P, 8, SEQ], F32R), ("y1T_lo", [P, 8, SEQ], F32R)],
            [("cl", [P, 2, BG, LOC + 1, CH], F32), ("cl_t", [P, BG, LOC + 1, CH], F32),
             ("wb", [P, BG, LOC, CH], F32)],
            [("xT", [P, KB, SEQ], F32)],
            [("mt", [P, 2, 16, P], F32), ("clr", [P, 2, BG, P], F32)],
            [("h2B_hi", [P, 8, SEQ], F32R), ("h2B_lo", [P, 8, SEQ], F32R)],
        )
        y1T_hi, y1T_lo, cl, cl_t, wb, xT, mt, clr, h2B_hi, h2B_lo = (
            m[k] for k in ("y1T_hi", "y1T_lo", "cl", "cl_t", "wb", "xT", "mt", "clr", "h2B_hi", "h2B_lo"))
        m = overlay(
            [("wb_t", [P, BG, LOC, CH], F32), ("wbT", [P, BG, 3 * STATE], F32)],
            [("dec", [P, 2, TOK, SEQ], F32), ("sT", [P, 2, TOK, SEQ], F32)],
        )
        wb_t, wbT, dec, sT = (m[k] for k in ("wb_t", "wbT", "dec", "sT"))
        kst = sb("kst", [P, 2, KPAD * CH])
        vec = sb("vec", [P, N_VEC])
        ident = sb("ident", [P, P])
        ones = sb("ones", [P, 1])
        par = sb("par", [P, 3, GROUPS])
        dsk = sb("dsk", [P, GROUPS // 4])
        eye16 = sb("eye16", [P, CH])
        dtmp = sb("dtmp", [P, GROUPS // 4, CH])
        rope = sb("rope", [P, TOK, 2, HEAD_DIM])
        scr = sb("scr", [P, 14, GROUPS])
        scan_a = sb("scan_a", [P, 2, GROUPS])
        scan_b = sb("scan_b", [P, 2, GROUPS])
        mul_r = sb("mul_r", [P, 2, GROUPS])
        mul_i = sb("mul_i", [P, 2, GROUPS])
        half = sb("half", [P, 2 * HEADS])
        e_tile = sb("e_tile", [P, GROUPS])
        ss = sb("ss", [P, 5, TOK])
        ss4 = sb("ss4", [P, 2, 4, TOK])
        rstd = sb("rstd", [P, 5, TOK])
        bn = sb("bn", [P, 2 * HEADS, 6])
        mv = sb("mv", [P, 2 * HEADS, 2])
        rv = sb("rv", [P, 2 * HEADS])
        rret = sb("rret", [P, 2 * HEADS])

        ps = ctx.enter_context(nc.psum_tensor("ps", [P, 8, NCOL], F32))
        R_MIX, R_SSM, R_FFN, R_FIN = range(4)

        u_dram = nc.dram_tensor("u_scratch", (RET_W, SEQ), F32, kind="Internal").ap()
        y_dram = nc.dram_tensor("y_scratch", (RET_W, SEQ), F32, kind="Internal").ap()
        k_dram = nc.dram_tensor("k_scratch", (GROUPS, CH, KPAD * CH), F32, kind="Internal").ap()
        c_dram = nc.dram_tensor("c_scratch", (P, GROUPS, P), F32, kind="Internal").ap()

        d_raw = [sem(f"d_raw{i}") for i in range(RAW)]
        d_xT = [sem(f"d_xT{i}") for i in range(4)]
        d_dec = [sem(f"d_dec{i}") for i in range(2)]
        d_mt = [sem(f"d_mt{i}") for i in range(2)]
        d_clst = [sem(f"d_clst{i}") for i in range(2)]
        d_clr = [sem(f"d_clr{i}") for i in range(2)]
        (d_vec, d_par, d_bc, d_rope, d_xtok, d_uTst, d_u, d_u2, d_kst, d_xres, d_y1st, d_y1T, d_gfin,
         d_out) = (sem(n) for n in (
             "d_vec", "d_par", "d_bc", "d_rope", "d_xtok", "d_uTst", "d_u", "d_u2", "d_kst", "d_xres",
             "d_y1st", "d_y1T", "d_gfin", "d_out"))
        names = (
            "high_done low_done pe_done xg_ready xh_ready xl_ready proj_free dve_step pool_step scan_step "
            "const_ready ss_ready rstd_mix_ready rstd_ssm_ready rstd_ffn_ready rstd_fin_ready dt_ready trig_in_ready "
            "trig_ready mag_ready pow_ready inputs_ready uT_mm u_copied cl_ready wb_ready tab_mm wbT_ready "
            "kpsum_free kst_ready v_mm v_free mul_ready qr_ready qk_mm qk_free score_mm sT_ready head_mm out_free "
            "bn_ready rret_ready ret_ready retT_mm ret_hi ret_lo y_mm y1_ready y1T_hi_ready y1T_lo_ready sig_ready "
            "zT_ready sqT_ready ssm_hi ssm_lo ssq_mm ssq_ready cols_added h2_mm h2_hi h2_lo x2_sq silu_ready ff_ready "
            "ffT_mm ffT_hi_ready ffT_lo_ready fin_sq fin_ready"
        ).split()
        S = {n: sem(n) for n in names}
        block = ctx.enter_context(nc.Block())

        def in_col(n):
            return IN_COLS[n // GRP]

        def chunk_source(n):
            if n < GLU0:
                c, k = in_col(n), 2 * (n % GRP)
                w = A["w_in"]
            elif n < RET0:
                c, k = (n - GLU0) // 4, 2 * ((n - GLU0) % 4)
                w = A["ssm_w_glu"]
            elif n < SSM0:
                c, k = (n - RET0) // 4, 2 * ((n - RET0) % 4)
                w = A["w_out"]
            elif n < FFN0:
                c, k = (n - SSM0) // 4, 8 + 2 * ((n - SSM0) % 4)
                w = A["w_out"]
            else:
                c, k = 0, 2 * ((n - FFN0) % GRP)
                w = A["w_gate"] if n < FFN0 + GRP else A["w_up"]
            return w[k * P:(k + 2) * P, c * NCOL:(c + 1) * NCOL].rearrange("(b p) n -> p b n", p=P)

        def h2(kb, part):
            if kb < 8:
                return (actA_hi, actA_lo)[part][:, kb, :]
            return (h2B_hi, h2B_lo)[part][:, kb - 8, :]

        def act_block(kb, part):
            if kb < 8:
                return (actA_hi, actA_lo)[part][:, kb, :]
            return (actB_hi, actB_lo)[part][:, kb - 8, :]

        def s5_group(b):
            return slice(BG * b, BG * (b + 1))

        raw2 = raw[:].rearrange("p s (b n) -> p s b n", b=2)
        wbT_v = wbT[:]
        kst_w = kst[:].rearrange("p h (d c) -> p h d c", c=CH)

        @block.sync
        def _(sp):
            def load(n, src, turn=None):
                slot = (n if turn is None else n[1]) % RAW
                if turn is None:
                    if n >= RAW:
                        sp.wait_ge(S["low_done"], n - RAW + 1)
                else:
                    sp.wait_ge(S["low_done"], turn * TURN + (n[1] - RAW + 1))
                sp.dma_start(raw2[:, slot], src).then_inc(d_raw[slot], 16)

            def before(n):
                b, r = divmod(n - 12 - S5_AT, S5_STEP)
                if n == 30:
                    sp.wait_ge(S["u_copied"], 1)
                    sp.dma_start(u_dram.rearrange("(b r) p -> r b p", r=P), uT[:]).then_inc(d_uTst, 16)
                    sp.wait_ge(d_uTst, 16)
                    for i in range(LOC):
                        sp.dma_start(u_loc[i * CH:(i + 1) * CH],
                                     u_dram.rearrange("(g c) (i k) -> i c g k", c=CH, k=NCH)[LOC - 1 - i]
                                     ).then_inc(d_u, 16)
                if r == 0 and 0 <= b < NB:
                    sp.wait_ge(S["cl_ready"], b + 1)
                    sp.dma_start(c_dram[:, s5_group(b)],
                                 cl[:, b % 2, :, 1:].rearrange("p g d c -> p g (d c)")).then_inc(d_clst[b % 2], 16)
                    sp.wait_ge(S["kst_ready"], b + 1)
                    for q in range(4):
                        sp.dma_start(k_dram.rearrange("(b h q) c w -> b q c h w", h=2, q=4)[b, q],
                                     kst[32 * q:32 * q + CH]).then_inc(d_kst, 16)
                if n == 76:
                    sp.wait_ge(d_kst, 16 * 4 * NB)
                    for x in range(2):
                        sp.wait_ge(d_clst[x], 16 * NB // 2)
                    sp.wait_ge(S["tab_mm"], NB)
                    for i in range(LOC):
                        sp.dma_start(u_loc2[i * CH:(i + 1) * CH],
                                     u_dram.rearrange("(g c) (i k) -> i c g k", c=CH, k=NCH)[LOC - 1 - i]
                                     ).then_inc(d_u2, 16)
                    for t in range(2):
                        load_mt(t)
                        load_clr(t)
                if n in (78, 79):
                    load_decay(n - 78)

            def load_decay(h):
                if h < 2:
                    sp.wait_ge(S["v_mm"], NB)
                else:
                    sp.wait_ge(S["sT_ready"], h - 1)
                sp.dma_start(dec[:, h % 2], A["decay"][h]).then_inc(d_dec[h % 2], 16)

            def load_mt(t):
                if t >= 2:
                    sp.wait_ge(S["y_mm"], 2 * (t - 1))
                for i in range(LOC):
                    sp.dma_start(mt[i * CH:(i + 1) * CH, t % 2],
                                 k_dram[16 * t:16 * t + 16, :, i * CH:i * CH + P].rearrange("g c w -> c g w")
                                 ).then_inc(d_mt[t % 2], 16)

            def load_clr(b):
                if b >= 2:
                    sp.wait_ge(S["y_mm"], b - 1)
                sp.dma_start(clr[:, b % 2], c_dram[:, s5_group(b)]).then_inc(d_clr[b % 2], 16)

            for r in range(4):
                sp.dma_start(xT[:, 4 * r:4 * r + 4], A["xT"][:, 4 * r:4 * r + 4]).then_inc(d_xT[r], 16)
                if r < 2:
                    load(2 * r, chunk_source(2 * r))
                    load(2 * r + 1, chunk_source(2 * r + 1))
            for n in range(4, 84):
                before(n)
                load(n, chunk_source(n))
            for h in range(2, 4):
                load_decay(h)
            for b in range(2, NB):
                load_clr(b)
                if b in (3, 5):
                    load_mt((b + 1) // 2)
            for h in range(4, 6):
                load_decay(h)
            sp.wait_ge(S["y1_ready"], 4)
            for j in range(LOC):
                sp.dma_start(y_dram.rearrange("(g c) (j k) -> j c g k", c=CH, k=NCH)[j],
                             y1[j * CH:(j + 1) * CH]).then_inc(d_y1st, 16)
            for h in range(6, 8):
                load_decay(h)
            sp.wait_ge(d_y1st, 16 * LOC)
            sp.wait_ge(S["qk_mm"], 4)
            sp.dma_start(y1T[:], y_dram.rearrange("(b r) p -> r b p", r=P)).then_inc(d_y1T, 16)
            sp.wait_ge(S["y_mm"], NB)
            sp.dma_start(x2[:], A["x_tok"]).then_inc(d_xres, 16)
            for n in range(84, LOOP0):
                load(n, chunk_source(n))
            sp.wait_ge(S["ret_ready"], 2)
            sp.dma_start(g_final[:], A["g_final"]).then_inc(d_gfin, 16)
            with sp.Fori(0, FG - 1) as j:
                for c in range(TURN):
                    if c < 2 * GRP:
                        w = A["w_gate"] if c < GRP else A["w_up"]
                        k = 2 * (c % GRP)
                        src = w[k * P:(k + 2) * P, bass.ds((j + 1) * NCOL, NCOL)]
                    else:
                        col, k = divmod(c - 2 * GRP, 2)
                        src = A["w_down"][bass.ds(j * (4 * P) + 2 * k * P, 2 * P), col * NCOL:(col + 1) * NCOL]
                    load((None, LOOP0 + c), src.rearrange("(b p) n -> p b n", p=P), turn=j)
            for c in range(GRP):
                col, k = divmod(c, 2)
                row = (FG - 1) * 4 * P + 2 * k * P
                load(TAIL0 + c, A["w_down"][row:row + 2 * P, col * NCOL:(col + 1) * NCOL]
                     .rearrange("(b p) n -> p b n", p=P))
            for t in range(TOK):
                for h in range(2):
                    sp.wait_ge(S["fin_ready"], 2 * t + h + 1)
                    sp.dma_start(out[:, t, 1024 * h:1024 * (h + 1)], x2[:, t, 1024 * h:1024 * (h + 1)]
                                 ).then_inc(d_out, 16)
            sp.wait_ge(d_out, 64)

        @block.scalar
        def _(act):
            def high(n, turn=None, at=None):
                if turn is None:
                    act.wait_ge(d_raw[n % RAW], 16 * (n // RAW + 1))
                    if n >= SPL:
                        act.wait_ge(S["pe_done"], n - SPL + 1)
                    s = n
                else:
                    s = at
                    act.wait_ge(d_raw[s % RAW], turn * (16 * TURN // RAW) + 16 * (s // RAW + 1))
                    act.wait_ge(S["pe_done"], turn * TURN + (s - SPL + 1))
                nc.scalar.activation(w_hi[:, s % SPL], raw[:, s % RAW], ACT.Copy).then_inc(S["high_done"], 1)

            def xh(r):
                act.wait_ge(S["xg_ready"], r + 1)
                dst = (actA_hi, actB_hi)[r // 2][:, 4 * (r % 2):4 * (r % 2) + 4]
                nc.scalar.activation(dst, xT[:, 4 * r:4 * r + 4], ACT.Copy).then_inc(S["xh_ready"], 1)

            act.dma_start(vec[:], A["vec"]).then_inc(d_vec, 16)
            act.dma_start(par[:], A["par"]).then_inc(d_par, 16)
            act.dma_start(x_tok[:], A["x_tok"]).then_inc(d_xtok, 16)
            act.dma_start(bc[:], A["bc"]).then_inc(d_bc, 16)
            act.dma_start(ident[:], A["ident"]).then_inc(d_rope, 16)
            act.dma_start(dsk[:], A["dsk"]).then_inc(d_rope, 16)
            act.dma_start(eye16[:], A["eye16"]).then_inc(d_rope, 16)
            act.dma_start(rope[:], A["rope"]).then_inc(d_rope, 16)

            def ret_out(p):
                act.wait_ge(S["head_mm"], 2 * p + 2)
                nc.scalar.activation(ret[:, 2 * p:2 * p + 2].rearrange("p h s -> p (h s)"), ps[:, 6 + p % 2],
                                     ACT.Copy).then_inc(S["out_free"], 1)

            def qk_evac(i):
                act.wait_ge(S["qk_mm"], i + 1)
                dst = (qT, kT)[i // 2][:, 4 * (i % 2):4 * (i % 2) + 4]
                nc.scalar.activation(dst.rearrange("p (a b) s -> p a (b s)", a=2), ps[:, 4:6], ACT.Copy
                                     ).then_inc(S["qk_free"], 1)

            def side(n):
                gi, r = divmod(n - 4 - (GRP - 1), GRP)
                if n in (5, 6):
                    t = n - 5
                    if t == 0:
                        act.wait_ge(d_xtok, 16)
                    else:
                        act.wait_ge(S["ss_ready"], 1)
                    nc.scalar.activation(ps[:, 4:8], x_tok[:, t].rearrange("p (a b) -> p a b", a=4), ACT.Square,
                                         accum_out=ss[:, R_MIX, t:t + 1]).then_inc(S["ss_ready"], 1)
                if n == 9:
                    act.wait_ge(S["trig_in_ready"], 1)
                    nc.scalar.activation(scr[:, 6], scr[:, 4], ACT.Sin).then_inc(S["trig_ready"], 1)
                    nc.scalar.activation(scr[:, 7], scr[:, 4], ACT.Sin, scale=0.5).then_inc(S["trig_ready"], 1)
                if r == 0 and 0 <= gi < len(IN_COLS):
                    c = IN_COLS[gi]
                    if gi == 0:
                        act.wait_ge(S["rstd_mix_ready"], 1)
                    act.wait_ge(S["pe_done"], GRP * (gi + 1))
                    for t in range(TOK):
                        src = ps[:, 2 * (gi % 2) + t]
                        scale = rstd[:, R_MIX, t:t + 1]
                        half_ = (c % 2) * NCOL
                        if c >= 8:
                            dst, func = u_tok[:, t, half_:half_ + NCOL], ACT.Copy
                        elif c >= 6:
                            dst, func = sg[:, t, half_:half_ + NCOL], ACT.Silu
                        elif c >= 4:
                            dst, func = v[:, t, half_:half_ + NCOL], ACT.Copy
                        else:
                            dst, func = qs[:, t], ACT.Copy
                            if gi == 6 and t == 0:
                                act.wait_ge(S["cl_ready"], NB)
                                act.wait_ge(S["wb_ready"], NB)
                                act.wait_ge(S["tab_mm"], NB)
                            if t == 0 and gi > 6:
                                act.wait_ge(S["qr_ready"], gi - 6)
                        if gi == 4 and t == 0:
                            act.wait_ge(d_uTst, 16)
                        nc.scalar.activation(dst, src, func, scale=scale).then_inc(S["proj_free"], 1)
                if n == 25:
                    act.wait_ge(S["uT_mm"], 1)
                    nc.scalar.activation(uT[:].rearrange("p (a b) s -> p a (b s)", a=4), ps[:, 4:8], ACT.Copy
                                         ).then_inc(S["u_copied"], 1)
                b, r = divmod(n - (S5_AT + 7), S5_STEP)
                if r == 0 and 0 <= b < NB:
                    act.wait_ge(S["tab_mm"], b + 1)
                    if b:
                        act.wait_ge(S["v_mm"], b)
                    src = ps[:, 4:6].rearrange("p a (g s) -> p (a g) s", g=4)
                    nc.scalar.activation(wbT_v[:, :, 0:2 * STATE], src, ACT.Copy).then_inc(S["wbT_ready"], 1)
                    nc.scalar.activation(wbT_v[:, :, 2 * STATE:], src[:, :, 0:STATE], ACT.Copy
                                         ).then_inc(S["wbT_ready"], 1)
                    if b == 0:
                        act.wait_ge(S["const_ready"], 1)
                    else:
                        act.wait_ge(d_kst, 64 * b)
                    nc.scalar.activation(kst_w[:, :, LOC - 1:], ps[:, 6, 0:2 * P]
                                         .rearrange("p (h d c) -> p h d c", h=2, c=CH), ACT.Copy
                                         ).then_inc(S["kpsum_free"], 1)
                b, r = divmod(n - (S5_AT + 12), S5_STEP)
                if r == 0 and 0 <= b < NB:
                    act.wait_ge(S["v_mm"], b + 1)
                    for x in range(2):
                        dst = state[:, :, x, s5_group(b)].rearrange("p k g -> p g k")
                        src = ps[:, 7, 256 * x:256 * (x + 1)].rearrange("p (g k) -> p g k", g=BG)
                        nc.scalar.activation(dst, src, ACT.Copy, scale=vec[:, V_SGN:V_SGN + 1] if x else 1.0
                                             ).then_inc(S["v_free"], 1)
                if n in (66, 74, 82):
                    qk_evac((n - 66) // 8)

            xh(0)
            for n in range(84):
                high(n)
                if n in (1, 3, 5):
                    xh(n // 2 + 1)
                side(n)
            for p in range(2):
                ret_out(p)
            for t in range(4):
                act.wait_ge(S["y_mm"], 2 * t + 2)
                nc.scalar.activation(y1[:, 16 * t:16 * t + 16].rearrange("p g k -> p (g k)"), ps[:, 4 + t],
                                     ACT.Gelu_apprx_tanh).then_inc(S["y1_ready"], 1)
            qk_evac(3)
            for p in range(2, 4):
                ret_out(p)
            act.wait_ge(d_y1T, 16)
            for q in range(2):
                nc.scalar.activation(y1T_hi[:, 4 * q:4 * q + 4], y1T[:, 4 * q:4 * q + 4], ACT.Copy
                                     ).then_inc(S["y1T_hi_ready"], 1)

            def glu_half(q):
                act.wait_ge(S["pe_done"], GLU0 + 4 * q + 4)
                for c in range(4):
                    c8 = 4 * q + c
                    nc.scalar.activation(zT[:, c8], ps[:, c8, 0:SEQ], ACT.Sigmoid,
                                         bias=vec[:, V_BGLU + c8:V_BGLU + c8 + 1]).then_inc(S["sig_ready"], 1)
                act.wait_ge(S["zT_ready"], q + 1)
                nc.scalar.activation(sqT[:, 4 * q:4 * q + 4], zT[:, 4 * q:4 * q + 4], ACT.Square
                                     ).then_inc(S["sqT_ready"], 1)
                for c in range(4):
                    c8 = 4 * q + c
                    nc.scalar.activation(actB_hi[:, c8], zT[:, c8], ACT.Copy,
                                         scale=vec[:, V_OUTG + c8:V_OUTG + c8 + 1]).then_inc(S["ssm_hi"], 1)

            def ret_high():
                for p in range(4):
                    act.wait_ge(S["retT_mm"], p + 1)
                    for h in range(2):
                        nc.scalar.activation(actA_hi[:, 2 * p + h], ps[:, p, SEQ * h:SEQ * (h + 1)], ACT.Copy,
                                             scale=vec[:, V_RETG + 2 * p + h:V_RETG + 2 * p + h + 1]
                                             ).then_inc(S["ret_hi"], 1)

            def h2_high(c):
                act.wait_ge(S["h2_mm"], c + 1)
                for k in range(4):
                    kb = 4 * c + k
                    src = ps[:, 4 + 2 * (c % 2) + k // 2, SEQ * (k % 2):SEQ * (k % 2 + 1)]
                    nc.scalar.activation(h2(kb, 0), src, ACT.Copy, scale=vec[:, V_FFN + kb:V_FFN + kb + 1]
                                         ).then_inc(S["h2_hi"], 1)

            def x2_square(c):
                act.wait_ge(S["cols_added"], 5 + c)
                for t in range(TOK):
                    if c or t:
                        act.wait_ge(S["x2_sq"], 2 * c + t)
                    nc.scalar.activation(sqT[:, 0:2].rearrange("p a s -> p (a s)"),
                                         x2[:, t, NCOL * c:NCOL * (c + 1)], ACT.Square,
                                         accum_out=ss4[:, 0, c, t:t + 1]).then_inc(S["x2_sq"], 1)

            for n in range(84, FFN0 + GRP + 4):
                high(n)
                if n == GLU0 + 7:
                    glu_half(0)
                if n == RET0 + 3:
                    ret_high()
                    glu_half(1)
                c, r = divmod(n - (SSM0 + 9), 4)
                if r == 0 and 0 <= c < 4:
                    h2_high(c)
                    x2_square(c)

            def silu(chunks):
                act.wait_ge(S["pe_done"], chunks)
                for t in range(TOK):
                    nc.scalar.activation(ff_act[:, t], ps[:, t], ACT.Silu, scale=rstd[:, R_FFN, t:t + 1]
                                         ).then_inc(S["silu_ready"], 1)

            def ffT_high(count):
                act.wait_ge(S["ffT_mm"], count)
                nc.scalar.activation(ffT_hi[:].rearrange("p (a b) s -> p a (b s)", a=2), ps[:, 4:6], ACT.Copy
                                     ).then_inc(S["ffT_hi_ready"], 1)

            act.wait_ge(S["rstd_ffn_ready"], 1)
            silu(FFN0 + GRP)
            for n in range(FFN0 + GRP + 4, LOOP0 + SPL):
                high(n)
            with act.Fori(0, FG - 1) as j:
                for c in range(SPL, TURN + SPL):
                    high(None, turn=j, at=LOOP0 + c)
                    if c == GRP + SPL - 1:
                        ffT_high(j + 1)
                        silu(j * TURN + (LOOP0 + GRP))
            ffT_high(FG)
            for c in range(SPL, GRP):
                high(TAIL0 + c)
            for c in range(4):
                act.wait_ge(S["cols_added"], 8 + 4 * (FG - 1) + c + 1)
                for t in range(TOK):
                    if c or t:
                        act.wait_ge(S["fin_sq"], 2 * c + t)
                    nc.scalar.activation(sqT[:, 0:2].rearrange("p a s -> p (a s)"),
                                         x2[:, t, NCOL * c:NCOL * (c + 1)], ACT.Square,
                                         accum_out=ss4[:, 1, c, t:t + 1]).then_inc(S["fin_sq"], 1)

        @block.vector
        def _(dve):
            steps = [0]

            def link(ins):
                steps[0] += 1
                ins.then_inc(S["dve_step"], 1)
                dve.wait_ge(S["dve_step"], steps[0])

            tt, ts, stt = nc.vector.tensor_tensor, nc.vector.tensor_scalar, nc.vector.scalar_tensor_tensor

            def low(n, turn=None, at=None):
                if turn is None:
                    dve.wait_ge(S["high_done"], n + 1)
                    s = n
                else:
                    s = at
                    dve.wait_ge(S["high_done"], turn * TURN + (s + 1))
                tt(w_lo[:, s % SPL], raw[:, s % RAW], w_hi[:, s % SPL].bitcast(F32), ALU.subtract
                   ).then_inc(S["low_done"], 1)

            def xg(r):
                dve.wait_ge(d_xT[r], 16)
                if r == 0:
                    dve.wait_ge(d_vec, 16)
                part = xT[:, 4 * r:4 * r + 4]
                gain = vec[:, V_MIX + 4 * r:V_MIX + 4 * r + 4].unsqueeze(2).to_broadcast([P, 4, SEQ])
                tt(part, part, gain, ALU.mult).then_inc(S["xg_ready"], 1)
                dve.wait_ge(S["xh_ready"], r + 1)
                hi, lo = ((actA_hi, actA_lo), (actB_hi, actB_lo))[r // 2]
                at = slice(4 * (r % 2), 4 * (r % 2) + 4)
                tt(lo[:, at], part, hi[:, at].bitcast(F32), ALU.subtract).then_inc(S["xl_ready"], 1)

            a_re, a_im = par[:, 0], par[:, 1]
            C1, C2, C3 = 6.28125, 0.0019350051879882812, 3.019916050561733e-07
            MAGIC = 12582912.0

            def angles():
                dve.wait_ge(d_par, 16)
                dve.wait_ge(S["dt_ready"], 1)
                tt(scr[:, 1], a_re, scr[:, 0], ALU.mult).then_inc(S["mag_ready"], 1)
                link(tt(scr[:, 2], a_im, scr[:, 0], ALU.mult))
                link(ts(scr[:, 3], scr[:, 2], 1 / (2 * np.pi), MAGIC, ALU.mult, ALU.add))
                link(ts(scr[:, 3], scr[:, 3], -MAGIC, None, ALU.add))
                link(stt(scr[:, 8], scr[:, 3], -C1, scr[:, 2], ALU.mult, ALU.add))
                link(stt(scr[:, 9], scr[:, 3], -C2, scr[:, 8], ALU.mult, ALU.add))
                link(stt(scr[:, 10], scr[:, 3], -C3, scr[:, 9], ALU.mult, ALU.add))
                ts(scr[:, 4], scr[:, 10], -3.1415925, 3.1415925, ALU.max, ALU.min).then_inc(S["trig_in_ready"], 1)

            def complex_mul(o_r, o_i, x_r, x_i, y_r, y_i, t_r, t_i):
                tt(t_r, x_i, y_i, ALU.mult)
                tt(t_i, x_i, y_r, ALU.mult)
                tt(o_r, x_r, y_r, ALU.mult)
                link(tt(o_i, x_r, y_i, ALU.mult))
                tt(o_r, o_r, t_r, ALU.subtract)
                link(tt(o_i, o_i, t_i, ALU.add))

            def s5_params():
                dve.wait_ge(S["trig_ready"], 2)
                dve.wait_ge(S["pow_ready"], 1)
                mag, sin, sinh = scr[:, 5], scr[:, 6], scr[:, 7]
                link(tt(scr[:, 8], sinh, sinh, ALU.mult))
                link(ts(scr[:, 8], scr[:, 8], -2.0, 1.0, ALU.mult, ALU.add))
                nc.vector.memset(pr[:, 0], 1.0)
                nc.vector.memset(pi[:, 0], 0.0)
                tt(pr[:, 1], mag, scr[:, 8], ALU.mult)
                link(tt(pi[:, 1], mag, sin, ALU.mult))
                link(ts(scr[:, 8], pr[:, 1], -1.0, None, ALU.add))
                tt(scr[:, 9], a_re, a_re, ALU.mult)
                link(tt(scr[:, 10], a_im, a_im, ALU.mult))
                link(tt(scr[:, 9], scr[:, 9], scr[:, 10], ALU.add))
                link(nc.vector.reciprocal(scr[:, 9], scr[:, 9]))
                tt(scr[:, 10], scr[:, 8], a_re, ALU.mult)
                tt(scr[:, 11], pi[:, 1], a_im, ALU.mult)
                tt(scr[:, 12], pi[:, 1], a_re, ALU.mult)
                link(tt(scr[:, 13], scr[:, 8], a_im, ALU.mult))
                tt(scr[:, 10], scr[:, 10], scr[:, 11], ALU.add)
                link(tt(scr[:, 12], scr[:, 12], scr[:, 13], ALU.subtract))
                tt(scr[:, 10], scr[:, 10], scr[:, 9], ALU.mult)
                link(tt(scr[:, 12], scr[:, 12], scr[:, 9], ALU.mult))

            def s5_powers():
                def two(x, a, b):
                    return x[:, a:b]

                def wide(x, k, n):
                    return x[:, k].unsqueeze(1).to_broadcast([P, n, GROUPS])

                tr = cl_t[:].rearrange("p g d c -> p (g d c)")[:, 0:4 * GROUPS].rearrange("p (a g) -> p a g", a=4)
                ti = cl_t[:].rearrange("p g d c -> p (g d c)")[:, 4 * GROUPS:8 * GROUPS].rearrange(
                    "p (a g) -> p a g", a=4)
                for done in (1, 2, 4):
                    complex_mul(pr[:, done + 1:2 * done + 1], pi[:, done + 1:2 * done + 1],
                                pr[:, 1:done + 1], pi[:, 1:done + 1], wide(pr, done, done), wide(pi, done, done),
                                tr[:, 0:done], ti[:, 0:done])
                nc.vector.tensor_copy(mul_r[:, 0], pr[:, LOC])
                nc.vector.tensor_copy(mul_r[:, 1], pr[:, LOC])
                nc.vector.tensor_copy(mul_i[:, 0], pi[:, LOC])
                ts(mul_i[:, 1], pi[:, LOC], -1.0, None, ALU.mult).then_inc(S["mul_ready"], 1)

            def s5_inputs():
                sgn = vec[:, V_SGN:V_SGN + 1]
                dve.wait_ge(d_bc, 16)

                def wide(k):
                    return scr[:, k].unsqueeze(2).to_broadcast([P, GROUPS, CH])

                nc.vector.memset(bb[:, GROUPS], 0.0)
                ts(bc[:, 1], bc[:, 1], sgn, None, ALU.mult)
                ts(bc[:, 2], bc[:, 2], sgn, -1.0, ALU.mult, ALU.mult)
                link(ts(bc[:, 3], bc[:, 3], -1.0, None, ALU.mult))
                t_a, t_b = (cl[:].rearrange("p a g d c -> p (a g d c)")[:, 1024 * k:1024 * (k + 1)]
                            .rearrange("p (g c) -> p g c", c=CH) for k in range(2))
                tt(bb[:, 0:GROUPS], bc[:, 0], wide(10), ALU.mult)
                tt(t_a, bc[:, 1], wide(12), ALU.mult)
                tt(bbx[:], bc[:, 1], wide(10), ALU.mult)
                link(tt(t_b, bc[:, 0], wide(12), ALU.mult))
                tt(bb[:, 0:GROUPS], bb[:, 0:GROUPS], t_a, ALU.add)
                tt(bbx[:], bbx[:], t_b, ALU.subtract).then_inc(S["inputs_ready"], 1)

            def d_skip():
                dve.wait_ge(d_rope, 64)
                link(tt(dtmp[:], dsk[:].unsqueeze(2).to_broadcast([P, GROUPS // 4, CH]),
                        eye16[:].unsqueeze(1).to_broadcast([P, GROUPS // 4, CH]), ALU.mult))

            def cl_table(b):
                o = cl[:, b % 2]
                if b >= 2:
                    dve.wait_ge(d_clst[b % 2], 16 * (b // 2))
                    dve.wait_ge(S["tab_mm"], b - 1)

                if b:
                    dve.wait_ge(S["cl_ready"], b)

                def c_(k):
                    return bc[:, k, s5_group(b)].unsqueeze(2).to_broadcast([P, BG, LOC + 1, CH])

                def p_(x):
                    return x[:, :, s5_group(b)].rearrange("p d g -> p g d").unsqueeze(3).to_broadcast(
                        [P, BG, LOC + 1, CH])

                tt(o, c_(2), p_(pr), ALU.mult)
                link(tt(cl_t[:], c_(3), p_(pi), ALU.mult))
                tt(o, o, cl_t[:], ALU.add).then_inc(S["cl_ready"], 1)

            def rotate(i):
                dve.wait_ge(S["proj_free"], 2 * (6 + i) + 2)
                if i:
                    dve.wait_ge(S["qk_mm"], i)
                four = [P, 4, HEAD_DIM]
                x = [qs[:, t].rearrange("p (h d) -> p h d", h=4) for t in range(TOK)]
                y = [qr[:, t].rearrange("p (h d) -> p h d", h=4) for t in range(TOK)]
                for t in range(TOK):
                    last = tt(y[t], x[t], rope[:, t, 0].unsqueeze(1).to_broadcast(four), ALU.mult)
                for t in range(TOK):
                    for a in range(2):
                        lo_, hi_ = slice(64 * a, 64 * a + 64), slice(64 * (1 - a), 64 * (1 - a) + 64)
                        last = tt(rot[:, t].rearrange("p (h d) -> p h d", h=4)[:, :, lo_], x[t][:, :, hi_],
                                  rope[:, t, 1, lo_].unsqueeze(1).to_broadcast([P, 4, 64]), ALU.mult)
                link(last)
                tt(qr[:], qr[:], rot[:], ALU.add).then_inc(S["qr_ready"], 1)

            def decayed(h):
                dve.wait_ge(S["score_mm"], h + 1)
                dve.wait_ge(d_dec[h % 2], 16 * (h // 2 + 1))
                if h >= 2:
                    dve.wait_ge(S["head_mm"], h - 1)
                tt(sT[:, h % 2].rearrange("p a s -> p (a s)"), ps[:, 4 + h % 2],
                   dec[:, h % 2].rearrange("p a s -> p (a s)"), ALU.mult).then_inc(S["sT_ready"], 1)

            def head_stats(p):
                dve.wait_ge(S["out_free"], p + 1)
                last = None
                for k in range(4 * p, 4 * p + 4):
                    last = nc.vector.bn_stats(bn[:, k], ret[:, k // 2, P * (k % 2):P * (k % 2 + 1)])
                link(last)
                for k in range(4 * p, 4 * p + 4):
                    last = nc.vector.bn_aggr(mv[:, k], bn[:, k])
                if p % 2:
                    last.then_inc(S["bn_ready"], 1)

            def normalise(q):
                dve.wait_ge(S["rret_ready"], q + 1)
                for h in range(4 * q, 4 * q + 4):
                    for t in range(TOK):
                        g = sg[:, t, P * h:P * (h + 1)]
                        last = ts(g, g, rret[:, 2 * h + t:2 * h + t + 1], None, ALU.mult)
                link(last)
                for h in range(4 * q, 4 * q + 4):
                    for t in range(TOK):
                        o = ret[:, h, P * t:P * (t + 1)]
                        last = stt(o, o, mv[:, 2 * h + t, 0:1], sg[:, t, P * h:P * (h + 1)], ALU.subtract, ALU.mult)
                last.then_inc(S["ret_ready"], 1)

            def y1_low(q):
                dve.wait_ge(S["y1T_hi_ready"], q + 1)
                at = slice(4 * q, 4 * q + 4)
                tt(y1T_lo[:, at], y1T[:, at], y1T_hi[:, at].bitcast(F32), ALU.subtract
                   ).then_inc(S["y1T_lo_ready"], 1)

            def gain_low(dst, src, at, hi):
                return stt(dst, src, vec[:, at:at + 1], hi.bitcast(F32), ALU.mult, ALU.subtract)

            def glu_half(q):
                dve.wait_ge(S["sig_ready"], 4 * q + 4)
                at = slice(4 * q, 4 * q + 4)
                tt(zT[:, at], zT[:, at], y1T[:, at], ALU.mult).then_inc(S["zT_ready"], 1)
                dve.wait_ge(S["ssm_hi"], 4 * q + 4)
                dve.wait_ge(S["zT_ready"], q + 1)
                for c in range(4 * q, 4 * q + 4):
                    gain_low(actB_lo[:, c], zT[:, c], V_OUTG + c, actB_hi[:, c]).then_inc(S["ssm_lo"], 1)

            def ret_low():
                for p in range(4):
                    dve.wait_ge(S["ret_hi"], 2 * p + 2)
                    for h in range(2):
                        gain_low(actA_lo[:, 2 * p + h], ps[:, p, SEQ * h:SEQ * (h + 1)], V_RETG + 2 * p + h,
                                 actA_hi[:, 2 * p + h]).then_inc(S["ret_lo"], 1)

            def h2_low(c):
                for k in range(4):
                    kb = 4 * c + k
                    if k % 2 == 0:
                        dve.wait_ge(S["h2_hi"], kb + 2)
                    src = ps[:, 4 + 2 * (c % 2) + k // 2, SEQ * (k % 2):SEQ * (k % 2 + 1)]
                    gain_low(h2(kb, 1), src, V_FFN + kb, h2(kb, 0)).then_inc(S["h2_lo"], 1)

            def out_col_ret(c):
                if c == 0:
                    dve.wait_ge(d_xres, 16)
                dve.wait_ge(S["pe_done"], RET0 + 4 * (c + 1))
                cols = x2[:, :, NCOL * c:NCOL * (c + 1)]
                b0 = 2 * (c % 2)
                tt(cols, ps[:, b0:b0 + 2], cols, ALU.add).then_inc(S["cols_added"], 1)

            def out_col_ssm(c):
                if c == 0:
                    dve.wait_ge(S["rstd_ssm_ready"], 1)
                dve.wait_ge(S["pe_done"], SSM0 + 4 * (c + 1))
                dve.wait_ge(S["cols_added"], c + 1)
                for t in range(TOK):
                    cols = x2[:, t, NCOL * c:NCOL * (c + 1)]
                    last = stt(cols, ps[:, 2 * (c % 2) + t], rstd[:, R_SSM, t:t + 1], cols, ALU.mult, ALU.add)
                last.then_inc(S["cols_added"], 1)

            def ff(count, chunks):
                dve.wait_ge(S["pe_done"], chunks)
                dve.wait_ge(S["silu_ready"], count * 2)
                for t in range(TOK):
                    last = stt(ff_act[:, t], ps[:, 2 + t], rstd[:, R_FFN, t:t + 1], ff_act[:, t], ALU.mult, ALU.mult)
                last.then_inc(S["ff_ready"], 1)

            def ffT_low(count):
                dve.wait_ge(S["ffT_hi_ready"], count)
                tt(ffT_lo[:].rearrange("p (a b) s -> p a (b s)", a=2), ps[:, 4:6],
                   ffT_hi[:].rearrange("p (a b) s -> p a (b s)", a=2).bitcast(F32), ALU.subtract
                   ).then_inc(S["ffT_lo_ready"], 1)

            def down_col(chunks, before, c):
                dve.wait_ge(S["pe_done"], chunks)
                dve.wait_ge(S["cols_added"], before)
                b0 = 6 - 2 * (c % 2)
                cols = x2[:, :, NCOL * c:NCOL * (c + 1)]
                tt(cols, ps[:, b0:b0 + 2], cols, ALU.add).then_inc(S["cols_added"], 1)

            def side(n):
                if n == 7:
                    angles()
                if n == 13:
                    s5_params()
                if n == 15:
                    s5_powers()
                if n == 16:
                    s5_inputs()
                if n == 17:
                    d_skip()
                b, r = divmod(n - S5_AT, S5_STEP)
                if r == 0 and 0 <= b < NB:
                    cl_table(b)
                b, r = divmod(n - (S5_AT + 7), S5_STEP)
                if r == 0 and 0 <= b < NB:
                    dve.wait_ge(S["kpsum_free"], b + 1)
                    diag = kst_w[:, :, LOC - 1]
                    tt(diag, diag, dtmp[:, 2 * b:2 * b + 2], ALU.add).then_inc(S["kst_ready"], 1)
                if n in (59, 67, 75):
                    rotate((n - 59) // 8)

            for n in range(84):
                if n in (0, 2, 4, 6):
                    xg(n // 2)
                low(n)
                side(n)
            for h in range(4):
                decayed(h)
            rotate(3)
            head_stats(0)
            head_stats(1)
            normalise(0)
            for h in range(4, 8):
                decayed(h)
            for q in range(2):
                y1_low(q)
            head_stats(2)
            head_stats(3)
            normalise(1)
            for n in range(84, LOOP0 + SPL):
                low(n)
                if n == GLU0 + 7:
                    glu_half(0)
                if n == RET0 + 3:
                    ret_low()
                    glu_half(1)
                if n == RET0 + 8:
                    dve.wait_ge(S["ssq_mm"], 1)
                    ts(ss[:, R_SSM], ps[:, 4, 0:TOK], 1 / RET_W, EPS, ALU.mult, ALU.add).then_inc(S["ssq_ready"], 1)
                c, r = divmod(n - (RET0 + 7), 4)
                if r == 0 and 0 <= c < 4:
                    out_col_ret(c)
                if r == 0 and 4 <= c < 8:
                    out_col_ssm(c - 4)
                c, r = divmod(n - (SSM0 + 9), 4)
                if r == 0 and 0 <= c < 4:
                    h2_low(c)
                if n == LOOP0 + 3:
                    ff(1, LOOP0)
            with dve.Fori(0, FG - 1) as j:
                for c in range(SPL, TURN + SPL):
                    low(None, turn=j, at=LOOP0 + c)
                    if c == GRP + 3:
                        ffT_low(j + 1)
                    if c == 2 * GRP + 3:
                        ff(j + 2, j * TURN + (LOOP0 + 2 * GRP))
                    if c >= 2 * GRP + 5 and c % 2:
                        col = (c - 2 * GRP - 5) // 2
                        down_col(j * TURN + (LOOP0 + 2 * GRP + 2 * col + 2), j * 4 + (col + 5), col)
            ffT_low(FG)
            for c in range(SPL, GRP):
                low(TAIL0 + c)
            for col in range(4):
                down_col(TAIL0 + 2 * col + 2, 4 * (FG - 1) + col + 5, col)
            dve.wait_ge(d_gfin, 16)
            dve.wait_ge(S["cols_added"], 8 + 4 * FG)
            dve.wait_ge(S["rstd_fin_ready"], 1)
            for t in range(TOK):
                for h in range(2):
                    at = slice(1024 * h, 1024 * (h + 1))
                    stt(x2[:, t, at], x2[:, t, at], rstd[:, R_FIN, t:t + 1], g_final[:, at], ALU.mult, ALU.mult
                        ).then_inc(S["fin_ready"], 1)

        @block.gpsimd
        def _(pool):
            steps = [0]

            def link(ins):
                steps[0] += 1
                ins.then_inc(S["pool_step"], 1)
                pool.wait_ge(S["pool_step"], steps[0])

            tt, ts = nc.gpsimd.tensor_tensor, nc.gpsimd.tensor_scalar

            def rsqrt(dst, src, ready, width=TOK):
                tt(dst, src, half[:, 0:width], ALU.pow).then_inc(ready, 1)

            nc.gpsimd.memset(half[:], -0.5)
            nc.gpsimd.memset(ones[:], 1.0)
            nc.gpsimd.memset(kst_w[:, :, 0:LOC - 1], 0.0).then_inc(S["const_ready"], 1)
            link(nc.gpsimd.memset(e_tile[:], float(np.e)))
            pool.wait_ge(d_par, 16)
            tt(scr[:, 0], e_tile[:], par[:, 2], ALU.pow).then_inc(S["dt_ready"], 1)
            pool.wait_ge(S["ss_ready"], 2)
            link(ts(ss[:, R_MIX], ss[:, R_MIX], 1 / D_MODEL, EPS, ALU.mult, ALU.add))
            rsqrt(rstd[:, R_MIX], ss[:, R_MIX], S["rstd_mix_ready"])
            pool.wait_ge(S["mag_ready"], 1)
            tt(scr[:, 5], e_tile[:], scr[:, 1], ALU.pow).then_inc(S["pow_ready"], 1)
            pool.wait_ge(S["mul_ready"], 1)
            for b in range(NB):
                if b == 0:
                    pool.wait_ge(S["inputs_ready"], 1)
                else:
                    pool.wait_ge(S["tab_mm"], b)
                    pool.wait_ge(S["wb_ready"], b)

                def b_(x):
                    return x[:, s5_group(b)].unsqueeze(2).to_broadcast([P, BG, LOC, CH])

                def p_(x):
                    return x[:, 0:LOC, s5_group(b)].rearrange("p d g -> p g d").unsqueeze(3).to_broadcast(
                        [P, BG, LOC, CH])

                tt(wb[:], b_(bb), p_(pr), ALU.mult)
                link(tt(wb_t[:], b_(bbx), p_(pi), ALU.mult))
                tt(wb[:], wb[:], wb_t[:], ALU.add).then_inc(S["wb_ready"], 1)
            pool.wait_ge(S["v_free"], 2 * NB)
            with pool.Fori(0, NCH - 2) as k:
                prev = state[:, bass.ds(k, 1)]
                cur = state[:, bass.ds(k + 1, 1)]
                tt(scan_a[:].unsqueeze(1), prev, mul_r[:].unsqueeze(1), ALU.mult)
                for x in range(2):
                    last = tt(scan_b[:, x:x + 1].unsqueeze(1), prev[:, :, 1 - x:2 - x],
                              mul_i[:, x:x + 1].unsqueeze(1), ALU.mult)
                last.then_inc(S["scan_step"], 1)
                pool.wait_ge(S["scan_step"], k * 3 + 1)
                tt(scan_a[:], scan_a[:], scan_b[:], ALU.add).then_inc(S["scan_step"], 1)
                pool.wait_ge(S["scan_step"], k * 3 + 2)
                tt(cur, cur, scan_a[:].unsqueeze(1), ALU.add).then_inc(S["scan_step"], 1)
                pool.wait_ge(S["scan_step"], k * 3 + 3)
            for q in range(2):
                pool.wait_ge(S["bn_ready"], q + 1)
                at = slice(8 * q, 8 * q + 8)
                link(ts(rv[:, at], mv[:, at, 1], 1.0, EPS, ALU.mult, ALU.add))
                rsqrt(rret[:, at], rv[:, at], S["rret_ready"], 8)
            pool.wait_ge(S["ssq_ready"], 1)
            rsqrt(rstd[:, R_SSM], ss[:, R_SSM], S["rstd_ssm_ready"])
            for i, (src, row, ready) in enumerate((("x2_sq", R_FFN, "rstd_ffn_ready"),
                                                   ("fin_sq", R_FIN, "rstd_fin_ready"))):
                pool.wait_ge(S[src], 8)
                tt(ss4[:, i, 0], ss4[:, i, 0], ss4[:, i, 1], ALU.add)
                link(tt(ss4[:, i, 2], ss4[:, i, 2], ss4[:, i, 3], ALU.add))
                link(tt(ss4[:, i, 0], ss4[:, i, 0], ss4[:, i, 2], ALU.add))
                link(ts(ss[:, row], ss4[:, i, 0], 1 / D_MODEL, EPS, ALU.mult, ALU.add))
                rsqrt(rstd[:, row], ss[:, row], S[ready])

        @block.tensor
        def _(pe):
            mm, tr = nc.tensor.matmul, nc.tensor.transpose

            def three(o, x_hi, x_lo, h, l, first, last):
                mm(o, x_hi, h, start=first, stop=False)
                mm(o, x_hi, l, start=False, stop=False)
                return mm(o, x_lo, h, start=False, stop=last)

            def column_chunk(s, blocks, banks, first, last):
                for k in range(2):
                    at = slice(NCOL * k, NCOL * (k + 1))
                    hi, lo = blocks[k]
                    for t in range(TOK):
                        tok = slice(P * t, P * (t + 1))
                        ins = three(ps[:, banks + t], hi[:, tok], lo[:, tok], w_hi[:, s, at], w_lo[:, s, at],
                                    first and k == 0, last and k == 1)
                ins.then_inc(S["pe_done"], 1)

            def ready(n, turn=None):
                pe.wait_ge(S["low_done"], n + 1 if turn is None else turn * TURN + (n + 1))

            def act_pair(kb):
                return [(act_block(kb + k, 0), act_block(kb + k, 1)) for k in range(2)]

            def h2_pair(kb):
                return [(h2(kb + k, 0), h2(kb + k, 1)) for k in range(2)]

            def ff_pair(kb):
                return [(ffT_hi[:, kb + k], ffT_lo[:, kb + k]) for k in range(2)]

            def u_transposes():
                pe.wait_ge(S["proj_free"], 4)
                pe.wait_ge(S["ss_ready"], 2)
                pe.wait_ge(d_rope, 64)
                for blk in range(8):
                    for t in range(TOK):
                        at = (blk % 2) * SEQ + t * P
                        ins = tr(ps[:, 4 + blk // 2, at:at + P], u_tok[:, t, P * blk:P * (blk + 1)], ident[:])
                ins.then_inc(S["uT_mm"], 1)

            def tables(b):
                pe.wait_ge(S["cl_ready"], b + 1)
                pe.wait_ge(S["wb_ready"], b + 1)
                if b == 0:
                    pe.wait_ge(S["u_copied"], 1)
                else:
                    pe.wait_ge(S["kpsum_free"], b)
                for g in range(BG):
                    h, q = divmod(g, 4)
                    gg = BG * b + g
                    mm(ps[32 * q:32 * q + 32, 6, P * h:P * (h + 1)], bb[:, gg:gg + 2].rearrange("p a c -> p (a c)"),
                       cl[:, b % 2, g, 0:LOC].rearrange("p d c -> p (d c)"), start=True, stop=True)
                for g in range(BG):
                    ins = tr(ps[:, 4 + g // 4, P * (g % 4):P * (g % 4 + 1)],
                             wb[:, g].rearrange("p d c -> p (d c)"), ident[:])
                ins.then_inc(S["tab_mm"], 1)

            def chunk_inputs(b):
                pe.wait_ge(S["wbT_ready"], 2 * b + 2)
                if b == 0:
                    pe.wait_ge(d_u, 16 * LOC)
                else:
                    pe.wait_ge(S["v_free"], 2 * b)
                for x in range(2):
                    for g in range(BG):
                        at = 256 * x + NCH * g
                        ins = mm(ps[:, 7, at:at + NCH], wbT[:, g, STATE * x:STATE * x + P], u_loc[:, BG * b + g],
                                 start=True, stop=True)
                ins.then_inc(S["v_mm"], 1)

            def qk_transposes(i):
                pe.wait_ge(S["qr_ready"], i + 1)
                if i < 3:
                    pe.wait_ge(S["wbT_ready"], 2 * NB)
                    if i:
                        pe.wait_ge(S["qk_free"], i)
                else:
                    pe.wait_ge(S["y1_ready"], 2)
                for h in range(4):
                    for t in range(TOK):
                        at = (h % 2) * SEQ + t * P
                        ins = tr(ps[:, 4 + h // 2, at:at + P], qr[:, t, P * h:P * (h + 1)], ident[:])
                ins.then_inc(S["qk_mm"], 1)

            def pe_score(h):
                if h >= 2:
                    pe.wait_ge(S["sT_ready"], h - 1)
                for a in range(TOK):
                    ins = mm(ps[:, 4 + h % 2, SEQ * a:SEQ * (a + 1)], kT[:, h, P * a:P * (a + 1)], qT[:, h],
                             start=True, stop=True)
                ins.then_inc(S["score_mm"], 1)

            def pe_out(h):
                pe.wait_ge(S["sT_ready"], h + 1)
                if h % 2 == 0:
                    if h == 0:
                        pe.wait_ge(S["proj_free"], 12)
                        pe.wait_ge(S["kpsum_free"], NB)
                        pe.wait_ge(S["v_free"], 2 * NB)
                    elif h == 4:
                        pe.wait_ge(S["y1_ready"], 4)
                for t in range(TOK):
                    at = (h % 2) * SEQ + t * P
                    for a in range(TOK):
                        ins = mm(ps[:, 6 + (h // 2) % 2, at:at + P], sT[:, h % 2, a, P * t:P * (t + 1)],
                                 v[:, a, P * h:P * (h + 1)], start=(a == 0), stop=(a == TOK - 1))
                ins.then_inc(S["head_mm"], 1)

            def heads(h0):
                pe.wait_ge(S["qk_free"], 3 if h0 == 0 else 4)
                pe_score(h0)
                for h in range(h0, h0 + 4):
                    if h + 1 < h0 + 4:
                        pe_score(h + 1)
                    pe_out(h)

            def y_batch(b):
                t = b // 2
                if b == 0:
                    pe.wait_ge(S["scan_step"], 3 * (NCH - 2))
                    pe.wait_ge(d_u2, 16 * LOC)
                    pe.wait_ge(S["sT_ready"], 4)
                    pe.wait_ge(S["out_free"], 2)
                pe.wait_ge(d_mt[t % 2], 16 * LOC * (t // 2 + 1))
                pe.wait_ge(d_clr[b % 2], 16 * (b // 2 + 1))
                for g in range(BG):
                    gg = BG * b + g
                    at = 256 * (b % 2) + NCH * g
                    mm(ps[:, 4 + t, at:at + NCH], mt[:, t % 2, BG * (b % 2) + g], u_loc2[:, gg],
                       start=True, stop=False)
                    ins = mm(ps[:, 4 + t, at + 1:at + NCH], clr[:, b % 2, g], state[:, 0:NCH - 1, 0, gg],
                             start=False, stop=True)
                ins.then_inc(S["y_mm"], 1)

            def ret_transposes():
                pe.wait_ge(S["ret_ready"], 2)
                pe.wait_ge(S["sig_ready"], 4)
                for p in range(4):
                    for h in range(2):
                        for t in range(TOK):
                            at = SEQ * h + P * t
                            ins = tr(ps[:, p, at:at + P], ret[:, 2 * p + h, P * t:P * (t + 1)], ident[:])
                    ins.then_inc(S["retT_mm"], 1)

            def channel_squares():
                pe.wait_ge(S["const_ready"], 1)
                pe.wait_ge(S["sqT_ready"], 2)
                pe.wait_ge(S["sig_ready"], 8)
                for t in range(TOK):
                    for k in range(8):
                        ins = mm(ps[:, 4, t:t + 1], sqT[:, k, P * t:P * (t + 1)], ones[:],
                                 start=(k == 0), stop=(k == 7))
                ins.then_inc(S["ssq_mm"], 1)

            def h2_transposes(c):
                pe.wait_ge(S["cols_added"], 5 + c)
                if c >= 2:
                    pe.wait_ge(S["h2_lo"], 4 * (c - 1))
                elif c == 0:
                    pe.wait_ge(S["ssq_ready"], 1)
                for k in range(4):
                    for t in range(TOK):
                        at = (k % 2) * SEQ + t * P
                        col = P * (4 * c + k)
                        ins = tr(ps[:, 4 + 2 * (c % 2) + k // 2, at:at + P], x2[:, t, col:col + P], ident[:])
                ins.then_inc(S["h2_mm"], 1)

            def ff_transposes(count):
                pe.wait_ge(S["ff_ready"], count)
                for k in range(4):
                    for t in range(TOK):
                        at = (k % 2) * SEQ + t * P
                        ins = tr(ps[:, 4 + k // 2, at:at + P], ff_act[:, t, P * k:P * (k + 1)], ident[:])
                ins.then_inc(S["ffT_mm"], 1)

            for n in range(N_IN):
                gi, i = divmod(n, GRP)
                if n < GRP and n % 2 == 0:
                    pe.wait_ge(S["xl_ready"], n // 2 + 1)
                if i == 0 and gi >= 2:
                    pe.wait_ge(S["proj_free"], 2 * gi - 2)
                ready(n)
                column_chunk(n % SPL, act_pair(2 * i), 2 * (gi % 2), i == 0, i == GRP - 1)
                if n == 20:
                    u_transposes()
                b, r = divmod(n - (S5_AT + 3), S5_STEP)
                if r == 0 and 0 <= b < NB:
                    tables(b)
                b, r = divmod(n - (S5_AT + 8), S5_STEP)
                if r == 0 and 0 <= b < NB:
                    chunk_inputs(b)
                if n in (61, 69, 77):
                    qk_transposes((n - 61) // 8)
            heads(0)
            for b in range(NB):
                y_batch(b)
            qk_transposes(3)
            heads(4)
            for n in range(GLU0, RET0):
                q, i = divmod(n - GLU0, 4)
                if i == 0:
                    if q == 0:
                        pe.wait_ge(S["proj_free"], 20)
                        pe.wait_ge(S["y1T_lo_ready"], 1)
                    else:
                        pe.wait_ge(S["sT_ready"], 8)
                        pe.wait_ge(S["out_free"], 4)
                if i == 2 and q == 0:
                    pe.wait_ge(S["y1T_lo_ready"], 2)
                ready(n)
                for k in range(2):
                    kb = 2 * i + k
                    for c in range(4):
                        at = slice(NCOL * k + P * c, NCOL * k + P * (c + 1))
                        s = n % SPL
                        o = ps[:, 4 * q + c, 0:SEQ]
                        mm(o, w_hi[:, s, at], y1T_hi[:, kb], start=(kb == 0), stop=False)
                        mm(o, w_hi[:, s, at], y1T_lo[:, kb], start=False, stop=False)
                        ins = mm(o, w_lo[:, s, at], y1T_hi[:, kb], start=False, stop=(kb == 7))
                ins.then_inc(S["pe_done"], 1)
            ret_transposes()
            for n in range(RET0, FFN0):
                idx, i = divmod(n - RET0, 4)
                c, part = idx % 4, idx // 4
                if i == 0 and idx >= 2:
                    pe.wait_ge(S["cols_added"], idx - 1)
                if part == 0 and c == 0:
                    pe.wait_ge(S["ret_lo"], max(4, 2 * i + 2))
                if n == RET0 + 4:
                    pe.wait_ge(S["ret_lo"], 8)
                if part == 1 and c == 0 and i == 0:
                    pe.wait_ge(S["ssm_lo"], 8)
                ready(n)
                column_chunk(n % SPL, act_pair(8 * part + 2 * i), 2 * (c % 2), i == 0, i == 3)
                if n == RET0 + 5:
                    channel_squares()
                c, r = divmod(n - (SSM0 + 5), 4)
                if r == 0 and 0 <= c < 4:
                    h2_transposes(c)
            for n in range(FFN0, LOOP0):
                up, i = divmod(n - FFN0, GRP)
                if n == FFN0:
                    pe.wait_ge(S["cols_added"], 7)
                if n == FFN0 + GRP:
                    pe.wait_ge(S["cols_added"], 8)
                if not up and i % 2 == 0:
                    pe.wait_ge(S["h2_lo"], 2 * i + 4)
                ready(n)
                column_chunk(n % SPL, h2_pair(2 * i), 2 * up, i == 0, i == GRP - 1)
                if n == FFN0 + 1:
                    h2_transposes(3)
            with pe.Fori(0, FG - 1) as j:
                for c in range(TURN):
                    part, i = divmod(c, GRP)
                    if c == 0:
                        pe.wait_ge(S["silu_ready"], (j + 1) * 2)
                    if c == GRP:
                        pe.wait_ge(S["ff_ready"], j + 1)
                    if c == 2 * GRP:
                        pe.wait_ge(S["ffT_lo_ready"], j + 1)
                    ready(LOOP0 + c, turn=j)
                    if part < 2:
                        column_chunk(c % SPL, h2_pair(2 * i), 2 * part, i == 0, i == GRP - 1)
                    else:
                        col, k = divmod(i, 2)
                        if k == 0 and col >= 2:
                            pe.wait_ge(S["cols_added"], j * 4 + (7 + col))
                        column_chunk(c % SPL, ff_pair(2 * k), 6 - 2 * (col % 2), k == 0, k == 1)
                    if c == GRP - 1:
                        pe.wait_ge(S["cols_added"], j * 4 + 8)
                        ff_transposes(j + 1)
            pe.wait_ge(S["cols_added"], 8 + 4 * (FG - 1))
            ff_transposes(FG)
            pe.wait_ge(S["ffT_lo_ready"], FG)
            for i in range(GRP):
                col, k = divmod(i, 2)
                if k == 0 and col >= 2:
                    pe.wait_ge(S["cols_added"], 8 + 4 * (FG - 1) + col - 1)
                ready(TAIL0 + i)
                column_chunk(i % SPL, ff_pair(2 * k), 6 - 2 * (col % 2), k == 0, k == 1)


def _time_order():
    return (LOC * np.arange(NCH)[None, :] + np.arange(LOC)[:, None]).reshape(-1)


def _constants():
    time = _time_order()
    f32 = np.float32
    h = np.arange(HEADS, dtype=np.float64)
    log_g = np.log1p(-(2.0 ** (-5.0 - h)))
    n, m = time[None, :], time[:, None]
    seen = (n // CHUNK >= m // CHUNK)
    dist = np.abs(n - m)
    decay = np.where(seen, np.exp(log_g[:, None, None] * dist), 0.0) * HEAD_DIM ** -0.5
    decay = decay.reshape(HEADS, TOK, P, SEQ).transpose(0, 2, 1, 3)
    hd = HEAD_DIM // 2
    freqs = f32(10000.0) ** (-np.arange(hd, dtype=f32) / f32(hd))
    ang = (time.astype(f32)[:, None] * freqs[None, :]).astype(np.float64)
    rope = np.stack([np.concatenate([np.cos(ang)] * 2, 1), np.concatenate([-np.sin(ang), np.sin(ang)], 1)], 1)
    rope = rope.reshape(TOK, P, 2, HEAD_DIM).transpose(1, 0, 2, 3)
    eye16 = np.zeros((P, CH))
    for q in range(4):
        eye16[32 * q:32 * q + CH] = np.eye(CH)
    sign = np.concatenate([-np.ones(STATE), np.ones(STATE)])[:, None]
    return [np.ascontiguousarray(a, dtype=f32) for a in (decay, rope, eye16, np.eye(P), sign)]


def kernel(**inputs):
    import concourse.bacc as bacc
    from concourse.bass_utils import run_bass_kernel_spmd

    a = {k: np.asarray(x) for k, x in inputs.items()}
    decay, rope, eye16, ident, sign = _constants()
    x = a["x"][0].reshape(NCH, LOC, D_MODEL).transpose(1, 0, 2).reshape(SEQ, D_MODEL)

    def cols(name):
        return a[name].reshape(-1, P).T

    def stack(re, im, axes):
        return np.concatenate([a[re][0].transpose(axes), a[im][0].transpose(axes)], 0)

    b, c = (1, 0, 2), (2, 0, 1)
    dsk = np.zeros((4, 2 * CH, GROUPS // 4), np.float32)
    dsk[:, :CH] = a["ssm_d"][0].reshape(GROUPS // 4, 4, CH).transpose(1, 2, 0)
    arrays = {
        "xT": x.T.reshape(KB, P, SEQ).transpose(1, 0, 2),
        "x_tok": x.reshape(TOK, P, D_MODEL).transpose(1, 0, 2),
        "vec": np.concatenate([cols("norm_mix_g"), cols("norm_ffn_g"), cols("ssm_b_glu"), cols("ssm_out_g"),
                               cols("ret_gn_g"), sign], 1),
        "par": np.stack([np.concatenate([a[n][0].T] * 2, 0) for n in ("ssm_a_re", "ssm_a_im")]
                        + [np.broadcast_to(a["ssm_log_dt"][0], (P, GROUPS))], 1),
        "bc": np.stack([stack("ssm_b_re", "ssm_b_im", b), stack("ssm_b_im", "ssm_b_re", b),
                        stack("ssm_c_re", "ssm_c_im", c), stack("ssm_c_im", "ssm_c_re", c)], 1),
        "dsk": dsk.reshape(P, GROUPS // 4),
        "g_final": np.broadcast_to(a["norm_final_g"], (P, D_MODEL)),
        "decay": decay, "rope": rope, "eye16": eye16, "ident": ident,
    }
    for n in ("w_in", "ssm_w_glu", "w_out", "w_gate", "w_up", "w_down"):
        arrays[n] = a[n][0]
    arrays = {n: np.ascontiguousarray(x) for n, x in arrays.items()}
    nc = bacc.Bacc("TRN2", target_bir_lowering=False, num_devices=1)
    A = {n: nc.dram_tensor("in_" + n, x.shape, mybir.dt.from_np(x.dtype), kind="ExternalInput").ap()
         for n, x in arrays.items()}
    out = nc.dram_tensor("out", (P, TOK, D_MODEL), F32, kind="ExternalOutput").ap()
    build(nc, A, out)
    r = run_bass_kernel_spmd(nc, [{"in_" + n: x for n, x in arrays.items()}], core_ids=[0])
    y = r.results[0]["out"].transpose(1, 0, 2).reshape(LOC, NCH, D_MODEL).transpose(1, 0, 2)
    return np.ascontiguousarray(y).reshape(1, SEQ, D_MODEL)
```

```python
from contextlib import ExitStack

import numpy as np

import concourse.bass as bass
from concourse import mybir

P = 128
D_MODEL = 2048
SEQ = 256
TOK = SEQ // P
CHUNK = 64
HEADS = 8
HEAD_DIM = 128
RET_W = D_MODEL // 2
GROUPS, STATE, CH = 64, 64, 16
D_FF = -(-8 * D_MODEL // (3 * 256)) * 256
IN_W = 5 * RET_W
KB = D_MODEL // P
NCOL = 512
EPS = 1e-6
LOC, NCH = 8, 32
KPAD = 2 * LOC - 1

RAW = 4
SPL = 4
CK = 2 * NCOL
GRP = KB // 2
IN_COLS = [8, 9, 4, 5, 0, 2, 1, 3, 6, 7]
N_IN = len(IN_COLS) * GRP
N_GLU = 8
N_OUT = 16
GLU0 = N_IN
RET0 = GLU0 + N_GLU
SSM0 = RET0 + N_OUT
FFN0 = SSM0 + N_OUT
FG = D_FF // NCOL
LOOP0 = FFN0 + 2 * GRP
TURN = 3 * GRP
TAIL0 = LOOP0 + TURN * (FG - 1)

F32 = mybir.dt.float32
F32R = mybir.dt.float32r
ALU = mybir.AluOpType
ACT = mybir.ActivationFunctionType

V_MIX, V_FFN, V_BGLU, V_OUTG, V_RETG, V_SGN = 0, 16, 32, 40, 48, 56
N_VEC = 57

BG = 8
NB = GROUPS // BG
HALF = GROUPS // 2
HB = NB // 2
U_TR = (12, 21)
CL_AT = (17, 19, 22, 25, 28, 31, 34, 37)
TAB_AT = (16, 19, 25, 28, 31, 34, 37, 40)
V_AT = tuple(t + 5 for t in TAB_AT)
SCAN_AT = 42
QK_AT = tuple(GRP * (gi + 1) + 3 for gi in (4, 5, 6, 7))
QK_TR = (45, 53, 64, 69)
SCORE_AT = (58, 58, 60, 61, 72, 72, 75, 76)
DECAY_AT = (62, 62, 65, 65, 76, 76, 80, 80)
HEAD_AT = (60, 61, 64, 65, 75, 76, 79, 80)
STATS_AT = (66, 70, 81, 84)
NORM_AT = (79, 86)
RET_TR = (83, 86)
Y_AT = (70, 71, 73, 74, 76, 77, 79, 80)
GLU_ORDER = ((0, 0), (1, 0), (0, 1), (1, 1), (2, 0), (2, 1), (3, 0), (3, 1))
GLU_END = (3, 4, 6, 8)
Y_STORE, Y_LOAD, Y1T_AT = (80, 85), (81, 85), (82, 85)



def build(nc, A, out):
    ctx = ExitStack()

    def sb(name, shape, dt=F32):
        return ctx.enter_context(nc.sbuf_tensor(name, shape, dt))

    def overlay(*layers):
        made, size = {}, 0
        for layer in layers:
            with ExitStack() as scope:
                for name, shape, dt in layer:
                    made[name] = scope.enter_context(nc.sbuf_tensor(name, shape, dt))
                size = max(size, sum(4 * int(np.prod(s[1:])) for _, s, _ in layer))
        sb("room_" + layers[0][0][0], [P, size // 4])
        return made

    def sem(name):
        return ctx.enter_context(nc.semaphore(name))

    with ctx:
        raw = sb("raw", [P, RAW, CK])
        w_hi = sb("w_hi", [P, SPL, CK], F32R)
        w_lo = sb("w_lo", [P, SPL, CK], F32R)
        actA_hi = sb("actA_hi", [P, 8, SEQ], F32R)
        actA_lo = sb("actA_lo", [P, 8, SEQ], F32R)
        m = overlay(
            [("actB_hi", [P, 8, SEQ], F32R), ("actB_lo", [P, 8, SEQ], F32R)],
            [("ffT_hi", [P, 4, SEQ], F32R), ("ffT_lo", [P, 4, SEQ], F32R), ("ff_act", [P, TOK, NCOL], F32)],
        )
        actB_hi, actB_lo, ffT_hi, ffT_lo, ff_act = (m[k] for k in ("actB_hi", "actB_lo", "ffT_hi", "ffT_lo", "ff_act"))
        m = overlay([("x2", [P, TOK, D_MODEL], F32)], [("state", [P, 2, 2, NCH, HALF], F32)])
        x2, state = m["x2"], m["state"]
        m = overlay([("qT", [P, HEADS, SEQ], F32)], [("u_tok", [P, TOK, 1024], F32)])
        qT, u_tok = m["qT"], m["u_tok"]
        ret = qT
        m = overlay([("kT", [P, HEADS, SEQ], F32)], [("u_loc", [P, GROUPS, NCH], F32)])
        kT, u_loc = m["kT"], m["u_loc"]
        m = overlay(
            [("v", [P, TOK, RET_W], F32), ("sg", [P, TOK, RET_W], F32)],
            [("below_uT", [P, TOK, RET_W], F32), ("uT", [P, 8, SEQ], F32)],
            [("x_tok", [P, TOK, D_MODEL], F32)],
            [("g_final", [P, D_MODEL], F32)],
        )
        v, sg, uT, x_tok, g_final = (m[k] for k in ("v", "sg", "uT", "x_tok", "g_final"))
        m = overlay(
            [("bc", [P, 4, GROUPS, CH], F32), ("bb", [P, GROUPS + 1, CH], F32), ("bbx", [P, GROUPS, CH], F32),
             ("pr", [P, LOC + 1, GROUPS], F32), ("pi", [P, LOC + 1, GROUPS], F32)],
            [("u_loc2", [P, GROUPS, NCH], F32), ("y1", [P, GROUPS, NCH], F32), ("qs", [P, TOK, NCOL], F32),
             ("qr", [P, TOK, NCOL], F32), ("rot", [P, TOK, NCOL], F32)],
            [("zT", [P, 8, SEQ], F32), ("sqT", [P, 8, SEQ], F32), ("y1T", [P, 8, SEQ], F32)],
        )
        bc, bb, bbx, pr, pi = (m[k] for k in ("bc", "bb", "bbx", "pr", "pi"))
        u_loc2, y1, qs, qr, rot, zT, sqT, y1T = (
            m[k] for k in ("u_loc2", "y1", "qs", "qr", "rot", "zT", "sqT", "y1T"))
        m = overlay(
            [("cl", [P, 2, BG, LOC + 1, CH], F32), ("cl_t", [P, BG, LOC + 1, CH], F32),
             ("wb", [P, BG, LOC, CH], F32)],
            [("xT", [P, KB, SEQ], F32)],
            [("mt", [P, 2, BG, P], F32), ("clr", [P, 2, BG, P], F32), ("y1A_hi", [P, 4, SEQ], F32R),
             ("y1A_lo", [P, 4, SEQ], F32R)],
            [("y1B_hi", [P, 4, SEQ], F32R), ("y1B_lo", [P, 4, SEQ], F32R)],
            [("h2B_hi", [P, 8, SEQ], F32R), ("h2B_lo", [P, 8, SEQ], F32R)],
        )
        y1A_hi, y1A_lo, y1B_hi, y1B_lo, cl, cl_t, wb, xT, mt, clr, h2B_hi, h2B_lo = (
            m[k] for k in ("y1A_hi", "y1A_lo", "y1B_hi", "y1B_lo", "cl", "cl_t", "wb", "xT", "mt", "clr",
                           "h2B_hi", "h2B_lo"))
        y1T_parts = ((y1A_hi, y1A_lo), (y1B_hi, y1B_lo))
        m = overlay(
            [("wb_t", [P, BG, LOC, CH], F32), ("wbT", [P, 2, BG, P], F32)],
            [("dec", [P, 2, TOK, SEQ], F32), ("sT", [P, 2, TOK, SEQ], F32)],
        )
        wb_t, wbT, dec, sT = (m[k] for k in ("wb_t", "wbT", "dec", "sT"))
        kst = sb("kst", [P, 2, 2, KPAD * CH])
        vec = sb("vec", [P, N_VEC])
        ident = sb("ident", [P, P])
        ones = sb("ones", [P, 1])
        par = sb("par", [P, 3, GROUPS])
        dsk = sb("dsk", [P, GROUPS // 4])
        eye16 = sb("eye16", [P, CH])
        dtmp = sb("dtmp", [P, GROUPS // 4, CH])
        rope = sb("rope", [P, TOK, 2, HEAD_DIM])
        scr = sb("scr", [P, 14, GROUPS])
        scan_t = sb("scan_t", [P, 2, 2, 2, HALF])
        mul = sb("mul", [P, 2, 2, GROUPS])
        half = sb("half", [P, 2 * HEADS])
        e_tile = sb("e_tile", [P, GROUPS])
        ss = sb("ss", [P, 5, TOK])
        ss4 = sb("ss4", [P, 2, 4, TOK])
        rstd = sb("rstd", [P, 5, TOK])
        bn = sb("bn", [P, 2 * HEADS, 6])
        mv = sb("mv", [P, 2 * HEADS, 2])
        rv = sb("rv", [P, 2 * HEADS])
        rret = sb("rret", [P, 2 * HEADS])

        ps = ctx.enter_context(nc.psum_tensor("ps", [P, 8, NCOL], F32))
        R_MIX, R_SSM, R_FFN, R_FIN = range(4)

        u_dram = nc.dram_tensor("u_scratch", (RET_W, SEQ), F32, kind="Internal").ap()
        y_dram = nc.dram_tensor("y_scratch", (RET_W, SEQ), F32, kind="Internal").ap()
        k_dram = nc.dram_tensor("k_scratch", (GROUPS, CH, KPAD * CH), F32, kind="Internal").ap()
        c_dram = nc.dram_tensor("c_scratch", (P, GROUPS, P), F32, kind="Internal").ap()

        d_raw = [sem(f"d_raw{i}") for i in range(RAW)]
        d_xT = [sem(f"d_xT{i}") for i in range(KB // 2)]
        d_uTst = [sem(f"d_uTst{i}") for i in range(2)]
        d_u = [sem(f"d_u{i}") for i in range(2)]
        d_swap = [sem(f"d_swap{i}") for i in range(2)]
        d_y1st = [sem(f"d_y1st{i}") for i in range(2)]
        d_y1T = [sem(f"d_y1T{i}") for i in range(2)]
        d_dec = [sem(f"d_dec{i}") for i in range(2)]
        d_mt = [sem(f"d_mt{i}") for i in range(2)]
        d_clst = [sem(f"d_clst{i}") for i in range(2)]
        d_clr = [sem(f"d_clr{i}") for i in range(2)]
        d_kst = [sem(f"d_kst{i}") for i in range(2)]
        d_vec, d_par, d_bc, d_rope, d_xtok, d_u2, d_xres, d_gfin, d_out = (sem(n) for n in (
            "d_vec", "d_par", "d_bc", "d_rope", "d_xtok", "d_u2", "d_xres", "d_gfin", "d_out"))
        names = (
            "high_done low_done pe_done xh_ready xl_ready proj_free dve_step pool_step scanA_done scanB_done "
            "const_ready ss_ready rstd_mix_ready rstd_ssm_ready rstd_ffn_ready rstd_fin_ready dt_ready trig_in_ready "
            "trig_ready mag_ready pow_ready bb_ready uT_mm u_copied cl_ready wb_ready tab_mm wbT_ready "
            "kpsum_free kst_ready signs_ready v_mm v_free mul_ready qr_ready qk_mm qk_free score_mm sT_ready head_mm out_free "
            "bn_ready rret_ready ret_ready retT_mm ret_hi ret_lo y_mm y1_ready y1T_hi_ready y1T_lo_ready sig_ready "
            "zT_ready sqT_ready ssm_hi ssm_lo ssq_mm ssq_ready cols_added h2_mm h2_hi h2_lo x2_sq silu_ready ff_ready "
            "ffT_mm ffT_hi_ready ffT_lo_ready fin_sq fin_ready"
        ).split()
        S = {n: sem(n) for n in names}
        block = ctx.enter_context(nc.Block())

        def in_col(n):
            return IN_COLS[n // GRP]

        def chunk_source(n):
            if n < GLU0:
                c, k = in_col(n), 2 * (n % GRP)
                w = A["w_in"]
            elif n < RET0:
                pair, half_ = GLU_ORDER[n - GLU0]
                return A["ssm_w_glu"][4 * P * half_:4 * P * (half_ + 1), SEQ * pair:SEQ * (pair + 1)
                                      ].rearrange("(b p) n -> p b n", p=P)
            elif n < SSM0:
                c, k = (n - RET0) // 4, 2 * ((n - RET0) % 4)
                w = A["w_out"]
            elif n < FFN0:
                c, k = (n - SSM0) // 4, 8 + 2 * ((n - SSM0) % 4)
                w = A["w_out"]
            else:
                c, k = 0, 2 * ((n - FFN0) % GRP)
                w = A["w_gate"] if n < FFN0 + GRP else A["w_up"]
            return w[k * P:(k + 2) * P, c * NCOL:(c + 1) * NCOL].rearrange("(b p) n -> p b n", p=P)

        def h2(kb, part):
            if kb < 8:
                return (actA_hi, actA_lo)[part][:, kb, :]
            return (h2B_hi, h2B_lo)[part][:, kb - 8, :]

        def act_block(kb, part):
            if kb < 8:
                return (actA_hi, actA_lo)[part][:, kb, :]
            return (actB_hi, actB_lo)[part][:, kb - 8, :]

        def wide(x, k):
            return x[:, k].unsqueeze(2).to_broadcast([P, GROUPS, CH])

        def s5_group(b):
            return slice(BG * b, BG * (b + 1))

        raw2 = raw[:].rearrange("p s (b n) -> p s b n", b=2)
        raw4 = raw[:].rearrange("p s (b n) -> p s b n", b=4)
        kst_w = kst[:].rearrange("p u h (d c) -> p u h d c", c=CH)

        def state_groups(b, x):
            g = BG * (b % HB)
            return state[:, b // HB, x, :, g:g + BG]

        def scan_step(tt, link, done, h, k):
            prev, cur, t = state[:, h, :, k], state[:, h, :, k + 1], scan_t[:, h]
            of_half = mul[:, :, :, HALF * h:HALF * (h + 1)]
            link(tt(t, prev.unsqueeze(1).to_broadcast([P, 2, 2, HALF]), of_half, ALU.mult))
            link(tt(cur, cur, t[:, 0], ALU.add))
            tt(cur[:, 0], cur[:, 0], t[:, 1, 1], ALU.add)
            last = tt(cur[:, 1], cur[:, 1], t[:, 1, 0], ALU.add)
            if k == NCH - 3:
                last.then_inc(done, 1)
            else:
                link(last)

        @block.sync
        def _(sp):
            def load(n, src, turn=None):
                slot = (n if turn is None else n[1]) % RAW
                if turn is None:
                    if n >= RAW:
                        sp.wait_ge(S["low_done"], n - RAW + 1)
                else:
                    sp.wait_ge(S["low_done"], turn * TURN + (n[1] - RAW + 1))
                glu = turn is None and GLU0 <= n < RET0
                sp.dma_start((raw4 if glu else raw2)[:, slot], src).then_inc(d_raw[slot], 16)

            def u_rows(h, dst, signal):
                for i in range(LOC):
                    sp.dma_start(dst[i * CH:(i + 1) * CH, HALF * h:HALF * (h + 1)],
                                 u_dram.rearrange("(g c) (i k) -> i c g k", c=CH, k=NCH)[
                                     LOC - 1 - i, :, HALF * h:HALF * (h + 1)]).then_inc(signal, 16)

            def load_decay(h):
                if h < 2:
                    sp.wait_ge(S["v_mm"], NB)
                else:
                    sp.wait_ge(S["sT_ready"], h - 1)
                sp.dma_start(dec[:, h % 2], A["decay"][h]).then_inc(d_dec[h % 2], 16)

            def load_y_tables(b):
                if b >= 2:
                    sp.wait_ge(S["y_mm"], b - 1)
                for i in range(LOC):
                    sp.dma_start(mt[i * CH:(i + 1) * CH, b % 2],
                                 k_dram[s5_group(b), :, i * CH:i * CH + P].rearrange("g c w -> c g w")
                                 ).then_inc(d_mt[b % 2], 16)
                sp.dma_start(clr[:, b % 2], c_dram[:, s5_group(b)]).then_inc(d_clr[b % 2], 16)

            def before(n):
                if n < KB // 2:
                    sp.dma_start(xT[:, 2 * n:2 * n + 2], A["xT"][:, 2 * n:2 * n + 2]).then_inc(d_xT[n], 16)
                if n == 4:
                    sp.dma_start(x_tok[:], A["x_tok"]).then_inc(d_xtok, 16)
                if n == 6:
                    sp.dma_start(bc[:], A["bc"]).then_inc(d_bc, 16)
                if n == 8:
                    sp.dma_start(ident[:], A["ident"]).then_inc(d_rope, 16)
                    sp.dma_start(dsk[:], A["dsk"]).then_inc(d_rope, 16)
                    sp.dma_start(eye16[:], A["eye16"]).then_inc(d_rope, 16)
                    sp.dma_start(rope[:], A["rope"]).then_inc(d_rope, 16)
                for h in range(2):
                    rows = slice(HALF * CH * h, HALF * CH * (h + 1))
                    if n == U_TR[h] + 9:
                        sp.wait_ge(S["u_copied"], h + 1)
                        sp.dma_start(u_dram[rows].rearrange("(b r) p -> r b p", r=P), uT[:, 4 * h:4 * h + 4]
                                     ).then_inc(d_uTst[h], 16)
                    if n == U_TR[h] + 10:
                        sp.wait_ge(d_uTst[h], 16)
                        u_rows(h, u_loc, d_u[h])
                    if n == V_AT[HB * (h + 1) - 1] + 9:
                        sp.wait_ge(S["v_free"], HB * (h + 1))
                        for x in range(2):
                            sp.dma_start(state[STATE * x:STATE * (x + 1), h, 1],
                                         state[STATE * (1 - x):STATE * (2 - x), h, 0]).then_inc(d_swap[h], 16)
                    if n == Y_STORE[h]:
                        sp.wait_ge(S["y1_ready"], 2 * h + 2)
                        for j in range(LOC):
                            sp.dma_start(y_dram.rearrange("(g c) (j k) -> j c g k", c=CH, k=NCH)[
                                             j, :, HALF * h:HALF * (h + 1)],
                                         y1[j * CH:(j + 1) * CH, HALF * h:HALF * (h + 1)]).then_inc(d_y1st[h], 16)
                    if n == Y_LOAD[h]:
                        sp.wait_ge(d_y1st[h], 16 * LOC)
                        if h == 0:
                            sp.wait_ge(S["qk_mm"], 4)
                        sp.dma_start(y1T[:, 4 * h:4 * h + 4], y_dram[rows].rearrange("(b r) p -> r b p", r=P)
                                     ).then_inc(d_y1T[h], 16)
                for b in range(NB):
                    if n == CL_AT[b] + 4:
                        sp.wait_ge(S["cl_ready"], b + 1)
                        sp.dma_start(c_dram[:, s5_group(b)],
                                     cl[:, b % 2, :, 1:].rearrange("p g d c -> p g (d c)")
                                     ).then_inc(d_clst[b % 2], 16)
                    if n == TAB_AT[b] + 9:
                        sp.wait_ge(S["kst_ready"], b + 1)
                        for q in range(4):
                            sp.dma_start(k_dram.rearrange("(b h q) c w -> b q c h w", h=2, q=4)[b, q],
                                         kst[32 * q:32 * q + CH, b % 2]).then_inc(d_kst[b % 2], 16)
                if n == TAB_AT[-1] + 11:
                    sp.wait_ge(S["tab_mm"], NB)
                    u_rows(0, u_loc2, d_u2)
                if n == TAB_AT[-1] + 12:
                    u_rows(1, u_loc2, d_u2)
                if n == TAB_AT[-1] + 14:
                    for x in range(2):
                        sp.wait_ge(d_kst[x], 16 * 4 * HB)
                        sp.wait_ge(d_clst[x], 16 * HB)
                for b in range(NB):
                    if n == (54, 56)[b] if b < 2 else n == Y_AT[b - 2] + 5:
                        load_y_tables(b)
                for h in range(HEADS):
                    if n == (55, 55, 65, 66, 70, 71, 79, 80)[h]:
                        load_decay(h)
                if n == GLU0 + 9:
                    sp.wait_ge(S["y_mm"], NB)
                    sp.dma_start(x2[:], A["x_tok"]).then_inc(d_xres, 16)

            for n in range(LOOP0):
                before(n)
                load(n, chunk_source(n))
            sp.wait_ge(S["ret_ready"], 2)
            sp.dma_start(g_final[:], A["g_final"]).then_inc(d_gfin, 16)
            with sp.Fori(0, FG - 1) as j:
                for c in range(TURN):
                    if c < 2 * GRP:
                        w = A["w_gate"] if c < GRP else A["w_up"]
                        k = 2 * (c % GRP)
                        src = w[k * P:(k + 2) * P, bass.ds((j + 1) * NCOL, NCOL)]
                    else:
                        col, k = divmod(c - 2 * GRP, 2)
                        src = A["w_down"][bass.ds(j * (4 * P) + 2 * k * P, 2 * P), col * NCOL:(col + 1) * NCOL]
                    load((None, LOOP0 + c), src.rearrange("(b p) n -> p b n", p=P), turn=j)
            for c in range(GRP):
                col, k = divmod(c, 2)
                row = (FG - 1) * 4 * P + 2 * k * P
                load(TAIL0 + c, A["w_down"][row:row + 2 * P, col * NCOL:(col + 1) * NCOL]
                     .rearrange("(b p) n -> p b n", p=P))
            for t in range(TOK):
                for h in range(2):
                    sp.wait_ge(S["fin_ready"], 2 * t + h + 1)
                    sp.dma_start(out[:, t, 1024 * h:1024 * (h + 1)], x2[:, t, 1024 * h:1024 * (h + 1)]
                                 ).then_inc(d_out, 16)
            sp.wait_ge(d_out, 64)

        @block.scalar
        def _(act):
            def high(n, turn=None, at=None):
                if turn is None:
                    act.wait_ge(d_raw[n % RAW], 16 * (n // RAW + 1))
                    if n >= SPL:
                        act.wait_ge(S["pe_done"], n - SPL + 1)
                    s = n
                else:
                    s = at
                    act.wait_ge(d_raw[s % RAW], turn * (16 * TURN // RAW) + 16 * (s // RAW + 1))
                    act.wait_ge(S["pe_done"], turn * TURN + (s - SPL + 1))
                nc.scalar.activation(w_hi[:, s % SPL], raw[:, s % RAW], ACT.Copy).then_inc(S["high_done"], 1)

            def xh(r):
                act.wait_ge(d_xT[r], 16)
                if r == 0:
                    act.wait_ge(d_vec, 16)
                for kb in (2 * r, 2 * r + 1):
                    nc.scalar.activation(act_block(kb, 0), xT[:, kb], ACT.Copy, scale=vec[:, V_MIX + kb:V_MIX + kb + 1]
                                         ).then_inc(S["xh_ready"], 1)

            act.dma_start(vec[:], A["vec"]).then_inc(d_vec, 16)
            act.dma_start(par[:], A["par"]).then_inc(d_par, 16)

            def ret_out(p):
                act.wait_ge(S["head_mm"], 2 * p + 2)
                nc.scalar.activation(ret[:, 2 * p:2 * p + 2].rearrange("p h s -> p (h s)"), ps[:, 7],
                                     ACT.Copy).then_inc(S["out_free"], 1)

            def qk_evac(i):
                act.wait_ge(S["qk_mm"], i + 1)
                dst = (qT, kT)[i % 2][:, 4 * (i // 2):4 * (i // 2) + 4]
                nc.scalar.activation(dst.rearrange("p (a b) s -> p a (b s)", a=2), ps[:, 4:6], ACT.Copy
                                     ).then_inc(S["qk_free"], 1)

            def side(n):
                gi, r = divmod(n - 4 - (GRP - 1), GRP)
                if n in (7, 8):
                    t = n - 7
                    if t == 0:
                        act.wait_ge(d_xtok, 16)
                    else:
                        act.wait_ge(S["ss_ready"], 1)
                    nc.scalar.activation(ps[:, 4:8], x_tok[:, t].rearrange("p (a b) -> p a b", a=4), ACT.Square,
                                         accum_out=ss[:, R_MIX, t:t + 1]).then_inc(S["ss_ready"], 1)
                if n == 9:
                    act.wait_ge(S["trig_in_ready"], 1)
                    nc.scalar.activation(scr[:, 6], scr[:, 4], ACT.Sin).then_inc(S["trig_ready"], 1)
                    nc.scalar.activation(scr[:, 7], scr[:, 4], ACT.Sin, scale=0.5).then_inc(S["trig_ready"], 1)
                if r == 0 and 0 <= gi < len(IN_COLS):
                    c = IN_COLS[gi]
                    if gi == 0:
                        act.wait_ge(S["rstd_mix_ready"], 1)
                    act.wait_ge(S["pe_done"], GRP * (gi + 1))
                    for t in range(TOK):
                        src = ps[:, 2 * (gi % 2) + t]
                        scale = rstd[:, R_MIX, t:t + 1]
                        half_ = (c % 2) * NCOL
                        if c >= 8:
                            dst, func = u_tok[:, t, half_:half_ + NCOL], ACT.Copy
                        elif c >= 6:
                            dst, func = sg[:, t, half_:half_ + NCOL], ACT.Silu
                        elif c >= 4:
                            dst, func = v[:, t, half_:half_ + NCOL], ACT.Copy
                        else:
                            dst, func = qs[:, t], ACT.Copy
                            if gi == 4 and t == 0:
                                act.wait_ge(S["cl_ready"], NB)
                                act.wait_ge(S["wb_ready"], NB)
                                act.wait_ge(S["tab_mm"], NB)
                            if t == 0 and gi > 4:
                                act.wait_ge(S["qr_ready"], gi - 4)
                        if gi == 8 and t == 0:
                            for h in range(2):
                                act.wait_ge(d_uTst[h], 16)
                        nc.scalar.activation(dst, src, func, scale=scale).then_inc(S["proj_free"], 1)
                for h in range(2):
                    if n == U_TR[h] + 4:
                        act.wait_ge(S["uT_mm"], h + 1)
                        nc.scalar.activation(uT[:, 4 * h:4 * h + 4].rearrange("p (a b) s -> p a (b s)", a=2),
                                             ps[:, 4:6], ACT.Copy).then_inc(S["u_copied"], 1)
                for b in range(NB):
                    if n == TAB_AT[b] + 4:
                        act.wait_ge(S["tab_mm"], b + 1)
                        if b >= 2:
                            act.wait_ge(S["v_mm"], b - 1)
                        nc.scalar.activation(wbT[:, b % 2].rearrange("p (a g) s -> p a (g s)", a=2), ps[:, 4:6],
                                             ACT.Copy).then_inc(S["wbT_ready"], 1)
                        if b == 0:
                            act.wait_ge(S["const_ready"], 1)
                        if b >= 2:
                            act.wait_ge(d_kst[b % 2], 64 * (b // 2))
                        nc.scalar.activation(kst_w[:, b % 2, :, LOC - 1:], ps[:, 6, 0:2 * P]
                                             .rearrange("p (h d c) -> p h d c", h=2, c=CH), ACT.Copy
                                             ).then_inc(S["kpsum_free"], 1)
                    if n == V_AT[b] + 4:
                        act.wait_ge(S["v_mm"], b + 1)
                        nc.scalar.activation(state_groups(b, 0).rearrange("p k g -> p g k"),
                                             ps[:, 7, 0:NCH * BG].rearrange("p (g k) -> p g k", g=BG), ACT.Copy
                                             ).then_inc(S["v_free"], 1)
                for i in range(4):
                    if n == QK_TR[i] + 4:
                        qk_evac(i)
                    if n == HEAD_AT[2 * i + 1] + 4:
                        ret_out(i)
                    if n == Y_AT[2 * i + 1] + 4:
                        act.wait_ge(S["y_mm"], 2 * i + 2)
                        nc.scalar.activation(y1[:, 16 * i:16 * i + 16].rearrange("p g k -> p (g k)"), ps[:, 6],
                                             ACT.Gelu_apprx_tanh).then_inc(S["y1_ready"], 1)
                for h in range(2):
                    if n == Y1T_AT[h]:
                        act.wait_ge(d_y1T[h], 16)
                        if h == 1:
                            act.wait_ge(S["y_mm"], NB)
                        nc.scalar.activation(y1T_parts[h][0][:], y1T[:, 4 * h:4 * h + 4], ACT.Copy
                                             ).then_inc(S["y1T_hi_ready"], 1)
                    if n == RET_TR[h] + 4:
                        ret_high(h)
                for p in range(4):
                    if n == GLU0 + GLU_END[p] + 3:
                        glu_pair(p)
                    if p % 2 and n == GLU0 + GLU_END[p] + 4:
                        glu_half(p // 2)
                c, r = divmod(n - (SSM0 + 9), 4)
                if r == 0 and 0 <= c < 4:
                    h2_high(c)
                    x2_square(c)

            def glu_pair(p):
                act.wait_ge(S["pe_done"], GLU0 + GLU_END[p])
                for j in range(2):
                    c8 = 2 * p + j
                    nc.scalar.activation(zT[:, c8], ps[:, 2 * (p % 2) + j, 0:SEQ], ACT.Sigmoid,
                                         bias=vec[:, V_BGLU + c8:V_BGLU + c8 + 1]).then_inc(S["sig_ready"], 1)

            def glu_half(q):
                act.wait_ge(S["zT_ready"], q + 1)
                nc.scalar.activation(sqT[:, 4 * q:4 * q + 4], zT[:, 4 * q:4 * q + 4], ACT.Square
                                     ).then_inc(S["sqT_ready"], 1)
                for c in range(4):
                    c8 = 4 * q + c
                    nc.scalar.activation(actB_hi[:, c8], zT[:, c8], ACT.Copy,
                                         scale=vec[:, V_OUTG + c8:V_OUTG + c8 + 1]).then_inc(S["ssm_hi"], 1)

            def ret_high(q):
                for p in (2 * q, 2 * q + 1):
                    act.wait_ge(S["retT_mm"], p + 1)
                    for h in range(2):
                        nc.scalar.activation(actA_hi[:, 2 * p + h], ps[:, 4 + p, SEQ * h:SEQ * (h + 1)], ACT.Copy,
                                             scale=vec[:, V_RETG + 2 * p + h:V_RETG + 2 * p + h + 1]
                                             ).then_inc(S["ret_hi"], 1)

            def h2_high(c):
                act.wait_ge(S["h2_mm"], c + 1)
                for k in range(4):
                    kb = 4 * c + k
                    src = ps[:, 4 + 2 * (c % 2) + k // 2, SEQ * (k % 2):SEQ * (k % 2 + 1)]
                    nc.scalar.activation(h2(kb, 0), src, ACT.Copy, scale=vec[:, V_FFN + kb:V_FFN + kb + 1]
                                         ).then_inc(S["h2_hi"], 1)

            def x2_square(c):
                act.wait_ge(S["cols_added"], 5 + c)
                for t in range(TOK):
                    if c or t:
                        act.wait_ge(S["x2_sq"], 2 * c + t)
                    nc.scalar.activation(sqT[:, 0:2].rearrange("p a s -> p (a s)"),
                                         x2[:, t, NCOL * c:NCOL * (c + 1)], ACT.Square,
                                         accum_out=ss4[:, 0, c, t:t + 1]).then_inc(S["x2_sq"], 1)

            for n in range(FFN0 + GRP + 4):
                if n < KB // 2:
                    xh(n)
                high(n)
                side(n)

            def silu(chunks):
                act.wait_ge(S["pe_done"], chunks)
                for t in range(TOK):
                    nc.scalar.activation(ff_act[:, t], ps[:, t], ACT.Silu, scale=rstd[:, R_FFN, t:t + 1]
                                         ).then_inc(S["silu_ready"], 1)

            def ffT_high(count):
                act.wait_ge(S["ffT_mm"], count)
                nc.scalar.activation(ffT_hi[:].rearrange("p (a b) s -> p a (b s)", a=2), ps[:, 4:6], ACT.Copy
                                     ).then_inc(S["ffT_hi_ready"], 1)

            act.wait_ge(S["rstd_ffn_ready"], 1)
            silu(FFN0 + GRP)
            for n in range(FFN0 + GRP + 4, LOOP0 + SPL):
                high(n)
            with act.Fori(0, FG - 1) as j:
                for c in range(SPL, TURN + SPL):
                    high(None, turn=j, at=LOOP0 + c)
                    if c == GRP + SPL - 1:
                        ffT_high(j + 1)
                        silu(j * TURN + (LOOP0 + GRP))
            ffT_high(FG)
            for c in range(SPL, GRP):
                high(TAIL0 + c)
            for c in range(4):
                act.wait_ge(S["cols_added"], 8 + 4 * (FG - 1) + c + 1)
                for t in range(TOK):
                    if c or t:
                        act.wait_ge(S["fin_sq"], 2 * c + t)
                    nc.scalar.activation(sqT[:, 0:2].rearrange("p a s -> p (a s)"),
                                         x2[:, t, NCOL * c:NCOL * (c + 1)], ACT.Square,
                                         accum_out=ss4[:, 1, c, t:t + 1]).then_inc(S["fin_sq"], 1)

        @block.vector
        def _(dve):
            steps = [0]

            def link(ins):
                steps[0] += 1
                ins.then_inc(S["dve_step"], 1)
                dve.wait_ge(S["dve_step"], steps[0])

            tt, ts, stt = nc.vector.tensor_tensor, nc.vector.tensor_scalar, nc.vector.scalar_tensor_tensor

            def low(n, turn=None, at=None):
                if turn is None:
                    dve.wait_ge(S["high_done"], n + 1)
                    s = n
                else:
                    s = at
                    dve.wait_ge(S["high_done"], turn * TURN + (s + 1))
                tt(w_lo[:, s % SPL], raw[:, s % RAW], w_hi[:, s % SPL].bitcast(F32), ALU.subtract
                   ).then_inc(S["low_done"], 1)

            def xl(r):
                dve.wait_ge(S["xh_ready"], 2 * r + 2)
                for kb in (2 * r, 2 * r + 1):
                    last = gain_low(act_block(kb, 1), xT[:, kb], V_MIX + kb, act_block(kb, 0))
                last.then_inc(S["xl_ready"], 1)

            def gain_low(dst, src, at, hi):
                return stt(dst, src, vec[:, at:at + 1], hi.bitcast(F32), ALU.mult, ALU.subtract)

            a_re, a_im = par[:, 0], par[:, 1]
            C1, C2, C3 = 6.28125, 0.0019350051879882812, 3.019916050561733e-07
            MAGIC = 12582912.0

            def angles():
                dve.wait_ge(d_par, 16)
                dve.wait_ge(S["dt_ready"], 1)
                link(tt(scr[:, 2], a_im, scr[:, 0], ALU.mult))
                link(ts(scr[:, 3], scr[:, 2], 1 / (2 * np.pi), MAGIC, ALU.mult, ALU.add))
                link(ts(scr[:, 3], scr[:, 3], -MAGIC, None, ALU.add))
                link(stt(scr[:, 8], scr[:, 3], -C1, scr[:, 2], ALU.mult, ALU.add))
                link(stt(scr[:, 9], scr[:, 3], -C2, scr[:, 8], ALU.mult, ALU.add))
                link(stt(scr[:, 10], scr[:, 3], -C3, scr[:, 9], ALU.mult, ALU.add))
                ts(scr[:, 4], scr[:, 10], -3.1415925, 3.1415925, ALU.max, ALU.min).then_inc(S["trig_in_ready"], 1)

            def complex_mul(o_r, o_i, x_r, x_i, y_r, y_i, t_r, t_i):
                tt(t_r, x_i, y_i, ALU.mult)
                tt(t_i, x_i, y_r, ALU.mult)
                tt(o_r, x_r, y_r, ALU.mult)
                link(tt(o_i, x_r, y_i, ALU.mult))
                tt(o_r, o_r, t_r, ALU.subtract)
                link(tt(o_i, o_i, t_i, ALU.add))

            def s5_params():
                dve.wait_ge(S["trig_ready"], 2)
                dve.wait_ge(S["pow_ready"], 1)
                mag, sin, sinh = scr[:, 5], scr[:, 6], scr[:, 7]
                link(tt(scr[:, 8], sinh, sinh, ALU.mult))
                link(ts(scr[:, 8], scr[:, 8], -2.0, 1.0, ALU.mult, ALU.add))
                nc.vector.memset(pr[:, 0], 1.0)
                nc.vector.memset(pi[:, 0], 0.0)
                tt(pr[:, 1], mag, scr[:, 8], ALU.mult)
                link(tt(pi[:, 1], mag, sin, ALU.mult))
                link(ts(scr[:, 8], pr[:, 1], -1.0, None, ALU.add))
                tt(scr[:, 9], a_re, a_re, ALU.mult)
                link(tt(scr[:, 10], a_im, a_im, ALU.mult))
                link(tt(scr[:, 9], scr[:, 9], scr[:, 10], ALU.add))
                link(nc.vector.reciprocal(scr[:, 9], scr[:, 9]))
                tt(scr[:, 10], scr[:, 8], a_re, ALU.mult)
                tt(scr[:, 11], pi[:, 1], a_im, ALU.mult)
                tt(scr[:, 12], pi[:, 1], a_re, ALU.mult)
                link(tt(scr[:, 13], scr[:, 8], a_im, ALU.mult))
                tt(scr[:, 10], scr[:, 10], scr[:, 11], ALU.add)
                link(tt(scr[:, 12], scr[:, 12], scr[:, 13], ALU.subtract))
                tt(scr[:, 10], scr[:, 10], scr[:, 9], ALU.mult)
                link(tt(scr[:, 12], scr[:, 12], scr[:, 9], ALU.mult))
                sgn = vec[:, V_SGN:V_SGN + 1]
                ts(scr[:, 11], scr[:, 10], sgn, None, ALU.mult)
                ts(scr[:, 13], scr[:, 12], sgn, None, ALU.mult).then_inc(S["signs_ready"], 1)
                dve.wait_ge(S["signs_ready"], 1)

            def s5_powers():
                def two(x, a, b):
                    return x[:, a:b]

                def times(x, k, n):
                    return x[:, k].unsqueeze(1).to_broadcast([P, n, GROUPS])

                tr = cl_t[:].rearrange("p g d c -> p (g d c)")[:, 0:4 * GROUPS].rearrange("p (a g) -> p a g", a=4)
                ti = cl_t[:].rearrange("p g d c -> p (g d c)")[:, 4 * GROUPS:8 * GROUPS].rearrange(
                    "p (a g) -> p a g", a=4)
                for done in (1, 2, 4):
                    complex_mul(pr[:, done + 1:2 * done + 1], pi[:, done + 1:2 * done + 1],
                                pr[:, 1:done + 1], pi[:, 1:done + 1], times(pr, done, done), times(pi, done, done),
                                tr[:, 0:done], ti[:, 0:done])
                sgn = vec[:, V_SGN:V_SGN + 1]
                nc.vector.tensor_copy(mul[:, 0, 0], pr[:, LOC])
                nc.vector.tensor_copy(mul[:, 0, 1], pr[:, LOC])
                ts(mul[:, 1, 0], pi[:, LOC], sgn, -1.0, ALU.mult, ALU.mult)
                ts(mul[:, 1, 1], pi[:, LOC], sgn, None, ALU.mult).then_inc(S["mul_ready"], 1)

            def c_signs():
                dve.wait_ge(d_bc, 16)
                ts(bc[:, 2], bc[:, 2], vec[:, V_SGN:V_SGN + 1], -1.0, ALU.mult, ALU.mult)
                link(ts(bc[:, 3], bc[:, 3], -1.0, None, ALU.mult))

            def s5_inputs():
                nc.vector.memset(bb[:, GROUPS], 0.0)
                t_a = cl[:].rearrange("p a g d c -> p (a g d c)")[:, 0:GROUPS * CH].rearrange(
                    "p (g c) -> p g c", c=CH)
                tt(bb[:, 0:GROUPS], bc[:, 0], wide(scr, 10), ALU.mult)
                link(tt(t_a, bc[:, 1], wide(scr, 13), ALU.mult))
                tt(bb[:, 0:GROUPS], bb[:, 0:GROUPS], t_a, ALU.add).then_inc(S["bb_ready"], 1)

            def d_skip():
                dve.wait_ge(d_rope, 64)
                link(tt(dtmp[:], dsk[:].unsqueeze(2).to_broadcast([P, GROUPS // 4, CH]),
                        eye16[:].unsqueeze(1).to_broadcast([P, GROUPS // 4, CH]), ALU.mult))

            def cl_table(b):
                o = cl[:, b % 2]
                if b >= 2:
                    dve.wait_ge(d_clst[b % 2], 16 * (b // 2))
                    dve.wait_ge(S["tab_mm"], b - 1)

                if b:
                    dve.wait_ge(S["cl_ready"], b)

                def c_(k):
                    return bc[:, k, s5_group(b)].unsqueeze(2).to_broadcast([P, BG, LOC + 1, CH])

                def p_(x):
                    return x[:, :, s5_group(b)].rearrange("p d g -> p g d").unsqueeze(3).to_broadcast(
                        [P, BG, LOC + 1, CH])

                tt(o, c_(2), p_(pr), ALU.mult)
                link(tt(cl_t[:], c_(3), p_(pi), ALU.mult))
                tt(o, o, cl_t[:], ALU.add).then_inc(S["cl_ready"], 1)

            def rotate(i):
                dve.wait_ge(S["proj_free"], 2 * (4 + i) + 2)
                if i:
                    dve.wait_ge(S["qk_mm"], i)
                four = [P, 4, HEAD_DIM]
                x = [qs[:, t].rearrange("p (h d) -> p h d", h=4) for t in range(TOK)]
                y = [qr[:, t].rearrange("p (h d) -> p h d", h=4) for t in range(TOK)]
                for t in range(TOK):
                    last = tt(y[t], x[t], rope[:, t, 0].unsqueeze(1).to_broadcast(four), ALU.mult)
                for t in range(TOK):
                    for a in range(2):
                        lo_, hi_ = slice(64 * a, 64 * a + 64), slice(64 * (1 - a), 64 * (1 - a) + 64)
                        last = tt(rot[:, t].rearrange("p (h d) -> p h d", h=4)[:, :, lo_], x[t][:, :, hi_],
                                  rope[:, t, 1, lo_].unsqueeze(1).to_broadcast([P, 4, 64]), ALU.mult)
                link(last)
                tt(qr[:], qr[:], rot[:], ALU.add).then_inc(S["qr_ready"], 1)

            def decayed(h):
                dve.wait_ge(S["score_mm"], h + 1)
                dve.wait_ge(d_dec[h % 2], 16 * (h // 2 + 1))
                if h >= 2:
                    dve.wait_ge(S["head_mm"], h - 1)
                tt(sT[:, h % 2].rearrange("p a s -> p (a s)"), ps[:, 4 + h % 2],
                   dec[:, h % 2].rearrange("p a s -> p (a s)"), ALU.mult).then_inc(S["sT_ready"], 1)

            def head_stats(p):
                dve.wait_ge(S["out_free"], p + 1)
                last = None
                for k in range(4 * p, 4 * p + 4):
                    last = nc.vector.bn_stats(bn[:, k], ret[:, k // 2, P * (k % 2):P * (k % 2 + 1)])
                link(last)
                for k in range(4 * p, 4 * p + 4):
                    last = nc.vector.bn_aggr(mv[:, k], bn[:, k])
                if p % 2:
                    last.then_inc(S["bn_ready"], 1)

            def normalise(q):
                dve.wait_ge(S["rret_ready"], q + 1)
                for h in range(4 * q, 4 * q + 4):
                    for t in range(TOK):
                        g = sg[:, t, P * h:P * (h + 1)]
                        last = ts(g, g, rret[:, 2 * h + t:2 * h + t + 1], None, ALU.mult)
                link(last)
                for h in range(4 * q, 4 * q + 4):
                    for t in range(TOK):
                        o = ret[:, h, P * t:P * (t + 1)]
                        last = stt(o, o, mv[:, 2 * h + t, 0:1], sg[:, t, P * h:P * (h + 1)], ALU.subtract, ALU.mult)
                last.then_inc(S["ret_ready"], 1)

            def y1_low(q):
                dve.wait_ge(S["y1T_hi_ready"], q + 1)
                hi, lo = y1T_parts[q]
                tt(lo[:], y1T[:, 4 * q:4 * q + 4], hi[:].bitcast(F32), ALU.subtract).then_inc(S["y1T_lo_ready"], 1)

            def glu_half(q):
                dve.wait_ge(S["sig_ready"], 4 * q + 4)
                at = slice(4 * q, 4 * q + 4)
                tt(zT[:, at], zT[:, at], y1T[:, at], ALU.mult).then_inc(S["zT_ready"], 1)
                dve.wait_ge(S["ssm_hi"], 4 * q + 4)
                dve.wait_ge(S["zT_ready"], q + 1)
                for c in range(4 * q, 4 * q + 4):
                    gain_low(actB_lo[:, c], zT[:, c], V_OUTG + c, actB_hi[:, c]).then_inc(S["ssm_lo"], 1)

            def ret_low(q):
                for p in (2 * q, 2 * q + 1):
                    dve.wait_ge(S["ret_hi"], 2 * p + 2)
                    for h in range(2):
                        gain_low(actA_lo[:, 2 * p + h], ps[:, 4 + p, SEQ * h:SEQ * (h + 1)], V_RETG + 2 * p + h,
                                 actA_hi[:, 2 * p + h]).then_inc(S["ret_lo"], 1)

            def h2_low(c):
                for k in range(4):
                    kb = 4 * c + k
                    if k % 2 == 0:
                        dve.wait_ge(S["h2_hi"], kb + 2)
                    src = ps[:, 4 + 2 * (c % 2) + k // 2, SEQ * (k % 2):SEQ * (k % 2 + 1)]
                    gain_low(h2(kb, 1), src, V_FFN + kb, h2(kb, 0)).then_inc(S["h2_lo"], 1)

            def out_col_ret(c):
                if c == 0:
                    dve.wait_ge(d_xres, 16)
                dve.wait_ge(S["pe_done"], RET0 + 4 * (c + 1))
                cols = x2[:, :, NCOL * c:NCOL * (c + 1)]
                b0 = 2 * (c % 2)
                tt(cols, ps[:, b0:b0 + 2], cols, ALU.add).then_inc(S["cols_added"], 1)

            def out_col_ssm(c):
                if c == 0:
                    dve.wait_ge(S["rstd_ssm_ready"], 1)
                dve.wait_ge(S["pe_done"], SSM0 + 4 * (c + 1))
                dve.wait_ge(S["cols_added"], c + 1)
                for t in range(TOK):
                    cols = x2[:, t, NCOL * c:NCOL * (c + 1)]
                    last = stt(cols, ps[:, 2 * (c % 2) + t], rstd[:, R_SSM, t:t + 1], cols, ALU.mult, ALU.add)
                last.then_inc(S["cols_added"], 1)

            def ff(count, chunks):
                dve.wait_ge(S["pe_done"], chunks)
                dve.wait_ge(S["silu_ready"], count * 2)
                for t in range(TOK):
                    last = stt(ff_act[:, t], ps[:, 2 + t], rstd[:, R_FFN, t:t + 1], ff_act[:, t], ALU.mult, ALU.mult)
                last.then_inc(S["ff_ready"], 1)

            def ffT_low(count):
                dve.wait_ge(S["ffT_hi_ready"], count)
                tt(ffT_lo[:].rearrange("p (a b) s -> p a (b s)", a=2), ps[:, 4:6],
                   ffT_hi[:].rearrange("p (a b) s -> p a (b s)", a=2).bitcast(F32), ALU.subtract
                   ).then_inc(S["ffT_lo_ready"], 1)

            def down_col(chunks, before, c):
                dve.wait_ge(S["pe_done"], chunks)
                dve.wait_ge(S["cols_added"], before)
                b0 = 6 - 2 * (c % 2)
                cols = x2[:, :, NCOL * c:NCOL * (c + 1)]
                tt(cols, ps[:, b0:b0 + 2], cols, ALU.add).then_inc(S["cols_added"], 1)

            def side(n):
                if n == 6:
                    angles()
                if n == 10:
                    c_signs()
                if n == 12:
                    s5_params()
                if n == 13:
                    s5_powers()
                if n == 14:
                    s5_inputs()
                if n == 15:
                    d_skip()
                for b in range(NB):
                    if n == CL_AT[b]:
                        cl_table(b)
                    if n == TAB_AT[b] + 4:
                        dve.wait_ge(S["kpsum_free"], b + 1)
                        diag = kst_w[:, b % 2, :, LOC - 1]
                        tt(diag, diag, dtmp[:, 2 * b:2 * b + 2], ALU.add).then_inc(S["kst_ready"], 1)
                if 0 <= n - SCAN_AT < NCH - 2:
                    if n == SCAN_AT:
                        dve.wait_ge(d_swap[0], 32)
                    scan_step(tt, link, S["scanA_done"], 0, n - SCAN_AT)
                for i in range(4):
                    if n == QK_AT[i]:
                        rotate(i)
                for h in range(HEADS):
                    if n == DECAY_AT[h]:
                        decayed(h)
                for p in range(4):
                    if n == STATS_AT[p]:
                        head_stats(p)
                for q in range(2):
                    if n == NORM_AT[q]:
                        normalise(q)
                    if n == Y1T_AT[q]:
                        y1_low(q)
                    if n == GLU0 + GLU_END[2 * q + 1] + 3:
                        glu_half(q)
                    if n == RET_TR[q] + 4:
                        ret_low(q)
                if n == RET0 + 8:
                    dve.wait_ge(S["ssq_mm"], 1)
                    ts(ss[:, R_SSM], ps[:, 4, 0:TOK], 1 / RET_W, EPS, ALU.mult, ALU.add).then_inc(S["ssq_ready"], 1)
                c, r = divmod(n - (RET0 + 7), 4)
                if r == 0 and 0 <= c < 4:
                    out_col_ret(c)
                if r == 0 and 4 <= c < 8:
                    out_col_ssm(c - 4)
                c, r = divmod(n - (SSM0 + 9), 4)
                if r == 0 and 0 <= c < 4:
                    h2_low(c)
                if n == LOOP0 + 3:
                    ff(1, LOOP0)

            for n in range(LOOP0 + SPL):
                if n < KB // 2:
                    xl(n)
                low(n)
                side(n)
            with dve.Fori(0, FG - 1) as j:
                for c in range(SPL, TURN + SPL):
                    low(None, turn=j, at=LOOP0 + c)
                    if c == GRP + 3:
                        ffT_low(j + 1)
                    if c == 2 * GRP + 3:
                        ff(j + 2, j * TURN + (LOOP0 + 2 * GRP))
                    if c >= 2 * GRP + 5 and c % 2:
                        col = (c - 2 * GRP - 5) // 2
                        down_col(j * TURN + (LOOP0 + 2 * GRP + 2 * col + 2), j * 4 + (col + 5), col)
            ffT_low(FG)
            for c in range(SPL, GRP):
                low(TAIL0 + c)
            for col in range(4):
                down_col(TAIL0 + 2 * col + 2, 4 * (FG - 1) + col + 5, col)
            dve.wait_ge(d_gfin, 16)
            dve.wait_ge(S["cols_added"], 8 + 4 * FG)
            dve.wait_ge(S["rstd_fin_ready"], 1)
            for t in range(TOK):
                for h in range(2):
                    at = slice(1024 * h, 1024 * (h + 1))
                    stt(x2[:, t, at], x2[:, t, at], rstd[:, R_FIN, t:t + 1], g_final[:, at], ALU.mult, ALU.mult
                        ).then_inc(S["fin_ready"], 1)

        @block.gpsimd
        def _(pool):
            steps = [0]

            def link(ins):
                steps[0] += 1
                ins.then_inc(S["pool_step"], 1)
                pool.wait_ge(S["pool_step"], steps[0])

            tt, ts = nc.gpsimd.tensor_tensor, nc.gpsimd.tensor_scalar

            def rsqrt(dst, src, ready, width=TOK):
                tt(dst, src, half[:, 0:width], ALU.pow).then_inc(ready, 1)

            nc.gpsimd.memset(half[:], -0.5)
            nc.gpsimd.memset(ones[:], 1.0)
            nc.gpsimd.memset(kst_w[:, 0, :, 0:LOC - 1], 0.0)
            nc.gpsimd.memset(kst_w[:, 1, :, 0:LOC - 1], 0.0).then_inc(S["const_ready"], 1)
            link(nc.gpsimd.memset(e_tile[:], float(np.e)))
            pool.wait_ge(d_par, 16)
            tt(scr[:, 0], e_tile[:], par[:, 2], ALU.pow).then_inc(S["dt_ready"], 1)
            pool.wait_ge(S["dt_ready"], 1)
            link(tt(scr[:, 1], par[:, 0], scr[:, 0], ALU.mult))
            tt(scr[:, 5], e_tile[:], scr[:, 1], ALU.pow).then_inc(S["pow_ready"], 1)
            pool.wait_ge(S["ss_ready"], 2)
            link(ts(ss[:, R_MIX], ss[:, R_MIX], 1 / D_MODEL, EPS, ALU.mult, ALU.add))
            rsqrt(rstd[:, R_MIX], ss[:, R_MIX], S["rstd_mix_ready"])
            pool.wait_ge(d_bc, 16)
            pool.wait_ge(S["signs_ready"], 1)
            t_b = wb_t[:].rearrange("p g d c -> p (g d) c")
            tt(bbx[:], bc[:, 1], wide(scr, 11), ALU.mult)
            link(tt(t_b, bc[:, 0], wide(scr, 12), ALU.mult))
            link(tt(bbx[:], bbx[:], t_b, ALU.subtract))
            pool.wait_ge(S["mul_ready"], 1)
            for b in range(NB):
                if b == 0:
                    pool.wait_ge(S["bb_ready"], 1)
                else:
                    pool.wait_ge(S["tab_mm"], b)
                    pool.wait_ge(S["wb_ready"], b)

                def b_(x):
                    return x[:, s5_group(b)].unsqueeze(2).to_broadcast([P, BG, LOC, CH])

                def p_(x):
                    return x[:, 0:LOC, s5_group(b)].rearrange("p d g -> p g d").unsqueeze(3).to_broadcast(
                        [P, BG, LOC, CH])

                tt(wb[:], b_(bb), p_(pr), ALU.mult)
                link(tt(wb_t[:], b_(bbx), p_(pi), ALU.mult))
                tt(wb[:], wb[:], wb_t[:], ALU.add).then_inc(S["wb_ready"], 1)
            pool.wait_ge(d_swap[1], 32)
            for k in range(NCH - 2):
                scan_step(tt, link, S["scanB_done"], 1, k)
            for q in range(2):
                pool.wait_ge(S["bn_ready"], q + 1)
                at = slice(8 * q, 8 * q + 8)
                link(ts(rv[:, at], mv[:, at, 1], 1.0, EPS, ALU.mult, ALU.add))
                rsqrt(rret[:, at], rv[:, at], S["rret_ready"], 8)
            pool.wait_ge(S["ssq_ready"], 1)
            rsqrt(rstd[:, R_SSM], ss[:, R_SSM], S["rstd_ssm_ready"])
            for i, (src, row, ready) in enumerate((("x2_sq", R_FFN, "rstd_ffn_ready"),
                                                   ("fin_sq", R_FIN, "rstd_fin_ready"))):
                pool.wait_ge(S[src], 8)
                tt(ss4[:, i, 0], ss4[:, i, 0], ss4[:, i, 1], ALU.add)
                link(tt(ss4[:, i, 2], ss4[:, i, 2], ss4[:, i, 3], ALU.add))
                link(tt(ss4[:, i, 0], ss4[:, i, 0], ss4[:, i, 2], ALU.add))
                link(ts(ss[:, row], ss4[:, i, 0], 1 / D_MODEL, EPS, ALU.mult, ALU.add))
                rsqrt(rstd[:, row], ss[:, row], S[ready])

        @block.tensor
        def _(pe):
            mm, tr = nc.tensor.matmul, nc.tensor.transpose

            def three(o, x_hi, x_lo, h, l, first, last):
                mm(o, x_hi, h, start=first, stop=False)
                mm(o, x_hi, l, start=False, stop=False)
                return mm(o, x_lo, h, start=False, stop=last)

            def column_chunk(s, blocks, banks, first, last):
                for k in range(2):
                    at = slice(NCOL * k, NCOL * (k + 1))
                    hi, lo = blocks[k]
                    for t in range(TOK):
                        tok = slice(P * t, P * (t + 1))
                        ins = three(ps[:, banks + t], hi[:, tok], lo[:, tok], w_hi[:, s, at], w_lo[:, s, at],
                                    first and k == 0, last and k == 1)
                ins.then_inc(S["pe_done"], 1)

            def ready(n, turn=None):
                pe.wait_ge(S["low_done"], n + 1 if turn is None else turn * TURN + (n + 1))

            def act_pair(kb):
                return [(act_block(kb + k, 0), act_block(kb + k, 1)) for k in range(2)]

            def h2_pair(kb):
                return [(h2(kb + k, 0), h2(kb + k, 1)) for k in range(2)]

            def ff_pair(kb):
                return [(ffT_hi[:, kb + k], ffT_lo[:, kb + k]) for k in range(2)]

            def u_transposes(h):
                pe.wait_ge(S["proj_free"], 2 * h + 2)
                if h == 0:
                    pe.wait_ge(S["ss_ready"], 2)
                    pe.wait_ge(d_rope, 64)
                else:
                    pe.wait_ge(S["wbT_ready"], 2)
                for blk in range(4 * h, 4 * h + 4):
                    for t in range(TOK):
                        at = (blk % 2) * SEQ + t * P
                        ins = tr(ps[:, 4 + blk // 2 % 2, at:at + P], u_tok[:, t, P * blk:P * (blk + 1)], ident[:])
                ins.then_inc(S["uT_mm"], 1)

            def tables(b):
                pe.wait_ge(S["cl_ready"], b + 1)
                pe.wait_ge(S["wb_ready"], b + 1)
                pe.wait_ge(S["u_copied"], 1 if b < 2 else 2)
                if b == 0:
                    pe.wait_ge(S["bb_ready"], 1)
                else:
                    pe.wait_ge(S["kpsum_free"], b)
                for g in range(BG):
                    h, q = divmod(g, 4)
                    gg = BG * b + g
                    mm(ps[32 * q:32 * q + 32, 6, P * h:P * (h + 1)], bb[:, gg:gg + 2].rearrange("p a c -> p (a c)"),
                       cl[:, b % 2, g, 0:LOC].rearrange("p d c -> p (d c)"), start=True, stop=True)
                for g in range(BG):
                    ins = tr(ps[:, 4 + g // 4, P * (g % 4):P * (g % 4 + 1)],
                             wb[:, g].rearrange("p d c -> p (d c)"), ident[:])
                ins.then_inc(S["tab_mm"], 1)

            def chunk_inputs(b):
                pe.wait_ge(S["wbT_ready"], b + 1)
                if b % HB == 0:
                    pe.wait_ge(d_u[b // HB], 16 * LOC)
                if b:
                    pe.wait_ge(S["v_free"], b)
                for g in range(BG):
                    ins = mm(ps[:, 7, NCH * g:NCH * (g + 1)], wbT[:, b % 2, g], u_loc[:, BG * b + g],
                             start=True, stop=True)
                ins.then_inc(S["v_mm"], 1)

            def qk_transposes(i):
                pe.wait_ge(S["qr_ready"], i + 1)
                if i == 0:
                    pe.wait_ge(S["wbT_ready"], NB)
                else:
                    pe.wait_ge(S["qk_free"], i)
                if i == 2:
                    pe.wait_ge(S["sT_ready"], 4)
                for h in range(4):
                    for t in range(TOK):
                        at = (h % 2) * SEQ + t * P
                        ins = tr(ps[:, 4 + h // 2, at:at + P], qr[:, t, P * h:P * (h + 1)], ident[:])
                ins.then_inc(S["qk_mm"], 1)

            def score(h):
                if h % 4 == 0:
                    pe.wait_ge(S["qk_free"], 2 + h // 2)
                if h >= 2:
                    pe.wait_ge(S["sT_ready"], h - 1)
                for a in range(TOK):
                    ins = mm(ps[:, 4 + h % 2, SEQ * a:SEQ * (a + 1)], kT[:, h, P * a:P * (a + 1)], qT[:, h],
                             start=True, stop=True)
                ins.then_inc(S["score_mm"], 1)

            def head(h):
                pe.wait_ge(S["sT_ready"], h + 1)
                if h == 0:
                    pe.wait_ge(S["proj_free"], 8)
                    pe.wait_ge(S["v_free"], NB)
                elif h % 2 == 0:
                    pe.wait_ge(S["out_free"], h // 2)
                for t in range(TOK):
                    at = (h % 2) * SEQ + t * P
                    for a in range(TOK):
                        ins = mm(ps[:, 7, at:at + P], sT[:, h % 2, a, P * t:P * (t + 1)],
                                 v[:, a, P * h:P * (h + 1)], start=(a == 0), stop=(a == TOK - 1))
                ins.then_inc(S["head_mm"], 1)

            def y_batch(b):
                if b == 0:
                    pe.wait_ge(S["scanA_done"], 1)
                    pe.wait_ge(d_u2, 2 * 16 * LOC)
                    pe.wait_ge(S["kpsum_free"], NB)
                elif b % 2 == 0:
                    pe.wait_ge(S["y1_ready"], b // 2)
                if b == HB:
                    pe.wait_ge(S["scanB_done"], 1)
                pe.wait_ge(d_mt[b % 2], 16 * LOC * (b // 2 + 1))
                pe.wait_ge(d_clr[b % 2], 16 * (b // 2 + 1))
                for g in range(BG):
                    at = NCH * (BG * (b % 2) + g)
                    mm(ps[:, 6, at:at + NCH], mt[:, b % 2, g], u_loc2[:, BG * b + g], start=True, stop=False)
                    ins = mm(ps[:, 6, at + 1:at + NCH], clr[:, b % 2, g],
                             state_groups(b, 0)[:, 0:NCH - 1, g], start=False, stop=True)
                ins.then_inc(S["y_mm"], 1)

            def ret_transposes(q):
                pe.wait_ge(S["ret_ready"], q + 1)
                if q:
                    pe.wait_ge(S["y1_ready"], 4)
                    pe.wait_ge(S["out_free"], 4)
                else:
                    pe.wait_ge(S["sT_ready"], 8)
                for p in (2 * q, 2 * q + 1):
                    for h in range(2):
                        for t in range(TOK):
                            at = SEQ * h + P * t
                            ins = tr(ps[:, 4 + p, at:at + P], ret[:, 2 * p + h, P * t:P * (t + 1)], ident[:])
                    ins.then_inc(S["retT_mm"], 1)

            def channel_squares():
                pe.wait_ge(S["const_ready"], 1)
                pe.wait_ge(S["sqT_ready"], 2)
                pe.wait_ge(S["ret_lo"], 4)
                for t in range(TOK):
                    for k in range(8):
                        ins = mm(ps[:, 4, t:t + 1], sqT[:, k, P * t:P * (t + 1)], ones[:],
                                 start=(k == 0), stop=(k == 7))
                ins.then_inc(S["ssq_mm"], 1)

            def h2_transposes(c):
                pe.wait_ge(S["cols_added"], 5 + c)
                if c >= 2:
                    pe.wait_ge(S["h2_lo"], 4 * (c - 1))
                elif c == 0:
                    pe.wait_ge(S["ssq_ready"], 1)
                for k in range(4):
                    for t in range(TOK):
                        at = (k % 2) * SEQ + t * P
                        col = P * (4 * c + k)
                        ins = tr(ps[:, 4 + 2 * (c % 2) + k // 2, at:at + P], x2[:, t, col:col + P], ident[:])
                ins.then_inc(S["h2_mm"], 1)

            def ff_transposes(count):
                pe.wait_ge(S["ff_ready"], count)
                for k in range(4):
                    for t in range(TOK):
                        at = (k % 2) * SEQ + t * P
                        ins = tr(ps[:, 4 + k // 2, at:at + P], ff_act[:, t, P * k:P * (k + 1)], ident[:])
                ins.then_inc(S["ffT_mm"], 1)

            def side(n):
                for h in range(2):
                    if n == U_TR[h]:
                        u_transposes(h)
                for b in range(NB):
                    if n == TAB_AT[b]:
                        tables(b)
                    if n == V_AT[b]:
                        chunk_inputs(b)
                for i in range(4):
                    if n == QK_TR[i]:
                        qk_transposes(i)
                for h in range(HEADS):
                    if n == HEAD_AT[h]:
                        head(h)
                    if n == SCORE_AT[h]:
                        score(h)
                for b in range(NB):
                    if n == Y_AT[b]:
                        y_batch(b)
                for q in range(2):
                    if n == RET_TR[q]:
                        ret_transposes(q)
                if n == RET0 + 5:
                    channel_squares()
                c, r = divmod(n - (SSM0 + 5), 4)
                if r == 0 and 0 <= c < 4:
                    h2_transposes(c)

            for n in range(N_IN):
                gi, i = divmod(n, GRP)
                if n < GRP:
                    pe.wait_ge(S["xl_ready"], n + 1)
                if i == 0 and gi >= 2:
                    pe.wait_ge(S["proj_free"], 2 * gi - 2)
                ready(n)
                column_chunk(n % SPL, act_pair(2 * i), 2 * (gi % 2), i == 0, i == GRP - 1)
                side(n)
            for n in range(GLU0, RET0):
                pair, half_ = GLU_ORDER[n - GLU0]
                if half_ == 0:
                    if pair < 2:
                        pe.wait_ge(S["proj_free"], 18 + 2 * pair)
                    else:
                        pe.wait_ge(S["sig_ready"], 2 * (pair - 1))
                pe.wait_ge(S["y1T_lo_ready"], 1 + half_)
                ready(n)
                for k in range(4):
                    hi, lo = (x[:, k] for x in y1T_parts[half_])
                    for j in range(2):
                        at = slice(SEQ * k + P * j, SEQ * k + P * (j + 1))
                        o = ps[:, 2 * (pair % 2) + j, 0:SEQ]
                        first, last = half_ == 0 and k == 0, half_ == 1 and k == 3
                        mm(o, w_hi[:, n % SPL, at], hi, start=first, stop=False)
                        mm(o, w_hi[:, n % SPL, at], lo, start=False, stop=False)
                        ins = mm(o, w_lo[:, n % SPL, at], hi, start=False, stop=last)
                ins.then_inc(S["pe_done"], 1)
                side(n)
            for n in range(RET0, FFN0):
                idx, i = divmod(n - RET0, 4)
                c, part = idx % 4, idx // 4
                if i == 0 and idx >= 2:
                    pe.wait_ge(S["cols_added"], idx - 1)
                if part == 0 and i == 0 and c < 2:
                    pe.wait_ge(S["sig_ready"], 6 + 2 * c)
                if part == 0 and c == 0:
                    pe.wait_ge(S["ret_lo"], 2 * i + 2)
                if part == 1 and c == 0 and i == 0:
                    pe.wait_ge(S["ssm_lo"], 8)
                ready(n)
                column_chunk(n % SPL, act_pair(8 * part + 2 * i), 2 * (c % 2), i == 0, i == 3)
                side(n)
            for n in range(FFN0, LOOP0):
                up, i = divmod(n - FFN0, GRP)
                if n == FFN0:
                    pe.wait_ge(S["cols_added"], 7)
                if n == FFN0 + GRP:
                    pe.wait_ge(S["cols_added"], 8)
                if not up and i % 2 == 0:
                    pe.wait_ge(S["h2_lo"], 2 * i + 4)
                ready(n)
                column_chunk(n % SPL, h2_pair(2 * i), 2 * up, i == 0, i == GRP - 1)
                side(n)
            with pe.Fori(0, FG - 1) as j:
                for c in range(TURN):
                    part, i = divmod(c, GRP)
                    if c == 0:
                        pe.wait_ge(S["silu_ready"], (j + 1) * 2)
                    if c == GRP:
                        pe.wait_ge(S["ff_ready"], j + 1)
                    if c == 2 * GRP:
                        pe.wait_ge(S["ffT_lo_ready"], j + 1)
                    ready(LOOP0 + c, turn=j)
                    if part < 2:
                        column_chunk(c % SPL, h2_pair(2 * i), 2 * part, i == 0, i == GRP - 1)
                    else:
                        col, k = divmod(i, 2)
                        if k == 0 and col >= 2:
                            pe.wait_ge(S["cols_added"], j * 4 + (7 + col))
                        column_chunk(c % SPL, ff_pair(2 * k), 6 - 2 * (col % 2), k == 0, k == 1)
                    if c == GRP - 1:
                        pe.wait_ge(S["cols_added"], j * 4 + 8)
                        ff_transposes(j + 1)
            pe.wait_ge(S["cols_added"], 8 + 4 * (FG - 1))
            ff_transposes(FG)
            pe.wait_ge(S["ffT_lo_ready"], FG)
            for i in range(GRP):
                col, k = divmod(i, 2)
                if k == 0 and col >= 2:
                    pe.wait_ge(S["cols_added"], 8 + 4 * (FG - 1) + col - 1)
                ready(TAIL0 + i)
                column_chunk(i % SPL, ff_pair(2 * k), 6 - 2 * (col % 2), k == 0, k == 1)


def _time_order():
    return (LOC * np.arange(NCH)[None, :] + np.arange(LOC)[:, None]).reshape(-1)


def _constants():
    time = _time_order()
    f32 = np.float32
    h = np.arange(HEADS, dtype=np.float64)
    log_g = np.log1p(-(2.0 ** (-5.0 - h)))
    n, m = time[None, :], time[:, None]
    seen = (n // CHUNK >= m // CHUNK)
    dist = np.abs(n - m)
    decay = np.where(seen, np.exp(log_g[:, None, None] * dist), 0.0) * HEAD_DIM ** -0.5
    decay = decay.reshape(HEADS, TOK, P, SEQ).transpose(0, 2, 1, 3)
    hd = HEAD_DIM // 2
    freqs = f32(10000.0) ** (-np.arange(hd, dtype=f32) / f32(hd))
    ang = (time.astype(f32)[:, None] * freqs[None, :]).astype(np.float64)
    rope = np.stack([np.concatenate([np.cos(ang)] * 2, 1), np.concatenate([-np.sin(ang), np.sin(ang)], 1)], 1)
    rope = rope.reshape(TOK, P, 2, HEAD_DIM).transpose(1, 0, 2, 3)
    eye16 = np.zeros((P, CH))
    for q in range(4):
        eye16[32 * q:32 * q + CH] = np.eye(CH)
    sign = np.concatenate([-np.ones(STATE), np.ones(STATE)])[:, None]
    return [np.ascontiguousarray(a, dtype=f32) for a in (decay, rope, eye16, np.eye(P), sign)]


def kernel(**inputs):
    import concourse.bacc as bacc
    from concourse.bass_utils import run_bass_kernel_spmd

    a = {k: np.asarray(x) for k, x in inputs.items()}
    decay, rope, eye16, ident, sign = _constants()
    x = a["x"][0].reshape(NCH, LOC, D_MODEL).transpose(1, 0, 2).reshape(SEQ, D_MODEL)

    def cols(name):
        return a[name].reshape(-1, P).T

    def stack(re, im, axes):
        return np.concatenate([a[re][0].transpose(axes), a[im][0].transpose(axes)], 0)

    b, c = (1, 0, 2), (2, 0, 1)
    dsk = np.zeros((4, 2 * CH, GROUPS // 4), np.float32)
    dsk[:, :CH] = a["ssm_d"][0].reshape(GROUPS // 4, 4, CH).transpose(1, 2, 0)
    arrays = {
        "xT": x.T.reshape(KB, P, SEQ).transpose(1, 0, 2),
        "x_tok": x.reshape(TOK, P, D_MODEL).transpose(1, 0, 2),
        "vec": np.concatenate([cols("norm_mix_g"), cols("norm_ffn_g"), cols("ssm_b_glu"), cols("ssm_out_g"),
                               cols("ret_gn_g"), sign], 1),
        "par": np.stack([np.concatenate([a[n][0].T] * 2, 0) for n in ("ssm_a_re", "ssm_a_im")]
                        + [np.broadcast_to(a["ssm_log_dt"][0], (P, GROUPS))], 1),
        "bc": np.stack([stack("ssm_b_re", "ssm_b_im", b), stack("ssm_b_im", "ssm_b_re", b),
                        stack("ssm_c_re", "ssm_c_im", c), stack("ssm_c_im", "ssm_c_re", c)], 1),
        "dsk": dsk.reshape(P, GROUPS // 4),
        "g_final": np.broadcast_to(a["norm_final_g"], (P, D_MODEL)),
        "decay": decay, "rope": rope, "eye16": eye16, "ident": ident,
    }
    for n in ("w_in", "ssm_w_glu", "w_out", "w_gate", "w_up", "w_down"):
        arrays[n] = a[n][0]
    arrays = {n: np.ascontiguousarray(x) for n, x in arrays.items()}
    nc = bacc.Bacc("TRN2", target_bir_lowering=False, num_devices=1)
    A = {n: nc.dram_tensor("in_" + n, x.shape, mybir.dt.from_np(x.dtype), kind="ExternalInput").ap()
         for n, x in arrays.items()}
    out = nc.dram_tensor("out", (P, TOK, D_MODEL), F32, kind="ExternalOutput").ap()
    build(nc, A, out)
    r = run_bass_kernel_spmd(nc, [{"in_" + n: x for n, x in arrays.items()}], core_ids=[0])
    y = r.results[0]["out"].transpose(1, 0, 2).reshape(LOC, NCH, D_MODEL).transpose(1, 0, 2)
    return np.ascontiguousarray(y).reshape(1, SEQ, D_MODEL)
```

```python
from contextlib import ExitStack

import numpy as np

import concourse.bass as bass
from concourse import mybir

P = 128
D_MODEL = 2048
SEQ = 256
TOK = SEQ // P
CHUNK = 64
HEADS = 8
HEAD_DIM = 128
RET_W = D_MODEL // 2
GROUPS, STATE, CH = 64, 64, 16
D_FF = -(-8 * D_MODEL // (3 * 256)) * 256
IN_W = 5 * RET_W
KB = D_MODEL // P
NCOL = 512
EPS = 1e-6
LOC, NCH = 8, 32
KPAD = 2 * LOC - 1

RAW = 4
SPL = 4
CK = 2 * NCOL
GRP = KB // 2
IN_COLS = [8, 9, 4, 5, 0, 2, 1, 3, 6, 7]
N_IN = len(IN_COLS) * GRP
N_GLU = 8
N_OUT = 16
GLU0 = N_IN
RET0 = GLU0 + N_GLU
SSM0 = RET0 + N_OUT
FFN0 = SSM0 + N_OUT
FG = D_FF // NCOL
LOOP0 = FFN0 + 2 * GRP
TURN = 3 * GRP
TAIL0 = LOOP0 + TURN * (FG - 1)

F32 = mybir.dt.float32
F32R = mybir.dt.float32r
ALU = mybir.AluOpType
ACT = mybir.ActivationFunctionType

V_MIX, V_FFN, V_BGLU, V_OUTG, V_RETG, V_SGN = 0, 16, 32, 40, 48, 56
N_VEC = 58

BG = 8
NB = GROUPS // BG
HALF = GROUPS // 2
HB = NB // 2
YBUF = 3
PARAM_AT = 9
U_TR = (12, 21)
CL_AT = (17, 19, 22, 25, 28, 31, 34, 37)
TAB_AT = (16, 19, 25, 28, 31, 34, 37, 40)
V_AT = tuple(t + 5 for t in TAB_AT)
SCAN_AT = tuple(41 + 4 * k // 5 for k in range(NCH - 2))
QK_AT = tuple(GRP * (gi + 1) + 3 for gi in (4, 5, 6, 7))
QK_TR = (45, 53, 65, 69)
SCORE_AT = (58, 58, 61, 62, 72, 72, 75, 76)
DECAY_AT = (62, 62, 65, 66, 76, 76, 79, 80)
DECAY_LOAD = (55, 55, 65, 66, 70, 71, 80, 81)
HEAD_AT = (61, 62, 65, 66, 75, 76, 78, 79)
STATS_AT = (67, 71, 81, 83)
NORM_AT = (79, 85)
RET_TR = (83, 85)
Y_AT = (64, 65, 67, 68, 70, 71, 73, 74)
Y_STORE, Y_LOAD, Y1T_AT = (75, 81), (77, 82), (80, 84)
GLU_ORDER = ((0, 0), (1, 0), (0, 1), (1, 1), (2, 0), (2, 1), (3, 0), (3, 1))
GLU_END = (3, 4, 6, 8)
SIDE_FIRST = (GLU0 + 3, GLU0 + 4)
SIDE_FIRST_LOW = (CL_AT[0], CL_AT[1], GLU0 + 4)
WARM = 4


def build(nc, A, out):
    ctx = ExitStack()

    def sb(name, shape, dt=F32):
        return ctx.enter_context(nc.sbuf_tensor(name, shape, dt))

    def overlay(*layers):
        made, size = {}, 0
        for layer in layers:
            with ExitStack() as scope:
                for name, shape, dt in layer:
                    made[name] = scope.enter_context(nc.sbuf_tensor(name, shape, dt))
                size = max(size, sum(4 * int(np.prod(s[1:])) for _, s, _ in layer))
        sb("room_" + layers[0][0][0], [P, size // 4])
        return made

    def sem(name):
        return ctx.enter_context(nc.semaphore(name))

    with ctx:
        raw = sb("raw", [P, RAW, CK])
        w_hi = sb("w_hi", [P, SPL, CK], F32R)
        w_lo = sb("w_lo", [P, SPL, CK], F32R)
        actA_hi = sb("actA_hi", [P, 8, SEQ], F32R)
        actA_lo = sb("actA_lo", [P, 8, SEQ], F32R)
        m = overlay(
            [("actB_hi", [P, 8, SEQ], F32R), ("actB_lo", [P, 8, SEQ], F32R)],
            [("ffT_hi", [P, 4, SEQ], F32R), ("ffT_lo", [P, 4, SEQ], F32R), ("ff_act", [P, TOK, NCOL], F32)],
        )
        actB_hi, actB_lo, ffT_hi, ffT_lo, ff_act = (m[k] for k in ("actB_hi", "actB_lo", "ffT_hi", "ffT_lo", "ff_act"))
        m = overlay([("x2", [P, TOK, D_MODEL], F32)], [("state", [P, 2, 2, NCH, HALF], F32)],
                    [("warm", [P, NCOL], F32)])
        x2, state, warm = m["x2"], m["state"], m["warm"]
        m = overlay([("qT", [P, HEADS, SEQ], F32)], [("u_tok", [P, TOK, 1024], F32)])
        qT, u_tok = m["qT"], m["u_tok"]
        ret = qT
        m = overlay([("kT", [P, HEADS, SEQ], F32)], [("u_loc", [P, GROUPS, NCH], F32)],
                    [("ffE_hi", [P, 4, SEQ], F32R), ("ffE_lo", [P, 4, SEQ], F32R)])
        kT, u_loc, ffE_hi, ffE_lo = (m[k] for k in ("kT", "u_loc", "ffE_hi", "ffE_lo"))
        m = overlay(
            [("v", [P, TOK, RET_W], F32), ("sg", [P, TOK, RET_W], F32)],
            [("below_uT", [P, TOK, RET_W], F32), ("uT", [P, 8, SEQ], F32)],
            [("x_tok", [P, TOK, D_MODEL], F32)],
            [("g_final", [P, D_MODEL], F32)],
        )
        v, sg, uT, x_tok, g_final = (m[k] for k in ("v", "sg", "uT", "x_tok", "g_final"))
        m = overlay(
            [("bc", [P, 4, GROUPS, CH], F32), ("bb", [P, GROUPS + 1, CH], F32), ("bbx", [P, GROUPS, CH], F32),
             ("pr", [P, LOC + 1, GROUPS], F32), ("pi", [P, LOC + 1, GROUPS], F32)],
            [("u_loc2", [P, GROUPS, NCH], F32), ("y1", [P, GROUPS, NCH], F32), ("qs", [P, TOK, NCOL], F32),
             ("qr", [P, TOK, NCOL], F32), ("rot", [P, TOK, NCOL], F32)],
            [("zT", [P, 8, SEQ], F32), ("sqT", [P, 8, SEQ], F32), ("y1T", [P, 8, SEQ], F32)],
            [("x_gain", [P, TOK, D_MODEL], F32)],
        )
        bc, bb, bbx, pr, pi = (m[k] for k in ("bc", "bb", "bbx", "pr", "pi"))
        u_loc2, y1, qs, qr, rot, zT, sqT, y1T, x_gain = (
            m[k] for k in ("u_loc2", "y1", "qs", "qr", "rot", "zT", "sqT", "y1T", "x_gain"))
        m = overlay(
            [("cl", [P, 2, BG, LOC + 1, CH], F32), ("cl_t", [P, BG, LOC + 1, CH], F32),
             ("wb", [P, BG, LOC, CH], F32)],
            [("xT", [P, KB, SEQ], F32)],
            [("y_tab", [P, YBUF, 2, BG, P], F32)],
            [("y1B_hi", [P, 4, SEQ], F32R), ("y1B_lo", [P, 4, SEQ], F32R), ("between", [P, 8, SEQ], F32),
             ("y1A_hi", [P, 4, SEQ], F32R), ("y1A_lo", [P, 4, SEQ], F32R)],
            [("h2B_hi", [P, 8, SEQ], F32R), ("h2B_lo", [P, 8, SEQ], F32R)],
        )
        y1A_hi, y1A_lo, y1B_hi, y1B_lo, cl, cl_t, wb, xT, y_tab, h2B_hi, h2B_lo = (
            m[k] for k in ("y1A_hi", "y1A_lo", "y1B_hi", "y1B_lo", "cl", "cl_t", "wb", "xT", "y_tab",
                           "h2B_hi", "h2B_lo"))
        y1T_parts = ((y1A_hi, y1A_lo), (y1B_hi, y1B_lo))
        m = overlay(
            [("wb_t", [P, BG, LOC, CH], F32), ("wbT", [P, 2, BG, P], F32)],
            [("dec", [P, 2, TOK, SEQ], F32), ("sT", [P, 2, TOK, SEQ], F32)],
        )
        wb_t, wbT, dec, sT = (m[k] for k in ("wb_t", "wbT", "dec", "sT"))
        kst = sb("kst", [P, 2, 2, KPAD * CH])
        vec = sb("vec", [P, N_VEC])
        ident = sb("ident", [P, P])
        ones = sb("ones", [P, 1])
        par = sb("par", [P, 3, GROUPS])
        dsk = sb("dsk", [P, GROUPS // 4])
        eye16 = sb("eye16", [P, CH])
        dtmp = sb("dtmp", [P, GROUPS // 4, CH])
        rope = sb("rope", [P, TOK, 2, HEAD_DIM])
        scr = sb("scr", [P, 14, GROUPS])
        scan_t = sb("scan_t", [P, 2, 2, 2, HALF])
        mul = sb("mul", [P, 2, 2, GROUPS])
        half = sb("half", [P, 2 * HEADS])
        e_tile = sb("e_tile", [P, GROUPS])
        ss = sb("ss", [P, 5, TOK])
        ss4 = sb("ss4", [P, 2, 4, TOK])
        rstd = sb("rstd", [P, 5, TOK])
        bn = sb("bn", [P, 2 * HEADS, 6])
        mv = sb("mv", [P, 2 * HEADS, 2])
        rv = sb("rv", [P, 2 * HEADS])
        rret = sb("rret", [P, 2 * HEADS])

        ps = ctx.enter_context(nc.psum_tensor("ps", [P, 8, NCOL], F32))
        R_MIX, R_SSM, R_FFN, R_FIN = range(4)

        u_dram = nc.dram_tensor("u_scratch", (RET_W, SEQ), F32, kind="Internal").ap()
        y_dram = nc.dram_tensor("y_scratch", (RET_W, SEQ), F32, kind="Internal").ap()
        k_dram = nc.dram_tensor("k_scratch", (GROUPS, CH, KPAD * CH), F32, kind="Internal").ap()
        c_dram = nc.dram_tensor("c_scratch", (P, GROUPS, P), F32, kind="Internal").ap()

        d_raw = [sem(f"d_raw{i}") for i in range(RAW)]
        d_xT = [sem(f"d_xT{i}") for i in range(KB // 2)]
        d_uTst = [sem(f"d_uTst{i}") for i in range(2)]
        d_u = [sem(f"d_u{i}") for i in range(2)]
        d_xtok = [sem(f"d_xtok{i}") for i in range(TOK)]
        d_bc = [sem(f"d_bc{i}") for i in range(2)]
        d_swap = [sem(f"d_swap{i}") for i in range(2)]
        d_y1st = [sem(f"d_y1st{i}") for i in range(2)]
        d_y1T = [sem(f"d_y1T{i}") for i in range(2)]
        d_dec = [sem(f"d_dec{i}") for i in range(2)]
        d_mt = [sem(f"d_mt{i}") for i in range(YBUF)]
        d_mt_pool = [sem(f"d_mt_pool{i}") for i in range(YBUF)]
        d_clst = [sem(f"d_clst{i}") for i in range(2)]
        d_clr = [sem(f"d_clr{i}") for i in range(YBUF)]
        d_kst = [sem(f"d_kst{i}") for i in range(2)]
        d_vec, d_par, d_rope, d_dsk, d_ident, d_u2, d_xres, d_gfin, d_out = (sem(n) for n in (
            "d_vec", "d_par", "d_rope", "d_dsk", "d_ident", "d_u2", "d_xres", "d_gfin", "d_out"))
        names = (
            "high_done low_done pe_done xh_ready xl_ready proj_free dve_step pool_step scanA_done scanB_done "
            "const_ready warm_ready table_ready c_ready ss_ready rstd_mix_ready rstd_ssm_ready rstd_ffn_ready rstd_fin_ready dt_ready trig_in_ready "
            "trig_ready pow_ready bb_ready uT_mm u_copied cl_ready wb_ready tab_mm wbT_ready "
            "kpsum_free kst_ready signs_ready v_mm v_free mul_ready qr_ready qk_mm qk_free score_mm sT_ready head_mm out_free "
            "bn_ready rret_ready ret_ready retT_mm ret_hi ret_lo y_mm y1_ready y1T_hi_ready y1T_lo_ready sig_ready "
            "zT_ready sqT_ready ssm_hi ssm_lo ssq_mm ssq_ready cols_added last_added h2_mm h2_hi h2_lo x2_sq silu_ready ff_ready "
            "ffT_mm ffT_hi_ready ffT_lo_ready fin_sq gain_done fin_ready fin1_ready"
        ).split()
        S = {n: sem(n) for n in names}
        block = ctx.enter_context(nc.Block())

        def in_col(n):
            return IN_COLS[n // GRP]

        def chunk_source(n):
            if n < GLU0:
                c, k = in_col(n), 2 * (n % GRP)
                w = A["w_in"]
            elif n < RET0:
                pair, half_ = GLU_ORDER[n - GLU0]
                return A["ssm_w_glu"][4 * P * half_:4 * P * (half_ + 1), SEQ * pair:SEQ * (pair + 1)
                                      ].rearrange("(b p) n -> p b n", p=P)
            elif n < SSM0:
                c, k = (n - RET0) // 4, 2 * ((n - RET0) % 4)
                w = A["w_out"]
            elif n < FFN0:
                c, k = (n - SSM0) // 4, 8 + 2 * ((n - SSM0) % 4)
                w = A["w_out"]
            else:
                c, k = 0, 2 * ((n - FFN0) % GRP)
                w = A["w_gate"] if n < FFN0 + GRP else A["w_up"]
            return w[k * P:(k + 2) * P, c * NCOL:(c + 1) * NCOL].rearrange("(b p) n -> p b n", p=P)

        def h2(kb, part):
            if kb < 8:
                return (actA_hi, actA_lo)[part][:, kb, :]
            return (h2B_hi, h2B_lo)[part][:, kb - 8, :]

        def act_block(kb, part):
            if kb < 8:
                return (actA_hi, actA_lo)[part][:, kb, :]
            return (actB_hi, actB_lo)[part][:, kb - 8, :]

        def wide(x, k):
            return x[:, k].unsqueeze(2).to_broadcast([P, GROUPS, CH])

        def s5_group(b):
            return slice(BG * b, BG * (b + 1))

        raw2 = raw[:].rearrange("p s (b n) -> p s b n", b=2)
        raw4 = raw[:].rearrange("p s (b n) -> p s b n", b=4)
        kst_w = kst[:].rearrange("p u h (d c) -> p u h d c", c=CH)

        def state_groups(b, x):
            g = BG * (b % HB)
            return state[:, b // HB, x, :, g:g + BG]

        def load_y_tables(eng, b, rows, signals):
            if b >= YBUF:
                eng.wait_ge(S["y_mm"], b - YBUF + 1)
            for i in rows:
                eng.dma_start(y_tab[i * CH:(i + 1) * CH, b % YBUF, 0],
                              k_dram[s5_group(b), :, i * CH:i * CH + P].rearrange("g c w -> c g w")
                              ).then_inc(signals[b % YBUF], 16)
            if 0 in rows:
                eng.dma_start(y_tab[:, b % YBUF, 1], c_dram[:, s5_group(b)]).then_inc(d_clr[b % YBUF], 16)

        def store_y(eng, h):
            eng.wait_ge(S["y1_ready"], 2 * h + 2)
            for j in range(LOC):
                eng.dma_start(y_dram.rearrange("(g c) (j k) -> j c g k", c=CH, k=NCH)[
                                  j, :, HALF * h:HALF * (h + 1)],
                              y1[j * CH:(j + 1) * CH, HALF * h:HALF * (h + 1)]).then_inc(d_y1st[h], 16)

        def load_y1T(eng, h):
            eng.wait_ge(d_y1st[h], 16 * LOC)
            if h == 0:
                eng.wait_ge(S["qk_mm"], 4)
            rows = slice(HALF * CH * h, HALF * CH * (h + 1))
            eng.dma_start(y1T[:, 4 * h:4 * h + 4], y_dram[rows].rearrange("(b r) p -> r b p", r=P)
                          ).then_inc(d_y1T[h], 16)

        def scan_step(tt, link, done, h, k):
            prev, cur, t = state[:, h, :, k], state[:, h, :, k + 1], scan_t[:, h]
            of_half = mul[:, :, :, HALF * h:HALF * (h + 1)]
            link(tt(t, prev.unsqueeze(1).to_broadcast([P, 2, 2, HALF]), of_half, ALU.mult))
            link(tt(cur, cur, t[:, 0], ALU.add))
            tt(cur[:, 0], cur[:, 0], t[:, 1, 1], ALU.add)
            last = tt(cur[:, 1], cur[:, 1], t[:, 1, 0], ALU.add)
            if k == NCH - 3:
                last.then_inc(done, 1)
            else:
                link(last)

        @block.sync
        def _(sp):
            def load(n, src, turn=None):
                slot = n % RAW
                if turn is not None:
                    sp.wait_ge(S["low_done"], turn * TURN + (n - RAW + 1))
                elif n >= RAW:
                    sp.wait_ge(S["low_done"], n - RAW + 1)
                glu = turn is None and GLU0 <= n < RET0
                sp.dma_start((raw4 if glu else raw2)[:, slot], src).then_inc(d_raw[slot], 16)

            def u_rows(h, dst, signal):
                for i in range(LOC):
                    sp.dma_start(dst[i * CH:(i + 1) * CH, HALF * h:HALF * (h + 1)],
                                 u_dram.rearrange("(g c) (i k) -> i c g k", c=CH, k=NCH)[
                                     LOC - 1 - i, :, HALF * h:HALF * (h + 1)]).then_inc(signal, 16)

            def load_decay(h):
                if h < 2:
                    sp.wait_ge(S["v_mm"], NB)
                else:
                    sp.wait_ge(S["sT_ready"], h - 1)
                sp.dma_start(dec[:, h % 2], A["decay"][h]).then_inc(d_dec[h % 2], 16)

            def before(n):
                if n < KB // 2:
                    sp.dma_start(xT[:, 2 * n:2 * n + 2], A["xT"][:, 2 * n:2 * n + 2]).then_inc(d_xT[n], 16)
                for t in range(TOK):
                    if n == 6 + 2 * t:
                        sp.dma_start(x_tok[:, t], A["x_tok"][:, t]).then_inc(d_xtok[t], 16)
                    if n == 10 + 3 * t:
                        sp.dma_start(bc[:, 2 * t:2 * t + 2], A["bc"][:, 2 * t:2 * t + 2]).then_inc(d_bc[t], 16)
                if n == 9:
                    sp.dma_start(ident[:], A["ident"]).then_inc(d_ident, 16)
                if n == 14:
                    sp.dma_start(dsk[:], A["dsk"]).then_inc(d_dsk, 16)
                    sp.dma_start(eye16[:], A["eye16"]).then_inc(d_dsk, 16)
                if n == 20:
                    sp.dma_start(rope[:], A["rope"]).then_inc(d_rope, 16)
                for h in range(2):
                    rows = slice(HALF * CH * h, HALF * CH * (h + 1))
                    if n == U_TR[h] + 9:
                        sp.wait_ge(S["u_copied"], h + 1)
                        sp.dma_start(u_dram[rows].rearrange("(b r) p -> r b p", r=P), uT[:, 4 * h:4 * h + 4]
                                     ).then_inc(d_uTst[h], 16)
                    if n == U_TR[h] + 10:
                        sp.wait_ge(d_uTst[h], 16)
                        u_rows(h, u_loc, d_u[h])
                    if n == V_AT[HB * (h + 1) - 1] + 9:
                        sp.wait_ge(S["v_free"], HB * (h + 1))
                        for x in range(2):
                            sp.dma_start(state[STATE * x:STATE * (x + 1), h, 1],
                                         state[STATE * (1 - x):STATE * (2 - x), h, 0]).then_inc(d_swap[h], 16)
                for h in range(2):
                    if n == Y_STORE[h]:
                        store_y(sp, h)
                    if n == Y_LOAD[h]:
                        load_y1T(sp, h)
                for b in range(NB):
                    if n == CL_AT[b] + 4:
                        sp.wait_ge(S["cl_ready"], b + 1)
                        sp.dma_start(c_dram[:, s5_group(b)],
                                     cl[:, b % 2, :, 1:].rearrange("p g d c -> p g (d c)")
                                     ).then_inc(d_clst[b % 2], 16)
                    if n == TAB_AT[b] + 9:
                        sp.wait_ge(S["kst_ready"], b + 1)
                        for q in range(4):
                            sp.dma_start(k_dram.rearrange("(b h q) c w -> b q c h w", h=2, q=4)[b, q],
                                         kst[32 * q:32 * q + CH, b % 2]).then_inc(d_kst[b % 2], 16)
                if n == TAB_AT[-1] + 11:
                    sp.wait_ge(S["tab_mm"], NB)
                    u_rows(0, u_loc2, d_u2)
                if n == TAB_AT[-1] + 12:
                    u_rows(1, u_loc2, d_u2)
                if n == TAB_AT[-1] + 14:
                    for x in range(2):
                        sp.wait_ge(d_kst[x], 16 * 4 * HB)
                        sp.wait_ge(d_clst[x], 16 * HB)
                for b in range(NB):
                    if b < YBUF and n == 54 + 2 * b:
                        load_y_tables(sp, b, range(LOC), d_mt)
                    if b >= YBUF and n == Y_AT[b - YBUF] + 7:
                        load_y_tables(sp, b, range(LOC // 2), d_mt)
                for h in range(HEADS):
                    if n == DECAY_LOAD[h]:
                        load_decay(h)
                if n == GLU0 + 9:
                    sp.wait_ge(S["y_mm"], NB)
                    sp.dma_start(x2[:], A["x_tok"]).then_inc(d_xres, 16)

            for n in range(LOOP0):
                before(n)
                load(n, chunk_source(n))
            sp.wait_ge(S["ret_ready"], 2)
            sp.dma_start(g_final[:], A["g_final"]).then_inc(d_gfin, 16)
            with sp.Fori(0, FG - 1) as j:
                for c in range(TURN):
                    if c < 2 * GRP:
                        w = A["w_gate"] if c < GRP else A["w_up"]
                        k = 2 * (c % GRP)
                        src = w[k * P:(k + 2) * P, bass.ds((j + 1) * NCOL, NCOL)]
                    else:
                        col, k = divmod(c - 2 * GRP, 2)
                        src = A["w_down"][bass.ds(j * (4 * P) + 2 * k * P, 2 * P), col * NCOL:(col + 1) * NCOL]
                    load(LOOP0 + c, src.rearrange("(b p) n -> p b n", p=P), turn=j)
            for c in range(GRP):
                col, k = divmod(c, 2)
                row = (FG - 1) * 4 * P + 2 * k * P
                load(TAIL0 + c, A["w_down"][row:row + 2 * P, col * NCOL:(col + 1) * NCOL]
                     .rearrange("(b p) n -> p b n", p=P))
            for h in range(2):
                for t in range(TOK):
                    sp.wait_ge(S[("fin_ready", "fin1_ready")[t]], h + 1)
                    sp.dma_start(out[:, t, 1024 * h:1024 * (h + 1)], x_gain[:, t, 1024 * h:1024 * (h + 1)]
                                 ).then_inc(d_out, 16)
            sp.wait_ge(d_out, 64)

        @block.scalar
        def _(act):
            def high(n, turn=None, at=None):
                if turn is None:
                    act.wait_ge(d_raw[n % RAW], 16 * (n // RAW + 1))
                    if n >= SPL:
                        act.wait_ge(S["pe_done"], n - SPL + 1)
                    s = n
                else:
                    s = at
                    act.wait_ge(d_raw[s % RAW], turn * (16 * TURN // RAW) + 16 * (s // RAW + 1))
                    act.wait_ge(S["pe_done"], turn * TURN + (s - SPL + 1))
                nc.scalar.activation(w_hi[:, s % SPL], raw[:, s % RAW], ACT.Copy).then_inc(S["high_done"], 1)

            def xh(r):
                act.wait_ge(d_xT[r], 16)
                if r == 0:
                    act.wait_ge(d_vec, 16)
                for kb in (2 * r, 2 * r + 1):
                    nc.scalar.activation(act_block(kb, 0), xT[:, kb], ACT.Copy, scale=vec[:, V_MIX + kb:V_MIX + kb + 1]
                                         ).then_inc(S["xh_ready"], 1)

            act.dma_start(vec[:], A["vec"]).then_inc(d_vec, 16)
            act.dma_start(par[:], A["par"]).then_inc(d_par, 16)
            act.wait_ge(S["warm_ready"], 1)
            nc.scalar.activation(half[:, 0:1], warm[:, 0:1], ACT.Copy).then_inc(S["table_ready"], 1)

            def ret_out(p):
                act.wait_ge(S["head_mm"], 2 * p + 2)
                nc.scalar.activation(ret[:, 2 * p:2 * p + 2].rearrange("p h s -> p (h s)"), ps[:, 7],
                                     ACT.Copy).then_inc(S["out_free"], 1)

            def qk_evac(i):
                act.wait_ge(S["qk_mm"], i + 1)
                dst = (qT, kT)[i % 2][:, 4 * (i // 2):4 * (i // 2) + 4]
                nc.scalar.activation(dst.rearrange("p (a b) s -> p a (b s)", a=2), ps[:, 4:6], ACT.Copy
                                     ).then_inc(S["qk_free"], 1)

            def side(n):
                gi, r = divmod(n - 4 - (GRP - 1), GRP)
                if n in (9, 10):
                    t = n - 9
                    act.wait_ge(d_xtok[t], 16)
                    if t:
                        act.wait_ge(S["ss_ready"], 1)
                    nc.scalar.activation(ps[:, 4:8], x_tok[:, t].rearrange("p (a b) -> p a b", a=4), ACT.Square,
                                         accum_out=ss[:, R_MIX, t:t + 1]).then_inc(S["ss_ready"], 1)
                if n == 16:
                    act.wait_ge(d_bc[1], 16)
                    for x, scale in ((2, vec[:, V_SGN + 1:V_SGN + 2]), (3, -1.0)):
                        flat = bc[:, x].rearrange("p g c -> p (g c)")
                        nc.scalar.activation(flat, flat, ACT.Copy, scale=scale).then_inc(S["c_ready"], 1)
                if n == 8:
                    act.wait_ge(S["trig_in_ready"], 1)
                    nc.scalar.activation(scr[:, 6], scr[:, 4], ACT.Sin).then_inc(S["trig_ready"], 1)
                    nc.scalar.activation(scr[:, 7], scr[:, 4], ACT.Sin, scale=0.5).then_inc(S["trig_ready"], 1)
                if r == 0 and 0 <= gi < len(IN_COLS):
                    c = IN_COLS[gi]
                    if gi == 0:
                        act.wait_ge(S["rstd_mix_ready"], 1)
                    act.wait_ge(S["pe_done"], GRP * (gi + 1))
                    for t in range(TOK):
                        src = ps[:, 2 * (gi % 2) + t]
                        scale = rstd[:, R_MIX, t:t + 1]
                        half_ = (c % 2) * NCOL
                        if c >= 8:
                            dst, func = u_tok[:, t, half_:half_ + NCOL], ACT.Copy
                        elif c >= 6:
                            dst, func = sg[:, t, half_:half_ + NCOL], ACT.Silu
                        elif c >= 4:
                            dst, func = v[:, t, half_:half_ + NCOL], ACT.Copy
                        else:
                            dst, func = qs[:, t], ACT.Copy
                            if gi == 4 and t == 0:
                                act.wait_ge(S["cl_ready"], NB)
                                act.wait_ge(S["wb_ready"], NB)
                                act.wait_ge(S["tab_mm"], NB)
                            if t == 0 and gi > 4:
                                act.wait_ge(S["qr_ready"], gi - 4)
                        if gi == 8 and t == 0:
                            for h in range(2):
                                act.wait_ge(d_uTst[h], 16)
                        nc.scalar.activation(dst, src, func, scale=scale).then_inc(S["proj_free"], 1)
                for h in range(2):
                    if n == U_TR[h] + 4:
                        act.wait_ge(S["uT_mm"], h + 1)
                        nc.scalar.activation(uT[:, 4 * h:4 * h + 4].rearrange("p (a b) s -> p a (b s)", a=2),
                                             ps[:, 4:6], ACT.Copy).then_inc(S["u_copied"], 1)
                for b in range(NB):
                    if n == TAB_AT[b] + 4:
                        act.wait_ge(S["tab_mm"], b + 1)
                        if b >= 2:
                            act.wait_ge(S["v_mm"], b - 1)
                        nc.scalar.activation(wbT[:, b % 2].rearrange("p (a g) s -> p a (g s)", a=2), ps[:, 4:6],
                                             ACT.Copy).then_inc(S["wbT_ready"], 1)
                        if b == 0:
                            act.wait_ge(S["const_ready"], 1)
                        if b >= 2:
                            act.wait_ge(d_kst[b % 2], 64 * (b // 2))
                        nc.scalar.activation(kst_w[:, b % 2, :, LOC - 1:], ps[:, 6, 0:2 * P]
                                             .rearrange("p (h d c) -> p h d c", h=2, c=CH), ACT.Copy
                                             ).then_inc(S["kpsum_free"], 1)
                    if n == V_AT[b] + 4:
                        act.wait_ge(S["v_mm"], b + 1)
                        nc.scalar.activation(state_groups(b, 0).rearrange("p k g -> p g k"),
                                             ps[:, 7, 0:NCH * BG].rearrange("p (g k) -> p g k", g=BG), ACT.Copy
                                             ).then_inc(S["v_free"], 1)
                for i in range(4):
                    if n == QK_TR[i] + 4:
                        qk_evac(i)
                    if n == HEAD_AT[2 * i + 1] + 4:
                        ret_out(i)
                    if n == Y_AT[2 * i + 1] + 4:
                        act.wait_ge(S["y_mm"], 2 * i + 2)
                        nc.scalar.activation(y1[:, 16 * i:16 * i + 16].rearrange("p g k -> p (g k)"), ps[:, 6],
                                             ACT.Gelu_apprx_tanh).then_inc(S["y1_ready"], 1)
                for h in range(2):
                    if n == Y1T_AT[h]:
                        act.wait_ge(d_y1T[h], 16)
                        act.wait_ge(S["y_mm"], NB)
                        nc.scalar.activation(y1T_parts[h][0][:], y1T[:, 4 * h:4 * h + 4], ACT.Copy
                                             ).then_inc(S["y1T_hi_ready"], 1)
                    if n == RET_TR[h] + 4:
                        ret_high(h)
                for p in range(4):
                    if n == GLU0 + GLU_END[p] + 3:
                        glu_pair(p)
                    if p % 2 and n == GLU0 + GLU_END[p] + 4:
                        glu_half(p // 2)
                c, r = divmod(n - (SSM0 + 9), 4)
                if r == 0 and 0 <= c < 4:
                    h2_high(c)
                    x2_square(c)

            def glu_pair(p):
                act.wait_ge(S["pe_done"], GLU0 + GLU_END[p])
                for j in range(2):
                    c8 = 2 * p + j
                    nc.scalar.activation(zT[:, c8], ps[:, 2 * (p % 2) + j, 0:SEQ], ACT.Sigmoid,
                                         bias=vec[:, V_BGLU + c8:V_BGLU + c8 + 1]).then_inc(S["sig_ready"], 1)

            def glu_half(q):
                act.wait_ge(S["zT_ready"], q + 1)
                nc.scalar.activation(sqT[:, 4 * q:4 * q + 4], zT[:, 4 * q:4 * q + 4], ACT.Square
                                     ).then_inc(S["sqT_ready"], 1)
                for c in range(4):
                    c8 = 4 * q + c
                    nc.scalar.activation(actB_hi[:, c8], zT[:, c8], ACT.Copy,
                                         scale=vec[:, V_OUTG + c8:V_OUTG + c8 + 1]).then_inc(S["ssm_hi"], 1)

            def ret_high(q):
                for p in (2 * q, 2 * q + 1):
                    act.wait_ge(S["retT_mm"], p + 1)
                    for h in range(2):
                        nc.scalar.activation(actA_hi[:, 2 * p + h], ps[:, 4 + p, SEQ * h:SEQ * (h + 1)], ACT.Copy,
                                             scale=vec[:, V_RETG + 2 * p + h:V_RETG + 2 * p + h + 1]
                                             ).then_inc(S["ret_hi"], 1)

            def h2_high(c):
                act.wait_ge(S["h2_mm"], c + 1)
                for k in range(4):
                    kb = 4 * c + k
                    src = ps[:, 4 + 2 * (c % 2) + k // 2, SEQ * (k % 2):SEQ * (k % 2 + 1)]
                    nc.scalar.activation(h2(kb, 0), src, ACT.Copy, scale=vec[:, V_FFN + kb:V_FFN + kb + 1]
                                         ).then_inc(S["h2_hi"], 1)

            def x2_square(c):
                act.wait_ge(S["cols_added"], 5 + c)
                for t in range(TOK):
                    if c or t:
                        act.wait_ge(S["x2_sq"], 2 * c + t)
                    nc.scalar.activation(sqT[:, 0:2].rearrange("p a s -> p (a s)"),
                                         x2[:, t, NCOL * c:NCOL * (c + 1)], ACT.Square,
                                         accum_out=ss4[:, 0, c, t:t + 1]).then_inc(S["x2_sq"], 1)

            for n in range(FFN0 + GRP + 4):
                if n < KB // 2:
                    xh(n)
                if n in SIDE_FIRST:
                    side(n)
                    high(n)
                else:
                    high(n)
                    side(n)

            def silu(chunks):
                act.wait_ge(S["pe_done"], chunks)
                for t in range(TOK):
                    nc.scalar.activation(ff_act[:, t], ps[:, t], ACT.Silu, scale=rstd[:, R_FFN, t:t + 1]
                                         ).then_inc(S["silu_ready"], 1)

            def ffT_high(count):
                act.wait_ge(S["ffT_mm"], count)
                nc.scalar.activation(ffT_hi[:].rearrange("p (a b) s -> p a (b s)", a=2), ps[:, 4:6], ACT.Copy
                                     ).then_inc(S["ffT_hi_ready"], 1)

            act.wait_ge(S["rstd_ffn_ready"], 1)
            silu(FFN0 + GRP)
            for n in range(FFN0 + GRP + 4, LOOP0 + SPL):
                high(n)
            def turn(j, last=False):
                for c in range(SPL, TURN + SPL):
                    high(None, turn=j, at=LOOP0 + c)
                    if c == GRP + SPL - 1:
                        ffT_high(j + 1)
                        silu(j * TURN + (LOOP0 + GRP))
                    if last and c == 2 * GRP + 8:
                        act.wait_ge(S["ffT_mm"], FG)
                        nc.scalar.activation(ffE_hi[:].rearrange("p (a b) s -> p a (b s)", a=2), ps[:, 0:2], ACT.Copy
                                             ).then_inc(S["ffT_hi_ready"], 1)

            with act.Fori(0, FG - 2) as j:
                turn(j)
            turn(FG - 2, last=True)
            for c in range(SPL, GRP):
                high(TAIL0 + c)
            for c in range(4):
                for t in range(TOK):
                    act.wait_ge(S["last_added"], 2 * c + t + 1)
                    if c or t:
                        act.wait_ge(S["fin_sq"], 2 * c + t)
                    nc.scalar.activation(y1T[:, 0:2].rearrange("p a s -> p (a s)"),
                                         x2[:, t, NCOL * c:NCOL * (c + 1)], ACT.Square,
                                         accum_out=ss4[:, 1, c, t:t + 1]).then_inc(S["fin_sq"], 1)
            act.wait_ge(S["gain_done"], 4)
            act.wait_ge(S["rstd_fin_ready"], 1)
            for h in range(2):
                at = slice(1024 * h, 1024 * (h + 1))
                nc.scalar.activation(x_gain[:, 1, at], x_gain[:, 1, at], ACT.Copy, scale=rstd[:, R_FIN, 1:2]
                                     ).then_inc(S["fin1_ready"], 1)

        @block.vector
        def _(dve):
            steps = [0]

            def link(ins):
                steps[0] += 1
                ins.then_inc(S["dve_step"], 1)
                dve.wait_ge(S["dve_step"], steps[0])

            tt, ts, stt = nc.vector.tensor_tensor, nc.vector.tensor_scalar, nc.vector.scalar_tensor_tensor

            def low(n, turn=None, at=None):
                if turn is None:
                    dve.wait_ge(S["high_done"], n + 1)
                    s = n
                else:
                    s = at
                    dve.wait_ge(S["high_done"], turn * TURN + (s + 1))
                tt(w_lo[:, s % SPL], raw[:, s % RAW], w_hi[:, s % SPL].bitcast(F32), ALU.subtract
                   ).then_inc(S["low_done"], 1)

            nc.vector.memset(warm[:], 0.0).then_inc(S["warm_ready"], 1)

            def xl(r):
                dve.wait_ge(S["xh_ready"], 2 * r + 2)
                for kb in (2 * r, 2 * r + 1):
                    last = gain_low(act_block(kb, 1), xT[:, kb], V_MIX + kb, act_block(kb, 0))
                last.then_inc(S["xl_ready"], 1)

            def gain_low(dst, src, at, hi):
                return stt(dst, src, vec[:, at:at + 1], hi.bitcast(F32), ALU.mult, ALU.subtract)

            a_re, a_im = par[:, 0], par[:, 1]
            C1, C2, C3 = 6.28125, 0.0019350051879882812, 3.019916050561733e-07
            MAGIC = 12582912.0

            def modulus():
                dve.wait_ge(d_par, 16)
                tt(scr[:, 9], a_re, a_re, ALU.mult)
                link(tt(scr[:, 12], a_im, a_im, ALU.mult))
                link(tt(scr[:, 9], scr[:, 9], scr[:, 12], ALU.add))
                link(nc.vector.reciprocal(scr[:, 9], scr[:, 9]))

            def angles():
                dve.wait_ge(d_par, 16)
                dve.wait_ge(S["dt_ready"], 1)
                link(tt(scr[:, 2], a_im, scr[:, 0], ALU.mult))
                link(ts(scr[:, 3], scr[:, 2], 1 / (2 * np.pi), MAGIC, ALU.mult, ALU.add))
                link(ts(scr[:, 3], scr[:, 3], -MAGIC, None, ALU.add))
                link(stt(scr[:, 8], scr[:, 3], -C1, scr[:, 2], ALU.mult, ALU.add))
                link(stt(scr[:, 11], scr[:, 3], -C2, scr[:, 8], ALU.mult, ALU.add))
                link(stt(scr[:, 10], scr[:, 3], -C3, scr[:, 11], ALU.mult, ALU.add))
                ts(scr[:, 4], scr[:, 10], -3.1415925, 3.1415925, ALU.max, ALU.min).then_inc(S["trig_in_ready"], 1)

            def complex_mul(o_r, o_i, x_r, x_i, y_r, y_i, t_r, t_i):
                tt(t_r, x_i, y_i, ALU.mult)
                tt(t_i, x_i, y_r, ALU.mult)
                tt(o_r, x_r, y_r, ALU.mult)
                link(tt(o_i, x_r, y_i, ALU.mult))
                tt(o_r, o_r, t_r, ALU.subtract)
                link(tt(o_i, o_i, t_i, ALU.add))

            def s5_params():
                dve.wait_ge(S["trig_ready"], 2)
                dve.wait_ge(S["pow_ready"], 1)
                mag, sin, sinh = scr[:, 5], scr[:, 6], scr[:, 7]
                link(tt(scr[:, 8], sinh, sinh, ALU.mult))
                link(ts(scr[:, 8], scr[:, 8], -2.0, 1.0, ALU.mult, ALU.add))
                nc.vector.memset(pr[:, 0], 1.0)
                nc.vector.memset(pi[:, 0], 0.0)
                tt(pr[:, 1], mag, scr[:, 8], ALU.mult)
                link(tt(pi[:, 1], mag, sin, ALU.mult))
                link(ts(scr[:, 8], pr[:, 1], -1.0, None, ALU.add))
                tt(scr[:, 10], scr[:, 8], a_re, ALU.mult)
                tt(scr[:, 11], pi[:, 1], a_im, ALU.mult)
                tt(scr[:, 12], pi[:, 1], a_re, ALU.mult)
                link(tt(scr[:, 13], scr[:, 8], a_im, ALU.mult))
                tt(scr[:, 10], scr[:, 10], scr[:, 11], ALU.add)
                link(tt(scr[:, 12], scr[:, 12], scr[:, 13], ALU.subtract))
                tt(scr[:, 10], scr[:, 10], scr[:, 9], ALU.mult)
                link(tt(scr[:, 12], scr[:, 12], scr[:, 9], ALU.mult))
                sgn = vec[:, V_SGN:V_SGN + 1]
                ts(scr[:, 11], scr[:, 10], sgn, None, ALU.mult)
                ts(scr[:, 13], scr[:, 12], sgn, None, ALU.mult).then_inc(S["signs_ready"], 1)
                dve.wait_ge(S["signs_ready"], 1)

            def s5_powers(done):
                def two(x, a, b):
                    return x[:, a:b]

                def times(x, k, n):
                    return x[:, k].unsqueeze(1).to_broadcast([P, n, GROUPS])

                tr = cl_t[:].rearrange("p g d c -> p (g d c)")[:, 0:4 * GROUPS].rearrange("p (a g) -> p a g", a=4)
                ti = cl_t[:].rearrange("p g d c -> p (g d c)")[:, 4 * GROUPS:8 * GROUPS].rearrange(
                    "p (a g) -> p a g", a=4)
                complex_mul(pr[:, done + 1:2 * done + 1], pi[:, done + 1:2 * done + 1],
                            pr[:, 1:done + 1], pi[:, 1:done + 1], times(pr, done, done), times(pi, done, done),
                            tr[:, 0:done], ti[:, 0:done])
                if done < 4:
                    return
                sgn = vec[:, V_SGN:V_SGN + 1]
                nc.vector.tensor_copy(mul[:, 0, 0], pr[:, LOC])
                nc.vector.tensor_copy(mul[:, 0, 1], pr[:, LOC])
                ts(mul[:, 1, 0], pi[:, LOC], sgn, -1.0, ALU.mult, ALU.mult)
                ts(mul[:, 1, 1], pi[:, LOC], sgn, None, ALU.mult).then_inc(S["mul_ready"], 1)

            def s5_inputs():
                dve.wait_ge(d_bc[0], 16)
                nc.vector.memset(bb[:, GROUPS], 0.0)
                t_a = cl[:].rearrange("p a g d c -> p (a g d c)")[:, 0:GROUPS * CH].rearrange(
                    "p (g c) -> p g c", c=CH)
                tt(bb[:, 0:GROUPS], bc[:, 0], wide(scr, 10), ALU.mult)
                link(tt(t_a, bc[:, 1], wide(scr, 13), ALU.mult))
                tt(bb[:, 0:GROUPS], bb[:, 0:GROUPS], t_a, ALU.add).then_inc(S["bb_ready"], 1)

            def d_skip():
                dve.wait_ge(d_dsk, 32)
                link(tt(dtmp[:], dsk[:].unsqueeze(2).to_broadcast([P, GROUPS // 4, CH]),
                        eye16[:].unsqueeze(1).to_broadcast([P, GROUPS // 4, CH]), ALU.mult))

            def cl_table(b):
                o = cl[:, b % 2]
                if b == 0:
                    dve.wait_ge(S["c_ready"], 2)
                    dve.wait_ge(S["bb_ready"], 1)
                if b >= 2:
                    dve.wait_ge(d_clst[b % 2], 16 * (b // 2))
                    dve.wait_ge(S["tab_mm"], b - 1)

                if b:
                    dve.wait_ge(S["cl_ready"], b)

                def c_(k):
                    return bc[:, k, s5_group(b)].unsqueeze(2).to_broadcast([P, BG, LOC + 1, CH])

                def p_(x):
                    return x[:, :, s5_group(b)].rearrange("p d g -> p g d").unsqueeze(3).to_broadcast(
                        [P, BG, LOC + 1, CH])

                tt(o, c_(2), p_(pr), ALU.mult)
                link(tt(cl_t[:], c_(3), p_(pi), ALU.mult))
                tt(o, o, cl_t[:], ALU.add).then_inc(S["cl_ready"], 1)

            def rotate(i):
                if i == 0:
                    dve.wait_ge(d_rope, 16)
                dve.wait_ge(S["proj_free"], 2 * (4 + i) + 2)
                if i:
                    dve.wait_ge(S["qk_mm"], i)
                four = [P, 4, HEAD_DIM]
                x = [qs[:, t].rearrange("p (h d) -> p h d", h=4) for t in range(TOK)]
                y = [qr[:, t].rearrange("p (h d) -> p h d", h=4) for t in range(TOK)]
                for t in range(TOK):
                    last = tt(y[t], x[t], rope[:, t, 0].unsqueeze(1).to_broadcast(four), ALU.mult)
                for t in range(TOK):
                    for a in range(2):
                        lo_, hi_ = slice(64 * a, 64 * a + 64), slice(64 * (1 - a), 64 * (1 - a) + 64)
                        last = tt(rot[:, t].rearrange("p (h d) -> p h d", h=4)[:, :, lo_], x[t][:, :, hi_],
                                  rope[:, t, 1, lo_].unsqueeze(1).to_broadcast([P, 4, 64]), ALU.mult)
                link(last)
                tt(qr[:], qr[:], rot[:], ALU.add).then_inc(S["qr_ready"], 1)

            def decayed(h):
                dve.wait_ge(S["score_mm"], h + 1)
                dve.wait_ge(d_dec[h % 2], 16 * (h // 2 + 1))
                if h >= 2:
                    dve.wait_ge(S["head_mm"], h - 1)
                tt(sT[:, h % 2].rearrange("p a s -> p (a s)"), ps[:, 4 + h % 2],
                   dec[:, h % 2].rearrange("p a s -> p (a s)"), ALU.mult).then_inc(S["sT_ready"], 1)

            def head_stats(p):
                dve.wait_ge(S["out_free"], p + 1)
                last = None
                for k in range(4 * p, 4 * p + 4):
                    last = nc.vector.bn_stats(bn[:, k], ret[:, k // 2, P * (k % 2):P * (k % 2 + 1)])
                link(last)
                for k in range(4 * p, 4 * p + 4):
                    last = nc.vector.bn_aggr(mv[:, k], bn[:, k])
                if p % 2:
                    last.then_inc(S["bn_ready"], 1)

            def normalise(q):
                dve.wait_ge(S["rret_ready"], q + 1)
                for h in range(4 * q, 4 * q + 4):
                    for t in range(TOK):
                        g = sg[:, t, P * h:P * (h + 1)]
                        last = ts(g, g, rret[:, 2 * h + t:2 * h + t + 1], None, ALU.mult)
                link(last)
                for h in range(4 * q, 4 * q + 4):
                    for t in range(TOK):
                        o = ret[:, h, P * t:P * (t + 1)]
                        last = stt(o, o, mv[:, 2 * h + t, 0:1], sg[:, t, P * h:P * (h + 1)], ALU.subtract, ALU.mult)
                last.then_inc(S["ret_ready"], 1)

            def y1_low(q):
                dve.wait_ge(S["y1T_hi_ready"], q + 1)
                hi, lo = y1T_parts[q]
                tt(lo[:], y1T[:, 4 * q:4 * q + 4], hi[:].bitcast(F32), ALU.subtract).then_inc(S["y1T_lo_ready"], 1)

            def glu_half(q):
                dve.wait_ge(S["sig_ready"], 4 * q + 4)
                at = slice(4 * q, 4 * q + 4)
                tt(zT[:, at], zT[:, at], y1T[:, at], ALU.mult).then_inc(S["zT_ready"], 1)
                dve.wait_ge(S["ssm_hi"], 4 * q + 4)
                dve.wait_ge(S["zT_ready"], q + 1)
                for c in range(4 * q, 4 * q + 4):
                    gain_low(actB_lo[:, c], zT[:, c], V_OUTG + c, actB_hi[:, c]).then_inc(S["ssm_lo"], 1)

            def ret_low(q):
                for p in (2 * q, 2 * q + 1):
                    dve.wait_ge(S["ret_hi"], 2 * p + 2)
                    for h in range(2):
                        gain_low(actA_lo[:, 2 * p + h], ps[:, 4 + p, SEQ * h:SEQ * (h + 1)], V_RETG + 2 * p + h,
                                 actA_hi[:, 2 * p + h]).then_inc(S["ret_lo"], 1)

            def h2_low(c):
                for k in range(4):
                    kb = 4 * c + k
                    if k % 2 == 0:
                        dve.wait_ge(S["h2_hi"], kb + 2)
                    src = ps[:, 4 + 2 * (c % 2) + k // 2, SEQ * (k % 2):SEQ * (k % 2 + 1)]
                    gain_low(h2(kb, 1), src, V_FFN + kb, h2(kb, 0)).then_inc(S["h2_lo"], 1)

            def out_col_ret(c):
                if c == 0:
                    dve.wait_ge(d_xres, 16)
                dve.wait_ge(S["pe_done"], RET0 + 4 * (c + 1))
                cols = x2[:, :, NCOL * c:NCOL * (c + 1)]
                b0 = 2 * (c % 2)
                tt(cols, ps[:, b0:b0 + 2], cols, ALU.add).then_inc(S["cols_added"], 1)

            def out_col_ssm(c):
                if c == 0:
                    dve.wait_ge(S["rstd_ssm_ready"], 1)
                dve.wait_ge(S["pe_done"], SSM0 + 4 * (c + 1))
                dve.wait_ge(S["cols_added"], c + 1)
                for t in range(TOK):
                    cols = x2[:, t, NCOL * c:NCOL * (c + 1)]
                    last = stt(cols, ps[:, 2 * (c % 2) + t], rstd[:, R_SSM, t:t + 1], cols, ALU.mult, ALU.add)
                last.then_inc(S["cols_added"], 1)

            def ff(count, chunks):
                dve.wait_ge(S["pe_done"], chunks)
                dve.wait_ge(S["silu_ready"], count * 2)
                for t in range(TOK):
                    last = stt(ff_act[:, t], ps[:, 2 + t], rstd[:, R_FFN, t:t + 1], ff_act[:, t], ALU.mult, ALU.mult)
                last.then_inc(S["ff_ready"], 1)

            def ffT_low(count):
                dve.wait_ge(S["ffT_hi_ready"], count)
                tt(ffT_lo[:].rearrange("p (a b) s -> p a (b s)", a=2), ps[:, 4:6],
                   ffT_hi[:].rearrange("p (a b) s -> p a (b s)", a=2).bitcast(F32), ALU.subtract
                   ).then_inc(S["ffT_lo_ready"], 1)

            def down_col(chunks, before, c):
                dve.wait_ge(S["pe_done"], chunks)
                dve.wait_ge(S["cols_added"], before)
                b0 = 6 - 2 * (c % 2)
                cols = x2[:, :, NCOL * c:NCOL * (c + 1)]
                tt(cols, ps[:, b0:b0 + 2], cols, ALU.add).then_inc(S["cols_added"], 1)

            def side(n):
                if n == 3:
                    modulus()
                if n == 6:
                    angles()
                if n == PARAM_AT:
                    s5_params()
                if PARAM_AT < n < PARAM_AT + 4:
                    s5_powers(1 << (n - PARAM_AT - 1))
                if n == PARAM_AT + 4:
                    s5_inputs()
                if n == 18:
                    d_skip()
                for b in range(NB):
                    if n == CL_AT[b]:
                        cl_table(b)
                    if n == TAB_AT[b] + 4:
                        dve.wait_ge(S["kpsum_free"], b + 1)
                        diag = kst_w[:, b % 2, :, LOC - 1]
                        tt(diag, diag, dtmp[:, 2 * b:2 * b + 2], ALU.add).then_inc(S["kst_ready"], 1)
                for k in range(NCH - 2):
                    if n == SCAN_AT[k]:
                        if k == 0:
                            dve.wait_ge(d_swap[0], 32)
                        scan_step(tt, link, S["scanA_done"], 0, k)
                for i in range(4):
                    if n == QK_AT[i]:
                        rotate(i)
                for h in range(HEADS):
                    if n == DECAY_AT[h]:
                        decayed(h)
                for p in range(4):
                    if n == STATS_AT[p]:
                        head_stats(p)
                for q in range(2):
                    if n == Y1T_AT[q]:
                        y1_low(q)
                    if n == NORM_AT[q]:
                        normalise(q)
                    if n == GLU0 + GLU_END[2 * q + 1] + 3:
                        glu_half(q)
                    if n == RET_TR[q] + 4:
                        ret_low(q)
                if n == RET0 + 10:
                    dve.wait_ge(S["ssq_mm"], 1)
                    ts(ss[:, R_SSM], ps[:, 4, 0:TOK], 1 / RET_W, EPS, ALU.mult, ALU.add).then_inc(S["ssq_ready"], 1)
                c, r = divmod(n - (RET0 + 7), 4)
                if r == 0 and 0 <= c < 4:
                    out_col_ret(c)
                if r == 0 and 4 <= c < 8:
                    out_col_ssm(c - 4)
                c, r = divmod(n - (SSM0 + 9), 4)
                if r == 0 and 0 <= c < 4:
                    h2_low(c)
                if n == LOOP0 + 3:
                    ff(1, LOOP0)

            for n in range(LOOP0 + SPL):
                if n < KB // 2:
                    xl(n)
                if n in SIDE_FIRST_LOW:
                    side(n)
                    low(n)
                else:
                    low(n)
                    side(n)
            def turn(j, last=False):
                for c in range(SPL, TURN + SPL):
                    low(None, turn=j, at=LOOP0 + c)
                    if c == GRP + 3:
                        ffT_low(j + 1)
                    if c == 2 * GRP + 3:
                        ff(j + 2, j * TURN + (LOOP0 + 2 * GRP))
                    if last and c == 2 * GRP + 8:
                        dve.wait_ge(S["ffT_hi_ready"], FG)
                        tt(ffE_lo[:].rearrange("p (a b) s -> p a (b s)", a=2), ps[:, 0:2],
                           ffE_hi[:].rearrange("p (a b) s -> p a (b s)", a=2).bitcast(F32), ALU.subtract
                           ).then_inc(S["ffT_lo_ready"], 1)
                    if c >= 2 * GRP + 5 and c % 2:
                        col = (c - 2 * GRP - 5) // 2
                        down_col(j * TURN + (LOOP0 + 2 * GRP + 2 * col + 2), j * 4 + (col + 5), col)

            with dve.Fori(0, FG - 2) as j:
                turn(j)
            turn(FG - 2, last=True)

            def finish_col(col):
                at = slice(NCOL * col, NCOL * (col + 1))
                dve.wait_ge(S["pe_done"], TAIL0 + 2 * col + 2)
                dve.wait_ge(S["cols_added"], 4 * (FG - 1) + col + 5)
                for t in range(TOK):
                    tt(x2[:, t, at], ps[:, 6 - 2 * (col % 2) + t], x2[:, t, at], ALU.add
                       ).then_inc(S["last_added"], 1)
                dve.wait_ge(S["last_added"], 2 * col + 2)
                tt(x_gain[:, :, at], x2[:, :, at], g_final[:, at].unsqueeze(1).to_broadcast([P, TOK, NCOL]),
                   ALU.mult).then_inc(S["gain_done"], 1)

            dve.wait_ge(d_gfin, 16)
            for c in range(SPL, GRP):
                low(TAIL0 + c)
                if c % 2:
                    finish_col((c - 5) // 2)
            for col in range(2, 4):
                finish_col(col)
            dve.wait_ge(S["gain_done"], 4)
            dve.wait_ge(S["rstd_fin_ready"], 1)
            for h in range(2):
                at = slice(1024 * h, 1024 * (h + 1))
                ts(x_gain[:, 0, at], x_gain[:, 0, at], rstd[:, R_FIN, 0:1], None, ALU.mult).then_inc(S["fin_ready"], 1)

        @block.gpsimd
        def _(pool):
            steps = [0]

            def link(ins):
                steps[0] += 1
                ins.then_inc(S["pool_step"], 1)
                pool.wait_ge(S["pool_step"], steps[0])

            tt, ts = nc.gpsimd.tensor_tensor, nc.gpsimd.tensor_scalar

            def rsqrt(dst, src, ready, width=TOK):
                tt(dst, src, half[:, 0:width], ALU.pow).then_inc(ready, 1)

            pool.wait_ge(S["table_ready"], 1)
            nc.gpsimd.memset(half[:], -0.5)
            nc.gpsimd.memset(ones[:], 1.0)
            nc.gpsimd.memset(kst_w[:, 0, :, 0:LOC - 1], 0.0)
            nc.gpsimd.memset(kst_w[:, 1, :, 0:LOC - 1], 0.0).then_inc(S["const_ready"], 1)
            link(nc.gpsimd.memset(e_tile[:], float(np.e)))
            pool.wait_ge(d_par, 16)
            tt(scr[:, 0], e_tile[:], par[:, 2], ALU.pow).then_inc(S["dt_ready"], 1)
            pool.wait_ge(S["dt_ready"], 1)
            link(tt(scr[:, 1], par[:, 0], scr[:, 0], ALU.mult))
            tt(scr[:, 5], e_tile[:], scr[:, 1], ALU.pow).then_inc(S["pow_ready"], 1)
            pool.wait_ge(S["ss_ready"], 2)
            link(ts(ss[:, R_MIX], ss[:, R_MIX], 1 / D_MODEL, EPS, ALU.mult, ALU.add))
            rsqrt(rstd[:, R_MIX], ss[:, R_MIX], S["rstd_mix_ready"])
            pool.wait_ge(d_bc[0], 16)
            pool.wait_ge(S["signs_ready"], 1)
            t_b = wb_t[:].rearrange("p g d c -> p (g d) c")
            tt(bbx[:], bc[:, 1], wide(scr, 11), ALU.mult)
            link(tt(t_b, bc[:, 0], wide(scr, 12), ALU.mult))
            link(tt(bbx[:], bbx[:], t_b, ALU.subtract))
            pool.wait_ge(S["mul_ready"], 1)
            for b in range(NB):
                if b == 0:
                    pool.wait_ge(S["bb_ready"], 1)
                else:
                    pool.wait_ge(S["tab_mm"], b)
                    pool.wait_ge(S["wb_ready"], b)

                def b_(x):
                    return x[:, s5_group(b)].unsqueeze(2).to_broadcast([P, BG, LOC, CH])

                def p_(x):
                    return x[:, 0:LOC, s5_group(b)].rearrange("p d g -> p g d").unsqueeze(3).to_broadcast(
                        [P, BG, LOC, CH])

                tt(wb[:], b_(bb), p_(pr), ALU.mult)
                link(tt(wb_t[:], b_(bbx), p_(pi), ALU.mult))
                tt(wb[:], wb[:], wb_t[:], ALU.add).then_inc(S["wb_ready"], 1)
            pool.wait_ge(d_swap[1], 32)
            for k in range(NCH - 2):
                scan_step(tt, link, S["scanB_done"], 1, k)
            for b in range(YBUF, 5):
                load_y_tables(pool, b, range(LOC // 2, LOC), d_mt_pool)
            for q in range(2):
                if q:
                    for b in range(5, NB):
                        load_y_tables(pool, b, range(LOC // 2, LOC), d_mt_pool)
                pool.wait_ge(S["bn_ready"], q + 1)
                at = slice(8 * q, 8 * q + 8)
                link(ts(rv[:, at], mv[:, at, 1], 1.0, EPS, ALU.mult, ALU.add))
                rsqrt(rret[:, at], rv[:, at], S["rret_ready"], 8)
            pool.wait_ge(S["ssq_ready"], 1)
            rsqrt(rstd[:, R_SSM], ss[:, R_SSM], S["rstd_ssm_ready"])
            for i, (src, row, ready) in enumerate((("x2_sq", R_FFN, "rstd_ffn_ready"),
                                                   ("fin_sq", R_FIN, "rstd_fin_ready"))):
                for c in range(1, 4):
                    pool.wait_ge(S[src], 2 * c + 2)
                    link(tt(ss4[:, i, 0], ss4[:, i, 0], ss4[:, i, c], ALU.add))
                link(ts(ss[:, row], ss4[:, i, 0], 1 / D_MODEL, EPS, ALU.mult, ALU.add))
                rsqrt(rstd[:, row], ss[:, row], S[ready])

        @block.tensor
        def _(pe):
            mm, tr = nc.tensor.matmul, nc.tensor.transpose

            def three(o, x_hi, x_lo, h, l, first, last):
                mm(o, x_hi, h, start=first, stop=False)
                mm(o, x_hi, l, start=False, stop=False)
                return mm(o, x_lo, h, start=False, stop=last)

            def column_chunk(n, s, blocks, banks, first, last):
                for k in range(2):
                    at = slice(NCOL * k, NCOL * (k + 1))
                    hi, lo = blocks[k]
                    for t in range(TOK):
                        tok = slice(P * t, P * (t + 1))
                        ins = three(ps[:, banks + t], hi[:, tok], lo[:, tok], w_hi[:, s, at], w_lo[:, s, at],
                                    first and k == 0, last and k == 1)
                        if 2 * k + t == 3:
                            ins.then_inc(S["pe_done"], 1)
                        if n is not None:
                            beside(n, 2 * k + t)

            def ready(n, turn=None):
                pe.wait_ge(S["low_done"], n + 1 if turn is None else turn * TURN + (n + 1))

            def act_pair(kb):
                return [(act_block(kb + k, 0), act_block(kb + k, 1)) for k in range(2)]

            def h2_pair(kb):
                return [(h2(kb + k, 0), h2(kb + k, 1)) for k in range(2)]

            def ff_pair(hi, lo, kb):
                return [(hi[:, kb + k], lo[:, kb + k]) for k in range(2)]

            def u_transposes(h):
                pe.wait_ge(S["proj_free"], 2 * h + 2)
                if h == 0:
                    pe.wait_ge(S["ss_ready"], 2)
                    pe.wait_ge(d_ident, 16)
                else:
                    pe.wait_ge(S["wbT_ready"], 2)
                for blk in range(4 * h, 4 * h + 4):
                    for t in range(TOK):
                        at = (blk % 2) * SEQ + t * P
                        ins = tr(ps[:, 4 + blk // 2 % 2, at:at + P], u_tok[:, t, P * blk:P * (blk + 1)], ident[:])
                ins.then_inc(S["uT_mm"], 1)

            def tables(b, part):
                if part == 0:
                    pe.wait_ge(S["cl_ready"], b + 1)
                    pe.wait_ge(S["wb_ready"], b + 1)
                    pe.wait_ge(S["u_copied"], 1 if b < 2 else 2)
                    if b == 0:
                        pe.wait_ge(S["bb_ready"], 1)
                    else:
                        pe.wait_ge(S["kpsum_free"], b)
                for g in (2 * part, 2 * part + 1):
                    h, q = divmod(g, 4)
                    gg = BG * b + g
                    mm(ps[32 * q:32 * q + 32, 6, P * h:P * (h + 1)], bb[:, gg:gg + 2].rearrange("p a c -> p (a c)"),
                       cl[:, b % 2, g, 0:LOC].rearrange("p d c -> p (d c)"), start=True, stop=True)
                    ins = tr(ps[:, 4 + g // 4, P * (g % 4):P * (g % 4 + 1)],
                             wb[:, g].rearrange("p d c -> p (d c)"), ident[:])
                if part == 3:
                    ins.then_inc(S["tab_mm"], 1)

            def chunk_inputs(b, part):
                if part == 0:
                    pe.wait_ge(S["wbT_ready"], b + 1)
                    if b % HB == 0:
                        pe.wait_ge(d_u[b // HB], 16 * LOC)
                    if b:
                        pe.wait_ge(S["v_free"], b)
                for g in (2 * part, 2 * part + 1):
                    ins = mm(ps[:, 7, NCH * g:NCH * (g + 1)], wbT[:, b % 2, g], u_loc[:, BG * b + g],
                             start=True, stop=True)
                if part == 3:
                    ins.then_inc(S["v_mm"], 1)

            def qk_transposes(i):
                pe.wait_ge(S["qr_ready"], i + 1)
                if i == 0:
                    pe.wait_ge(S["wbT_ready"], NB)
                else:
                    pe.wait_ge(S["qk_free"], i)
                if i == 2:
                    pe.wait_ge(S["sT_ready"], 4)
                for h in range(4):
                    for t in range(TOK):
                        at = (h % 2) * SEQ + t * P
                        ins = tr(ps[:, 4 + h // 2, at:at + P], qr[:, t, P * h:P * (h + 1)], ident[:])
                ins.then_inc(S["qk_mm"], 1)

            def score(h):
                if h % 4 == 0:
                    pe.wait_ge(S["qk_free"], 2 + h // 2)
                if h >= 2:
                    pe.wait_ge(S["sT_ready"], h - 1)
                for a in range(TOK):
                    ins = mm(ps[:, 4 + h % 2, SEQ * a:SEQ * (a + 1)], kT[:, h, P * a:P * (a + 1)], qT[:, h],
                             start=True, stop=True)
                ins.then_inc(S["score_mm"], 1)

            def head(h):
                pe.wait_ge(S["sT_ready"], h + 1)
                if h == 0:
                    pe.wait_ge(S["proj_free"], 8)
                    pe.wait_ge(S["v_free"], NB)
                elif h % 2 == 0:
                    pe.wait_ge(S["out_free"], h // 2)
                for t in range(TOK):
                    at = (h % 2) * SEQ + t * P
                    for a in range(TOK):
                        ins = mm(ps[:, 7, at:at + P], sT[:, h % 2, a, P * t:P * (t + 1)],
                                 v[:, a, P * h:P * (h + 1)], start=(a == 0), stop=(a == TOK - 1))
                ins.then_inc(S["head_mm"], 1)

            def y_batch(b, part):
                if part == 0:
                    if b == 0:
                        pe.wait_ge(S["scanA_done"], 1)
                        pe.wait_ge(d_u2, 2 * 16 * LOC)
                        pe.wait_ge(S["kpsum_free"], NB)
                    elif b % 2 == 0:
                        pe.wait_ge(S["y1_ready"], b // 2)
                    if b == HB:
                        pe.wait_ge(S["scanB_done"], 1)
                    pe.wait_ge(d_mt[b % YBUF], 16 * LOC + 8 * LOC * (b // YBUF))
                    if b >= YBUF:
                        pe.wait_ge(d_mt_pool[b % YBUF], 8 * LOC * (b // YBUF))
                    pe.wait_ge(d_clr[b % YBUF], 16 * (b // YBUF + 1))
                for g in (2 * part, 2 * part + 1):
                    at = NCH * (BG * (b % 2) + g)
                    mm(ps[:, 6, at:at + NCH], y_tab[:, b % YBUF, 0, g], u_loc2[:, BG * b + g], start=True, stop=False)
                    ins = mm(ps[:, 6, at + 1:at + NCH], y_tab[:, b % YBUF, 1, g],
                             state_groups(b, 0)[:, 0:NCH - 1, g], start=False, stop=True)
                if part == 3:
                    ins.then_inc(S["y_mm"], 1)

            def ret_transposes(q):
                pe.wait_ge(S["ret_ready"], q + 1)
                if q:
                    pe.wait_ge(S["y1_ready"], 4)
                    pe.wait_ge(S["out_free"], 4)
                else:
                    pe.wait_ge(S["sT_ready"], 8)
                for p in (2 * q, 2 * q + 1):
                    for h in range(2):
                        for t in range(TOK):
                            at = SEQ * h + P * t
                            ins = tr(ps[:, 4 + p, at:at + P], ret[:, 2 * p + h, P * t:P * (t + 1)], ident[:])
                    ins.then_inc(S["retT_mm"], 1)

            def channel_squares(part):
                if part == 0:
                    pe.wait_ge(S["const_ready"], 1)
                    pe.wait_ge(S["sqT_ready"], 2)
                    pe.wait_ge(S["ret_lo"], 4)
                t, half_ = divmod(part, 2)
                for k in range(4 * half_, 4 * half_ + 4):
                    ins = mm(ps[:, 4, t:t + 1], sqT[:, k, P * t:P * (t + 1)], ones[:], start=(k == 0), stop=(k == 7))
                if part == 3:
                    ins.then_inc(S["ssq_mm"], 1)

            def h2_transposes(c):
                pe.wait_ge(S["cols_added"], 5 + c)
                if c >= 2:
                    pe.wait_ge(S["h2_lo"], 4 * (c - 1))
                elif c == 0:
                    pe.wait_ge(S["ssq_ready"], 1)
                for k in range(4):
                    for t in range(TOK):
                        at = (k % 2) * SEQ + t * P
                        col = P * (4 * c + k)
                        ins = tr(ps[:, 4 + 2 * (c % 2) + k // 2, at:at + P], x2[:, t, col:col + P], ident[:])
                ins.then_inc(S["h2_mm"], 1)

            def ff_transposes(count, bank=4):
                pe.wait_ge(S["ff_ready"], count)
                for k in range(4):
                    for t in range(TOK):
                        at = (k % 2) * SEQ + t * P
                        ins = tr(ps[:, bank + k // 2, at:at + P], ff_act[:, t, P * k:P * (k + 1)], ident[:])
                ins.then_inc(S["ffT_mm"], 1)

            def beside(n, part):
                for b in range(NB):
                    if n == TAB_AT[b]:
                        tables(b, part)
                    if n == V_AT[b]:
                        chunk_inputs(b, part)
                    if n == Y_AT[b]:
                        y_batch(b, part)
                if n == RET0 + 6:
                    channel_squares(part)

            def side(n):
                for h in range(2):
                    if n == U_TR[h]:
                        u_transposes(h)
                for i in range(4):
                    if n == QK_TR[i]:
                        qk_transposes(i)
                for h in range(HEADS):
                    if n == HEAD_AT[h]:
                        head(h)
                    if n == SCORE_AT[h]:
                        score(h)
                for q in range(2):
                    if n == RET_TR[q]:
                        ret_transposes(q)
                c, r = divmod(n - (SSM0 + 5), 4)
                if r == 0 and 0 <= c < 4:
                    h2_transposes(c)

            pe.wait_ge(S["warm_ready"], 1)
            for _ in range(WARM):
                mm(ps[:, 7], warm[:, 0:P], warm[:], start=True, stop=True)

            for n in range(N_IN):
                gi, i = divmod(n, GRP)
                if n < GRP:
                    pe.wait_ge(S["xl_ready"], n + 1)
                if i == 0 and gi >= 2:
                    pe.wait_ge(S["proj_free"], 2 * gi - 2)
                ready(n)
                column_chunk(n, n % SPL, act_pair(2 * i), 2 * (gi % 2), i == 0, i == GRP - 1)
                side(n)
            for n in range(GLU0, RET0):
                pair, half_ = GLU_ORDER[n - GLU0]
                if half_ == 0:
                    if pair < 2:
                        pe.wait_ge(S["proj_free"], 18 + 2 * pair)
                    else:
                        pe.wait_ge(S["sig_ready"], 2 * (pair - 1))
                pe.wait_ge(S["y1T_lo_ready"], 1 + half_)
                ready(n)
                for k in range(4):
                    hi, lo = (x[:, k] for x in y1T_parts[half_])
                    for j in range(2):
                        at = slice(SEQ * k + P * j, SEQ * k + P * (j + 1))
                        o = ps[:, 2 * (pair % 2) + j, 0:SEQ]
                        first, last = half_ == 0 and k == 0, half_ == 1 and k == 3
                        mm(o, w_hi[:, n % SPL, at], hi, start=first, stop=False)
                        mm(o, w_hi[:, n % SPL, at], lo, start=False, stop=False)
                        ins = mm(o, w_lo[:, n % SPL, at], hi, start=False, stop=last)
                ins.then_inc(S["pe_done"], 1)
                side(n)
            for n in range(RET0, FFN0):
                idx, i = divmod(n - RET0, 4)
                c, part = idx % 4, idx // 4
                if i == 0 and idx >= 2:
                    pe.wait_ge(S["cols_added"], idx - 1)
                if part == 0 and i == 0 and c < 2:
                    pe.wait_ge(S["sig_ready"], 6 + 2 * c)
                if part == 0 and c == 0:
                    pe.wait_ge(S["ret_lo"], 2 * i + 2)
                if part == 1 and c == 0 and i == 0:
                    pe.wait_ge(S["ssm_lo"], 8)
                ready(n)
                column_chunk(n, n % SPL, act_pair(8 * part + 2 * i), 2 * (c % 2), i == 0, i == 3)
                side(n)
            for n in range(FFN0, LOOP0):
                up, i = divmod(n - FFN0, GRP)
                if n == FFN0:
                    pe.wait_ge(S["cols_added"], 7)
                if n == FFN0 + GRP:
                    pe.wait_ge(S["cols_added"], 8)
                if not up and i % 2 == 0:
                    pe.wait_ge(S["h2_lo"], 2 * i + 4)
                ready(n)
                column_chunk(n, n % SPL, h2_pair(2 * i), 2 * up, i == 0, i == GRP - 1)
                side(n)
            def turn(j, final=False):
                for c in range(TURN):
                    part, i = divmod(c, GRP)
                    if c == 0:
                        pe.wait_ge(S["silu_ready"], (j + 1) * 2)
                    if c == GRP:
                        pe.wait_ge(S["ff_ready"], j + 1)
                    if c == 2 * GRP:
                        pe.wait_ge(S["ffT_lo_ready"], j + 1)
                    ready(LOOP0 + c, turn=j)
                    if part < 2:
                        column_chunk(None, c % SPL, h2_pair(2 * i), 2 * part, i == 0, i == GRP - 1)
                    else:
                        col, k = divmod(i, 2)
                        if k == 0 and col >= 2:
                            pe.wait_ge(S["cols_added"], j * 4 + (7 + col))
                        column_chunk(None, c % SPL, ff_pair(ffT_hi, ffT_lo, 2 * k), 6 - 2 * (col % 2), k == 0, k == 1)
                    if final and c == 2 * GRP + 4:
                        ff_transposes(FG, 0)
                    if c == GRP - 1:
                        pe.wait_ge(S["cols_added"], j * 4 + 8)
                        ff_transposes(j + 1)

            with pe.Fori(0, FG - 2) as j:
                turn(j)
            turn(FG - 2, final=True)
            for i in range(GRP):
                col, k = divmod(i, 2)
                if k == 0 and col >= 2:
                    pe.wait_ge(S["last_added"], 2 * (col - 1))
                elif k == 0:
                    pe.wait_ge(S["cols_added"], 4 * (FG - 1) + 7 + col)
                if i == 0:
                    pe.wait_ge(S["ffT_lo_ready"], FG)
                ready(TAIL0 + i)
                column_chunk(None, i % SPL, ff_pair(ffE_hi, ffE_lo, 2 * k), 6 - 2 * (col % 2), k == 0, k == 1)


def _time_order():
    return (LOC * np.arange(NCH)[None, :] + np.arange(LOC)[:, None]).reshape(-1)


def _constants():
    time = _time_order()
    f32 = np.float32
    h = np.arange(HEADS, dtype=np.float64)
    log_g = np.log1p(-(2.0 ** (-5.0 - h)))
    n, m = time[None, :], time[:, None]
    seen = (n // CHUNK >= m // CHUNK)
    dist = np.abs(n - m)
    decay = np.where(seen, np.exp(log_g[:, None, None] * dist), 0.0) * HEAD_DIM ** -0.5
    decay = decay.reshape(HEADS, TOK, P, SEQ).transpose(0, 2, 1, 3)
    hd = HEAD_DIM // 2
    freqs = f32(10000.0) ** (-np.arange(hd, dtype=f32) / f32(hd))
    ang = (time.astype(f32)[:, None] * freqs[None, :]).astype(np.float64)
    rope = np.stack([np.concatenate([np.cos(ang)] * 2, 1), np.concatenate([-np.sin(ang), np.sin(ang)], 1)], 1)
    rope = rope.reshape(TOK, P, 2, HEAD_DIM).transpose(1, 0, 2, 3)
    eye16 = np.zeros((P, CH))
    for q in range(4):
        eye16[32 * q:32 * q + CH] = np.eye(CH)
    sign = np.concatenate([-np.ones(STATE), np.ones(STATE)])[:, None]
    return [np.ascontiguousarray(a, dtype=f32) for a in (decay, rope, eye16, np.eye(P), sign)]


def kernel(**inputs):
    import concourse.bacc as bacc
    from concourse.bass_utils import run_bass_kernel_spmd

    a = {k: np.asarray(x) for k, x in inputs.items()}
    decay, rope, eye16, ident, sign = _constants()
    x = a["x"][0].reshape(NCH, LOC, D_MODEL).transpose(1, 0, 2).reshape(SEQ, D_MODEL)

    def cols(name):
        return a[name].reshape(-1, P).T

    def stack(re, im, axes):
        return np.concatenate([a[re][0].transpose(axes), a[im][0].transpose(axes)], 0)

    b, c = (1, 0, 2), (2, 0, 1)
    dsk = np.zeros((4, 2 * CH, GROUPS // 4), np.float32)
    dsk[:, :CH] = a["ssm_d"][0].reshape(GROUPS // 4, 4, CH).transpose(1, 2, 0)
    arrays = {
        "xT": x.T.reshape(KB, P, SEQ).transpose(1, 0, 2),
        "x_tok": x.reshape(TOK, P, D_MODEL).transpose(1, 0, 2),
        "vec": np.concatenate([cols("norm_mix_g"), cols("norm_ffn_g"), cols("ssm_b_glu"), cols("ssm_out_g"),
                               cols("ret_gn_g"), sign, -sign], 1),
        "par": np.stack([np.concatenate([a[n][0].T] * 2, 0) for n in ("ssm_a_re", "ssm_a_im")]
                        + [np.broadcast_to(a["ssm_log_dt"][0], (P, GROUPS))], 1),
        "bc": np.stack([stack("ssm_b_re", "ssm_b_im", b), stack("ssm_b_im", "ssm_b_re", b),
                        stack("ssm_c_re", "ssm_c_im", c), stack("ssm_c_im", "ssm_c_re", c)], 1),
        "dsk": dsk.reshape(P, GROUPS // 4),
        "g_final": np.broadcast_to(a["norm_final_g"], (P, D_MODEL)),
        "decay": decay, "rope": rope, "eye16": eye16, "ident": ident,
    }
    for n in ("w_in", "ssm_w_glu", "w_out", "w_gate", "w_up", "w_down"):
        arrays[n] = a[n][0]
    arrays = {n: np.ascontiguousarray(x) for n, x in arrays.items()}
    nc = bacc.Bacc("TRN2", target_bir_lowering=False, num_devices=1)
    A = {n: nc.dram_tensor("in_" + n, x.shape, mybir.dt.from_np(x.dtype), kind="ExternalInput").ap()
         for n, x in arrays.items()}
    out = nc.dram_tensor("out", (P, TOK, D_MODEL), F32, kind="ExternalOutput").ap()
    build(nc, A, out)
    r = run_bass_kernel_spmd(nc, [{"in_" + n: x for n, x in arrays.items()}], core_ids=[0])
    y = r.results[0]["out"].transpose(1, 0, 2).reshape(LOC, NCH, D_MODEL).transpose(1, 0, 2)
    return np.ascontiguousarray(y).reshape(1, SEQ, D_MODEL)
```
